# Optimizing a Trainium2 kernel written in Bass

```python
import jax
import jax.numpy as jnp
from jax import lax
import numpy as np

D_MODEL = 1024
BATCH = 1
SEQ = 256
DEPTH = 2

GRID_W = 64
CTX_LEN = 256
HEAD_DIM = 64
Q_BLOCK = 128
ROPE_THETA = 10000.0
NORM_EPS = 1e-6

GQA_HEADS = 8
GQA_KV_HEADS = 2
NA_HEADS = 4
NA_WIN_R = 8
NA_WIN_C = 16
RWKV_HEADS = 4
RWKV_N = 64
RWKV_W = RWKV_HEADS * RWKV_N
RWKV_DECAY_LORA = 32
RWKV_AAA_LORA = 32
RWKV_GATE_LORA = 64
RWKV_GN_EPS = 64e-5
MLA_HEADS = 4
MLA_Q_LORA = 384
MLA_KV_LORA = 256
MLA_NOPE = 64
MLA_ROPE = 32
MLA_V = 64
N_BRANCH = 4
GQA_W = GQA_HEADS * HEAD_DIM
NA_W = NA_HEADS * HEAD_DIM
MLA_W = MLA_HEADS * MLA_V
BRANCH_WIDTHS = (GQA_W, NA_W, RWKV_W, MLA_W)
MIX_W = GQA_W + NA_W + RWKV_W + MLA_W
IN_SPLITS = (GQA_W, GQA_KV_HEADS * HEAD_DIM, GQA_KV_HEADS * HEAD_DIM, NA_W, NA_W, NA_W,
             RWKV_W, RWKV_W, RWKV_W, MLA_Q_LORA, MLA_KV_LORA, MLA_ROPE, N_BRANCH * D_MODEL)
ALL_PARTS = (0, 1, 2, 3, 4, 5, 6, 7, 8, 9, 10, 11, 12)
KV_PARTS = (1, 2, 4, 5, 7, 8, 10, 11)
P_IN = GQA_W + 4 * GQA_KV_HEADS * HEAD_DIM // 2 + 3 * NA_W + 3 * RWKV_W + MLA_Q_LORA + MLA_KV_LORA + MLA_ROPE + N_BRANCH * D_MODEL
DENSE_FF = 2816
N_EXPERTS = 8
TOP_K = 2
EXPERT_FF = 1408
N_DENSE = (DEPTH + 1) // 2
N_MOE = DEPTH // 2

kernel_name = 'hybrid_gated_branch_diffusion_trunk'

def _rms_norm(x, g):
    xf = x.astype(jnp.float32)
    y = xf * lax.rsqrt(jnp.mean(xf * xf, axis=-1, keepdims=True) + NORM_EPS)
    return (y * g.astype(jnp.float32)).astype(x.dtype)

def _modulate(h, shift, scale):
    return h * (1 + scale) + shift

def _split_heads(t, n):
    b, n_tok, _ = t.shape
    return t.reshape(b, n_tok, n, -1).transpose(0, 2, 1, 3)

def _merge_heads(t):
    b, n, n_tok, d = t.shape
    return t.transpose(0, 2, 1, 3).reshape(b, n_tok, n * d)

def _axial_rope_tables(n_tok, rot_dim):
    t = jnp.arange(n_tok)
    row = (t // GRID_W).astype(jnp.float32)
    col = (t % GRID_W).astype(jnp.float32)
    n_pairs = rot_dim // 4
    inv_freq = ROPE_THETA ** (-jnp.arange(n_pairs, dtype=jnp.float32) / n_pairs)
    ang = jnp.concatenate([row[:, None] * inv_freq, col[:, None] * inv_freq], axis=-1)
    return jnp.cos(ang), jnp.sin(ang)

def _apply_rope(x, cos, sin):
    half = x.shape[-1] // 2
    x1 = x[..., :half].astype(jnp.float32)
    x2 = x[..., half:].astype(jnp.float32)
    return jnp.concatenate([x1 * cos - x2 * sin, x1 * sin + x2 * cos], axis=-1).astype(x.dtype)

def _block_attention(q, k, v, scale):
    b, hq, n_q, dq = q.shape
    hkv, dv = k.shape[1], v.shape[-1]
    g = hq // hkv
    nb = n_q // Q_BLOCK
    qb = q.reshape(b, hkv, g, nb, Q_BLOCK, dq).transpose(3, 0, 1, 2, 4, 5)

    def one_block(qi):
        s = jnp.einsum('bkgqd,bkld->bkgql', qi, k).astype(jnp.float32) * scale
        p = jax.nn.softmax(s, axis=-1).astype(v.dtype)
        return jnp.einsum('bkgql,bkld->bkgqd', p, v)

    o = lax.map(one_block, qb)
    return o.transpose(1, 2, 3, 0, 4, 5).reshape(b, hq, n_q, dv)

def _in_project(hx, w_in, keep):
    offs = [0]
    for s in IN_SPLITS:
        offs.append(offs[-1] + s)
    if len(keep) == len(IN_SPLITS):
        z = hx @ w_in
        return [z[..., offs[i]:offs[i + 1]] for i in range(len(IN_SPLITS))]
    z = hx @ jnp.concatenate([w_in[:, offs[i]:offs[i + 1]] for i in keep], axis=1)
    parts = [None] * len(IN_SPLITS)
    pos = 0
    for i in keep:
        parts[i] = z[..., pos:pos + IN_SPLITS[i]]
        pos += IN_SPLITS[i]
    return parts

def _gqa_mixer(q, k, v, qc, kc, vc, q_gain, k_gain, cos, sin, ctx_out):
    scale = HEAD_DIM ** -0.5
    q = _apply_rope(_rms_norm(_split_heads(q, GQA_HEADS), q_gain), cos, sin)
    k = _apply_rope(_rms_norm(_split_heads(k, GQA_KV_HEADS), k_gain), cos, sin)
    v = _split_heads(v, GQA_KV_HEADS)
    kc = _rms_norm(_split_heads(kc, GQA_KV_HEADS), k_gain)
    vc = _split_heads(vc, GQA_KV_HEADS)
    y = _block_attention(q, jnp.concatenate([kc, k], axis=2), jnp.concatenate([vc, v], axis=2), scale)
    yc = None
    if ctx_out:
        yc = _merge_heads(_block_attention(_rms_norm(_split_heads(qc, GQA_HEADS), q_gain), kc, vc, scale))
    return _merge_heads(y), yc

def _na_mixer(q, k, v, qc, kc, vc, rpb, rows, ctx_out):
    b, n_lat, _ = q.shape
    wr = min(NA_WIN_R, rows)
    scale = HEAD_DIM ** -0.5

    def grid(t):
        return _split_heads(t, NA_HEADS).reshape(b, NA_HEADS, rows, GRID_W, HEAD_DIM)

    qg, kg, vg = grid(q), grid(k), grid(v)
    kc = _split_heads(kc, NA_HEADS)
    vc = _split_heads(vc, NA_HEADS)
    r_idx = jnp.arange(rows)
    c_idx = jnp.arange(GRID_W)
    key_rows = jnp.clip(r_idx - wr // 2, 0, rows - wr)[:, None] + jnp.arange(wr)[None, :]
    col_start = jnp.clip(c_idx - NA_WIN_C // 2, 0, GRID_W - NA_WIN_C)
    col_in = (c_idx[None, :] >= col_start[:, None]) & (c_idx[None, :] < col_start[:, None] + NA_WIN_C)
    dr = key_rows - r_idx[:, None] + (NA_WIN_R - 1)
    dc = jnp.clip(c_idx[None, :] - c_idx[:, None], 1 - NA_WIN_C, NA_WIN_C - 1) + (NA_WIN_C - 1)
    bias = rpb[:, dr[:, None, :, None], dc[None, :, None, :]].astype(jnp.float32)
    k_rows = kg[:, :, key_rows]
    v_rows = vg[:, :, key_rows]
    s_win = jnp.einsum('bhrqd,bhrnkd->bhrqnk', qg, k_rows).astype(jnp.float32) * scale + bias
    s_win = jnp.where(col_in[:, None, :], s_win, -jnp.inf)
    s_ctx = jnp.einsum('bhrqd,bhcd->bhrqc', qg, kc).astype(jnp.float32) * scale
    n_win = wr * GRID_W
    s = jnp.concatenate([s_win.reshape(b, NA_HEADS, rows, GRID_W, n_win), s_ctx], axis=-1)
    p = jax.nn.softmax(s, axis=-1).astype(v.dtype)
    p_win = p[..., :n_win].reshape(b, NA_HEADS, rows, GRID_W, wr, GRID_W)
    o = (jnp.einsum('bhrqnk,bhrnkd->bhrqd', p_win, v_rows)
         + jnp.einsum('bhrqc,bhcd->bhrqd', p[..., n_win:], vc))
    y = _merge_heads(o.reshape(b, NA_HEADS, n_lat, HEAD_DIM))
    yc = None
    if ctx_out:
        yc = _merge_heads(_block_attention(_split_heads(qc, NA_HEADS), kc, vc, scale))
    return y, yc

def _token_shift(t):
    p = jnp.pad(t, ((0, 0), (1, 1), (0, 0)))
    return 0.5 * (p[:, :-2] + p[:, 2:]) - t

def _unit_heads(t):
    b, n_tok, w = t.shape
    th = t.reshape(b, n_tok, RWKV_HEADS, RWKV_N).astype(jnp.float32)
    th = th * lax.rsqrt(jnp.maximum(jnp.sum(th * th, axis=-1, keepdims=True), 1e-12))
    return th.reshape(b, n_tok, w).astype(t.dtype)

def _rwkv_prepare(h, r0, k0, v0, rw, with_out):
    mu_x, mu_p, w0, w1, w2, a0, a1, a2, g1, g2, k_k, k_a = rw[:12]
    dh = _token_shift(h)
    xw = h + dh * mu_x[0]
    xa = h + dh * mu_x[1]
    k = k0 + _token_shift(k0) * mu_p[1]
    v = v0 + _token_shift(v0) * mu_p[2]
    kk = _unit_heads(k * k_k)
    per_dir = []
    for d in range(2):
        w_log = -jax.nn.softplus(-(w0[d] + jnp.tanh(xw @ w1[d]) @ w2[d])) - 0.5
        decay = jnp.exp(-jnp.exp(w_log.astype(jnp.float32)))
        a = jax.nn.sigmoid(a0[d] + (xa @ a1[d]) @ a2[d])
        per_dir.append((decay, k * (1 + (a - 1) * k_a), kk * a))
    if not with_out:
        return v, kk, per_dir, None, None
    r = r0 + _token_shift(r0) * mu_p[0]
    xg = h + dh * mu_x[2]
    gates = [jax.nn.sigmoid(xg @ g1[d]) @ g2[d] for d in range(2)]
    return v, kk, per_dir, r, gates

def _rwkv_scan(s0, decay, k, v, kk, b, r, reverse):
    def to_tm(t):
        return jnp.moveaxis(t.reshape(t.shape[0], t.shape[1], RWKV_HEADS, RWKV_N).astype(jnp.float32), 1, 0)

    xs = [to_tm(decay), to_tm(k), to_tm(v), to_tm(kk), to_tm(b)]
    if r is not None:
        xs.append(to_tm(r))

    def step(s, inp):
        w_t, k_t, v_t, kk_t, b_t = inp[:5]
        s_kk = jnp.einsum('bhvk,bhk->bhv', s, kk_t)
        s = s * w_t[:, :, None, :] - s_kk[..., None] * b_t[:, :, None, :] + v_t[..., None] * k_t[:, :, None, :]
        out = jnp.einsum('bhvk,bhk->bhv', s, inp[5]) if len(inp) > 5 else None
        return s, out

    s_fin, ys = lax.scan(step, s0, tuple(xs), reverse=reverse)
    if r is None:
        return s_fin, None
    return s_fin, jnp.moveaxis(ys, 0, 1)

def _rwkv_readout(o, r, k, v, g, r_k, ln_w, ln_b):
    b, n_tok = o.shape[:2]
    mu = jnp.mean(o, axis=-1, keepdims=True)
    var = jnp.mean(jnp.square(o - mu), axis=-1, keepdims=True)
    on = ((o - mu) * lax.rsqrt(var + RWKV_GN_EPS)).reshape(b, n_tok, RWKV_W) * ln_w + ln_b

    def hs(t):
        return t.reshape(b, n_tok, RWKV_HEADS, RWKV_N)

    bonus = (jnp.sum(hs(r) * hs(k) * r_k, axis=-1, keepdims=True) * hs(v)).reshape(b, n_tok, RWKV_W)
    return (on.astype(r.dtype) + bonus) * g

def _rwkv_mixer(h, r0, k0, v0, hc, rc0, kc0, vc0, rw, ctx_out):
    r_k, ln_w, ln_b = rw[12:]
    s0 = jnp.zeros((h.shape[0], RWKV_HEADS, RWKV_N, RWKV_N), jnp.float32)
    v, kk, dirs, r, g = _rwkv_prepare(h, r0, k0, v0, rw, True)
    vc, kkc, dirs_c, rc, gc = _rwkv_prepare(hc, rc0, kc0, vc0, rw, ctx_out)
    y = None
    yc = None
    for d in range(2):
        rev = d == 1
        dec_c, kd_c, b_c = dirs_c[d]
        s_ctx, oc = _rwkv_scan(s0, dec_c, kd_c, vc, kkc, b_c, rc, rev)
        dec, kd, bb = dirs[d]
        _, o = _rwkv_scan(s_ctx, dec, kd, v, kk, bb, r, rev)
        yd = _rwkv_readout(o, r, kd, v, g[d], r_k, ln_w, ln_b)
        y = yd if y is None else y + yd
        if ctx_out:
            ycd = _rwkv_readout(oc, rc, kd_c, vc, gc[d], r_k, ln_w, ln_b)
            yc = ycd if yc is None else yc + ycd
    return y, yc

def _mla_queries(cq, q_gain, w_uq):
    qh = _split_heads(_rms_norm(cq, q_gain) @ w_uq, MLA_HEADS)
    return qh[..., :MLA_NOPE], qh[..., MLA_NOPE:]

def _mla_keys_values(ckv, kr, kv_gain, w_ukv):
    kvh = _split_heads(_rms_norm(ckv, kv_gain) @ w_ukv, MLA_HEADS)
    return kvh[..., :MLA_NOPE], kvh[..., MLA_NOPE:], kr[:, None]

def _mla_mixer(cq, ckv, kr, cqc, ckvc, krc, q_gain, w_uq, kv_gain, w_ukv, cos, sin, ctx_out):
    def join(k_nope, k_rope):
        return jnp.concatenate([k_nope, jnp.broadcast_to(k_rope, k_nope.shape[:-1] + (MLA_ROPE,))], axis=-1)

    scale = (MLA_NOPE + MLA_ROPE) ** -0.5
    q_n, q_r = _mla_queries(cq, q_gain, w_uq)
    q = jnp.concatenate([q_n, _apply_rope(q_r, cos, sin)], axis=-1)
    k_n, v, k_r = _mla_keys_values(ckv, kr, kv_gain, w_ukv)
    k = join(k_n, _apply_rope(k_r, cos, sin))
    kc_n, vc, kc_r = _mla_keys_values(ckvc, krc, kv_gain, w_ukv)
    kc = join(kc_n, kc_r)
    y = _merge_heads(_block_attention(q, jnp.concatenate([kc, k], axis=2), jnp.concatenate([vc, v], axis=2), scale))
    yc = None
    if ctx_out:
        qc_n, qc_r = _mla_queries(cqc, q_gain, w_uq)
        yc = _merge_heads(_block_attention(jnp.concatenate([qc_n, qc_r], axis=-1), kc, vc, scale))
    return y, yc

def _gated_merge(branches, gate_logits, w_branch, w_out):
    b, n_tok, _ = gate_logits.shape
    gates = jax.nn.sigmoid(gate_logits.reshape(b, n_tok, N_BRANCH, D_MODEL))
    merged = None
    off = 0
    for i, yb in enumerate(branches):
        wd = BRANCH_WIDTHS[i]
        term = gates[:, :, i] * (yb @ w_branch[off:off + wd])
        merged = term if merged is None else merged + term
        off += wd
    return merged @ w_out

def _token_mixing(h, hc, rows, rope_h, rope_m, w_in, q_gain, k_gain, rpb, rw, mla_p, w_branch, w_out, ctx_out):
    z = _in_project(h, w_in, ALL_PARTS)
    zc = _in_project(hc, w_in, ALL_PARTS if ctx_out else KV_PARTS)
    ya, yca = _gqa_mixer(z[0], z[1], z[2], zc[0], zc[1], zc[2], q_gain, k_gain, rope_h[0], rope_h[1], ctx_out)
    yb, ycb = _na_mixer(z[3], z[4], z[5], zc[3], zc[4], zc[5], rpb, rows, ctx_out)
    yr, ycr = _rwkv_mixer(h, z[6], z[7], z[8], hc, zc[6], zc[7], zc[8], rw, ctx_out)
    ym, ycm = _mla_mixer(z[9], z[10], z[11], zc[9], zc[10], zc[11], mla_p[0], mla_p[1], mla_p[2], mla_p[3],
                         rope_m[0], rope_m[1], ctx_out)
    y = _gated_merge([ya, yb, yr, ym], z[12], w_branch, w_out)
    yc = _gated_merge([yca, ycb, ycr, ycm], zc[12], w_branch, w_out) if ctx_out else None
    return y, yc

def _swiglu(h, wg, wu, wd):
    return (jax.nn.silu(h @ wg) * (h @ wu)) @ wd

def _moe(h, w_router, b_router, wg, wu, wd):
    logits = (h @ w_router).astype(jnp.float32) + b_router.astype(jnp.float32)
    probs = jax.nn.softmax(logits, axis=-1)
    top_p, top_i = lax.top_k(probs, TOP_K)
    top_p = top_p / jnp.sum(top_p, axis=-1, keepdims=True)
    combine = jnp.sum(jax.nn.one_hot(top_i, N_EXPERTS, dtype=jnp.float32) * top_p[..., None], axis=-2)
    out = None
    for e in range(N_EXPERTS):
        term = combine[..., e:e + 1].astype(h.dtype) * _swiglu(h, wg[e], wu[e], wd[e])
        out = term if out is None else out + term
    return out

def _channel_mixer(hh, l, ffn_w_gate, ffn_w_up, ffn_w_down, moe_w_router, moe_b_router, moe_w_gate, moe_w_up, moe_w_down):
    i = l // 2
    if l % 2 == 0:
        return _swiglu(hh, ffn_w_gate[i], ffn_w_up[i], ffn_w_down[i])
    return _moe(hh, moe_w_router[i], moe_b_router[i], moe_w_gate[i], moe_w_up[i], moe_w_down[i])

def setup_inputs(seed: int = 0) -> dict:
    key = jax.random.key(seed)
    ks = iter(list(jax.random.split(key, 64)))
    D = D_MODEL

    def nrm(shape, s):
        return jax.random.normal(next(ks), shape, jnp.float32) * s

    def uni(shape, lo, hi):
        return jax.random.uniform(next(ks), shape, jnp.float32, lo, hi)

    def gain(shape):
        return 1.0 + nrm(shape, 0.05)

    return {
        'x': nrm((BATCH, SEQ, D), 1.0),
        'c': nrm((BATCH, D), 1.0),
        'ctx': nrm((BATCH, CTX_LEN, D), 1.0),
        'c_ctx': nrm((D,), 1.0),
        'w_mod': nrm((DEPTH, D, 6 * D), 0.5 * D ** -0.5),
        'b_mod': nrm((DEPTH, 6 * D), 0.02),
        'norm_mix_pre': gain((DEPTH, D)),
        'norm_mix_post': gain((DEPTH, D)),
        'norm_ffn_pre': gain((DEPTH, D)),
        'norm_ffn_post': gain((DEPTH, D)),
        'w_in': nrm((DEPTH, D, P_IN), D ** -0.5),
        'gqa_q_norm': gain((DEPTH, HEAD_DIM)),
        'gqa_k_norm': gain((DEPTH, HEAD_DIM)),
        'na_rpb': nrm((DEPTH, NA_HEADS, 2 * NA_WIN_R - 1, 2 * NA_WIN_C - 1), 0.1),
        'rwkv_mu_x': uni((DEPTH, 3, D), 0.0, 1.0),
        'rwkv_mu_p': uni((DEPTH, 3, RWKV_W), 0.0, 1.0),
        'rwkv_w0': uni((DEPTH, 2, RWKV_W), -6.0, -1.0),
        'rwkv_w1': nrm((DEPTH, 2, D, RWKV_DECAY_LORA), D ** -0.5),
        'rwkv_w2': nrm((DEPTH, 2, RWKV_DECAY_LORA, RWKV_W), 0.5 * RWKV_DECAY_LORA ** -0.5),
        'rwkv_a0': nrm((DEPTH, 2, RWKV_W), 0.5),
        'rwkv_a1': nrm((DEPTH, 2, D, RWKV_AAA_LORA), D ** -0.5),
        'rwkv_a2': nrm((DEPTH, 2, RWKV_AAA_LORA, RWKV_W), 0.5 * RWKV_AAA_LORA ** -0.5),
        'rwkv_g1': nrm((DEPTH, 2, D, RWKV_GATE_LORA), D ** -0.5),
        'rwkv_g2': nrm((DEPTH, 2, RWKV_GATE_LORA, RWKV_W), RWKV_GATE_LORA ** -0.5),
        'rwkv_k_k': 0.85 + nrm((DEPTH, RWKV_W), 0.05),
        'rwkv_k_a': 1.0 + nrm((DEPTH, RWKV_W), 0.05),
        'rwkv_r_k': nrm((DEPTH, RWKV_HEADS, RWKV_N), 0.1),
        'rwkv_ln_w': gain((DEPTH, RWKV_W)),
        'rwkv_ln_b': nrm((DEPTH, RWKV_W), 0.02),
        'mla_q_norm': gain((DEPTH, MLA_Q_LORA)),
        'mla_w_uq': nrm((DEPTH, MLA_Q_LORA, MLA_HEADS * (MLA_NOPE + MLA_ROPE)), MLA_Q_LORA ** -0.5),
        'mla_kv_norm': gain((DEPTH, MLA_KV_LORA)),
        'mla_w_ukv': nrm((DEPTH, MLA_KV_LORA, MLA_HEADS * (MLA_NOPE + MLA_V)), MLA_KV_LORA ** -0.5),
        'w_branch': nrm((DEPTH, MIX_W, D), NA_W ** -0.5),
        'w_out': nrm((DEPTH, D, D), D ** -0.5),
        'ffn_w_gate': nrm((N_DENSE, D, DENSE_FF), D ** -0.5),
        'ffn_w_up': nrm((N_DENSE, D, DENSE_FF), D ** -0.5),
        'ffn_w_down': nrm((N_DENSE, DENSE_FF, D), DENSE_FF ** -0.5),
        'moe_w_router': nrm((N_MOE, D, N_EXPERTS), D ** -0.5),
        'moe_b_router': nrm((N_MOE, N_EXPERTS), 0.01),
        'moe_w_gate': nrm((N_MOE, N_EXPERTS, D, EXPERT_FF), D ** -0.5),
        'moe_w_up': nrm((N_MOE, N_EXPERTS, D, EXPERT_FF), D ** -0.5),
        'moe_w_down': nrm((N_MOE, N_EXPERTS, EXPERT_FF, D), EXPERT_FF ** -0.5),
    }

def reference(x, c, ctx, c_ctx, w_mod, b_mod, norm_mix_pre, norm_mix_post, norm_ffn_pre, norm_ffn_post,
              w_in, gqa_q_norm, gqa_k_norm, na_rpb,
              rwkv_mu_x, rwkv_mu_p, rwkv_w0, rwkv_w1, rwkv_w2, rwkv_a0, rwkv_a1, rwkv_a2,
              rwkv_g1, rwkv_g2, rwkv_k_k, rwkv_k_a, rwkv_r_k, rwkv_ln_w, rwkv_ln_b,
              mla_q_norm, mla_w_uq, mla_kv_norm, mla_w_ukv, w_branch, w_out,
              ffn_w_gate, ffn_w_up, ffn_w_down,
              moe_w_router, moe_b_router, moe_w_gate, moe_w_up, moe_w_down):
    n_lat = x.shape[1]
    rows = n_lat // GRID_W
    rope_h = _axial_rope_tables(n_lat, HEAD_DIM)
    rope_m = _axial_rope_tables(n_lat, MLA_ROPE)
    silu_c = jax.nn.silu(c)
    silu_cc = jax.nn.silu(c_ctx)
    xc = ctx
    for l in range(DEPTH):
        ctx_out = l < DEPTH - 1
        m = jnp.split((silu_c @ w_mod[l] + b_mod[l])[:, None, :], 6, axis=-1)
        mc = jnp.split(silu_cc @ w_mod[l] + b_mod[l], 6, axis=-1)
        rw = (rwkv_mu_x[l], rwkv_mu_p[l], rwkv_w0[l], rwkv_w1[l], rwkv_w2[l], rwkv_a0[l], rwkv_a1[l], rwkv_a2[l],
              rwkv_g1[l], rwkv_g2[l], rwkv_k_k[l], rwkv_k_a[l], rwkv_r_k[l], rwkv_ln_w[l], rwkv_ln_b[l])
        mla_p = (mla_q_norm[l], mla_w_uq[l], mla_kv_norm[l], mla_w_ukv[l])
        h = _modulate(_rms_norm(x, norm_mix_pre[l]), m[0], m[1])
        hc = _modulate(_rms_norm(xc, norm_mix_pre[l]), mc[0], mc[1])
        y, yc = _token_mixing(h, hc, rows, rope_h, rope_m, w_in[l], gqa_q_norm[l], gqa_k_norm[l], na_rpb[l],
                              rw, mla_p, w_branch[l], w_out[l], ctx_out)
        x = x + m[2] * _rms_norm(y, norm_mix_post[l])
        h = _modulate(_rms_norm(x, norm_ffn_pre[l]), m[3], m[4])
        x = x + m[5] * _rms_norm(_channel_mixer(h, l, ffn_w_gate, ffn_w_up, ffn_w_down, moe_w_router, moe_b_router,
                                                moe_w_gate, moe_w_up, moe_w_down), norm_ffn_post[l])
        if ctx_out:
            xc = xc + mc[2] * _rms_norm(yc, norm_mix_post[l])
            hc = _modulate(_rms_norm(xc, norm_ffn_pre[l]), mc[3], mc[4])
            xc = xc + mc[5] * _rms_norm(_channel_mixer(hc, l, ffn_w_gate, ffn_w_up, ffn_w_down, moe_w_router,
                                                      moe_b_router, moe_w_gate, moe_w_up, moe_w_down),
                                       norm_ffn_post[l])
    return x


_drawn_inputs = setup_inputs


def setup_inputs(seed=0):
    import zlib

    import numpy as np

    out = dict(_drawn_inputs(seed))
    spreads = {}
    factors = {'gqa_q_norm': 3.835,
     'gqa_k_norm': 4.971,
     'na_rpb': 17.837,
     'rwkv_ln_b': 12.446,
     'mla_q_norm': 4.882,
     'mla_kv_norm': 3.773,
     'moe_b_router': 2.683,
     'rwkv_w1': 3.162,
     'rwkv_w2': 4.627,
     'rwkv_k_k': 3.207,
     'rwkv_ln_w': 4.628}
    for name, (base, spread) in spreads.items():
        noise = np.random.default_rng([zlib.crc32(name.encode()), seed]).standard_normal(out[name].shape)
        drawn = base * np.exp(spread * noise) if base else spread * noise
        out[name] = jnp.asarray(drawn.astype(out[name].dtype))
    for name, factor in factors.items():
        out[name] = (out[name] * factor).astype(out[name].dtype)
    return out
```

```python
import math
from contextlib import ExitStack

import numpy as np
import concourse.bass as bass
from concourse import mybir

F32 = mybir.dt.float32
ALU = mybir.AluOpType
ACT = mybir.ActivationFunctionType
AX = mybir.AxisListType

P = 128
D = 1024
SEQ = 256
CTX = 256
TOK = CTX + SEQ
DEPTH = 2
GRID_W = 64
GRID_H = SEQ // GRID_W
KD = D // P
TILES = TOK // P
HEAD = 64
NORM_EPS = 1e-6
GN_EPS = 64e-5
FF = 2816
FFC = FF // P
EXPERTS = 8
EFF = 1408
EFC = EFF // P
CHUNK = 64
LEVELS = 6
DECAY = math.exp(-0.5)
NA_ROWS = 2 * 8 - 1
NA_COLS = 2 * 16 - 1
NEG = -1e30

BRANCH_CHUNKS = (4, 2, 2, 2)
BRANCH_FIRST = (0, 4, 6, 8)

Z_Q, Z_K, Z_NQ, Z_NK, Z_R, Z_RK, Z_RV, Z_LMU, Z_CQ, Z_CKV, Z_KR = 0, 4, 5, 7, 9, 11, 13, 15, 17, 20, 22
Z_CHUNKS = 23
Z_STREAM = ([(Z_Q + i, True) for i in range(4)] + [(Z_K, False)]
            + [(Z_NQ + i, True) for i in range(2)] + [(Z_NK + i, False) for i in range(2)]
            + [(Z_R + i, False) for i in range(6)]
            + [(Z_CQ + i, True) for i in range(3)] + [(Z_CKV + i, False) for i in range(2)] + [(Z_KR, False)])

SLAB = 8
RING = 6
MOD_SLABS = 6 * D // P
Z_SLABS = len(Z_STREAM)
Z_EVEN, Z_ODD = (Z_SLABS + 5) // 2, (Z_SLABS + 4) // 2
V_SLABS = 3
MLA_SLABS = 3
MERGE_SLABS = (4 * KD * KD + 10 * KD) // SLAB
OUT_SLABS = KD
FFN_SLABS = 2 * FFC + FFC * KD // SLAB
MOE_SLABS = EXPERTS * (2 * EFC + EFC * KD // SLAB)
LAYER_SLABS = [MOD_SLABS + Z_SLABS + V_SLABS + MLA_SLABS + MERGE_SLABS + OUT_SLABS + (FFN_SLABS, MOE_SLABS)[l] for l in range(DEPTH)]

V_BMOD, V_NMPRE, V_NMPOST, V_NFPRE, V_NFPOST = 0, 48, 56, 64, 72
V_MUP, V_QG, V_KG, V_MQ, V_MKV = 80, 86, 87, 88, 91
V_COLS = 93
B_W0, B_A0, B_KK, B_KA, B_RK, B_LNW, B_LNB = 0, 512, 1024, 1280, 1536, 1792, 2048
B_COLS = 2304
C_ID, C_ONES, C_BLK, C_ROT, C_ROTM, C_TRI, C_LEV, C_ROPE, C_EPS, C_LOW = 0, 128, 256, 384, 512, 640, 1152, 1920, 3968, 3970
C_COLS = 4034

RW_ORDER = ((0, 1, 2, 3), (1, 0, 3, 2))
CHUNK_ORDER = ((0, 1), (1, 0))


class Steps:

    def __init__(self, eng, sem):
        self.eng, self.sem, self.n = eng, sem, 0

    def did(self, ins):
        ins.then_inc(self.sem, 1)
        self.n += 1
        return ins

    def settle(self):
        if self.n:
            self.eng.wait_ge(self.sem, self.n)


def build(nc, t):
    ctx = ExitStack()
    with ctx:
        def sb(name, cols):
            return ctx.enter_context(nc.sbuf_tensor(name, [P, cols], F32))

        sems = {}

        def S(name):
            if name not in sems:
                sems[name] = ctx.enter_context(nc.semaphore(name))
            return sems[name]

        xT = sb("xT", KD * TOK)[:, :].rearrange("p (k t) -> p k t", k=KD)
        hT = sb("hT", KD * TOK)[:, :].rearrange("p (k t) -> p k t", k=KD)
        ring = sb("ring", RING * SLAB * P)[:, :].rearrange("p (r b c) -> p r b c", r=RING, b=SLAB)
        yflat = sb("yT", 10 * TOK)[:, :]
        yT = yflat.rearrange("p (k t) -> p k t", k=10)
        arena = sb("arena", Z_CHUNKS * TOK + KD * TOK + TILES * 640)[:, :]
        rkv = sb("rkv", TILES * 768)[:, :].rearrange("p (t c) -> p t c", t=TILES)
        kk = sb("kk", TILES * 256)[:, :].rearrange("p (t c) -> p t c", t=TILES)
        state = sb("state", 3 * 256)[:, :].rearrange("p (s j v) -> p s j v", s=3, j=4)
        lor = sb("lor", 2 * TOK)[:, :].rearrange("p (k t) -> p k t", k=2)
        yr = sb("yr", TILES * 256)[:, :].rearrange("p (t c) -> p t c", t=TILES)
        rows = sb("rows", B_COLS)[:, :]
        lora2 = sb("lora2", 512)[:, :]
        cst = sb("cst", C_COLS)[:, :]
        vec = sb("vec", V_COLS)[:, :]
        mux = sb("mux", 3 * KD)[:, :]
        wrt = sb("wrt", KD * EXPERTS + EXPERTS)[:, :]
        rstd = sb("rstd", TOK)[:, :]
        scT = sb("scT", KD * 2)[:, :].rearrange("p (k j) -> p k j", j=2)
        mod = sb("mod", 96)[:, :].rearrange("p (n j) -> p n j", j=2)
        gmod = sb("gmod", 64)[:, :].rearrange("p (w k j) -> p w k j", w=4, j=2)
        small = sb("small", 108)[:, :]
        bank = [ctx.enter_context(nc.psum_tensor(f"bank{i}", [P, 512], F32))[:, :] for i in range(8)]

        ident = cst[:, C_ID:C_ID + P]
        ones = cst[:, C_ONES:C_ONES + P]
        blk = cst[:, C_BLK:C_BLK + P]
        eps_col = cst[:, C_EPS:C_EPS + 1]
        gn_eps_col = cst[:, C_EPS + 1:C_EPS + 2]

        def tri(i):
            return cst[:, C_TRI + i * P:C_TRI + (i + 1) * P]

        def level(i):
            return cst[:, C_LEV + i * P:C_LEV + (i + 1) * P]

        def rope(i):
            return cst[:, C_ROPE + i * TOK:C_ROPE + (i + 1) * TOK]

        zT = arena[:, 0:Z_CHUNKS * TOK].rearrange("p (k t) -> p k t", k=Z_CHUNKS)
        MID = Z_CHUNKS * TOK
        mid = arena[:, MID:MID + KD * TOK].rearrange("p (k t) -> p k t", k=KD)
        VT = MID + KD * TOK
        vT = arena[:, VT:VT + TILES * 640].rearrange("p (t c) -> p t c", t=TILES)
        lw = arena[:, MID:MID + 2048].rearrange("p (g k c) -> p g k c", g=2, k=KD)
        lwm = arena[:, MID + 2048:MID + 4096].rearrange("p (g k c) -> p g k c", g=2, k=KD)
        sq = yflat[:, 0:6 * TOK].rearrange("p (g k t) -> p g k t", g=2, k=3)
        rsb = yflat[:, 6 * TOK:8 * TOK].rearrange("p (g t) -> p g t", g=2)
        rtmp = yflat[:, 8 * TOK:9 * TOK]
        bias = arena[:, Z_R * TOK:Z_R * TOK + 2048].rearrange("p (j h c) -> p j h c", j=2, h=4)
        ytm = arena[:, Z_RV * TOK:Z_RV * TOK + 2048].rearrange("p (s c) -> p s c", s=2)
        prob = arena[:, Z_CQ * TOK:Z_CQ * TOK + 1024].rearrange("p (s c) -> p s c", s=2)
        probT = arena[:, Z_CQ * TOK + 1024:Z_CQ * TOK + 2048].rearrange("p (s c) -> p s c", s=2)
        nmax = small[:, 0:2]
        bmax = small[:, 2:4]
        rsum = small[:, 4:6]
        rinv = small[:, 8:12]
        at = [0]

        def cut(n):
            at[0] += n
            return arena[:, at[0] - n:at[0]]

        sw, aa, gg, kd, bb, eL, eN, eX, eA, Bd, Be = (cut(512).rearrange("p (d c) -> p d c", d=2) for _ in range(11))
        fmt_flat = cut(2048)
        fmt = fmt_flat.rearrange("p (q a t) -> p q a t", q=4, a=4)
        am = cut(4096).rearrange("p (u a t) -> p u a t", u=8, a=4)
        ct = cut(2048).rearrange("p (s u t) -> p s u t", s=2, u=8)
        Tm = cut(1024).rearrange("p (u t) -> p u t", u=8)
        TT = cut(1024).rearrange("p (u t) -> p u t", u=8)
        Xs = cut(1024).rearrange("p (u t) -> p u t", u=8)
        m1 = cut(512).rearrange("p (q t) -> p q t", q=4)
        gh = cut(1024).rearrange("p (c x q v) -> p c x q v", c=2, x=2, q=4)
        g0, h0 = gh[:, :, 0], gh[:, :, 1]
        ecol = small[:, 100:108]
        assert at[0] <= VT + TILES * 640
        rhs2, nwu = Xs, Tm
        oo = fmt_flat[:, 0:512]
        t1, t2 = eN, Bd
        merged = arena[:, 0:KD * TOK].rearrange("p (k t) -> p k t", k=KD)
        yo = arena[:, KD * TOK:2 * KD * TOK].rearrange("p (k t) -> p k t", k=KD)
        gate_sb = vT.rearrange("p t c -> p (t c)")[:, 0:1024].rearrange("p (s t) -> p s t", s=2)
        prod = vT.rearrange("p t c -> p (t c)")[:, 1024:2048].rearrange("p (s t) -> p s t", s=2)
        hid = arena[:, 0:FFC * TOK].rearrange("p (k t) -> p k t", k=FFC)
        ehid = arena[:, 0:2 * EFC * SEQ].rearrange("p (s k t) -> p s k t", s=2, k=EFC)
        cw = arena[:, 2 * EFC * SEQ:2 * EFC * SEQ + EXPERTS * SEQ].rearrange("p (e t) -> p e t", e=EXPERTS)
        sqy = yflat[:, 0:KD * TOK].rearrange("p (k t) -> p k t", k=KD)
        rt = small[:, 12:]

        def qs(l):
            return slice(0, TOK) if l < DEPTH - 1 else slice(CTX, TOK)

        def segs(l):
            return [(slice(CTX, TOK), 0)] + ([(slice(0, CTX), 1)] if l < DEPTH - 1 else [])

        def qtiles(l):
            return range(TILES) if l < DEPTH - 1 else range(CTX // P, TILES)

        def units(l):
            return [(tt, h) for tt in qtiles(l) for h in range(16)]

        def unit_q(tt, h):
            c = slice(tt * P, (tt + 1) * P)
            if h < 8:
                return zT[64 * (h // 4):64 * (h // 4) + 64, Z_Q + h % 4, c]
            if h < 12:
                return zT[64 * (h % 2):64 * (h % 2) + 64, Z_NQ + (h - 8) // 2, c]
            return mid[:, h - 12, c]

        def unit_keys(tt):
            return CTX if tt < CTX // P else TOK

        def unit_k(tt, h):
            c = slice(0, unit_keys(tt))
            if h < 8:
                return zT[64 * (h // 4):64 * (h // 4) + 64, Z_K, c]
            if h < 12:
                return zT[64 * (h % 2):64 * (h % 2) + 64, Z_NK + (h - 8) // 2, c]
            return mid[:, 4 + h - 12, c]

        def unit_v(h, j):
            col = 64 * (h // 4) if h < 8 else 128 + 64 * (h - 8) if h < 12 else 384 + 64 * (h - 12)
            return vT[:, j, col:col + 64]

        def unit_scale(h):
            return HEAD ** -0.5 if h < 12 else 96 ** -0.5

        NORMS = [([Z_Q + i], blk, HEAD, [V_QG]) for i in range(4)] + [([Z_K], blk, HEAD, [V_KG]),
                 ([Z_CQ + i for i in range(3)], ones, 384, [V_MQ + i for i in range(3)]),
                 ([Z_CKV + i for i in range(2)], ones, 256, [V_MKV + i for i in range(2)])]

        def norm_cols(l, g):
            return qs(l) if g < 4 or g == 5 else slice(0, TOK)

        def rotations(l):
            gq = [(zT[:, Z_Q + i, :], qs(l), 0) for i in range(4)] + [(zT[:, Z_K, :], slice(0, TOK), 0)]
            return gq + [(zT[:, Z_KR, :], slice(0, TOK), 1)] + [(mid[:, i, :], qs(l), 1) for i in range(4)]

        T_LAT = CTX // P

        def out_rounds_before(l, j):
            return j if l == 0 else TILES + max(0, j - CTX // P)

        def turned(act, l, i):
            gi = (TILES if l else 0) + i
            tt = qtiles(l)[i]
            cols = slice(tt * P, (tt + 1) * P)
            act.wait_ge(S("turn_mm"), gi + 1)
            act.activation(yT[:, 0:4, cols], bank[5].rearrange("p (k t) -> p k t", k=4), ACT.Copy)
            act.activation(yT[:, 4:6, cols], bank[6][:, 0:256].rearrange("p (k t) -> p k t", k=2), ACT.Copy)
            act.activation(yT[:, 8:10, cols], bank[6][:, 256:512].rearrange("p (k t) -> p k t", k=2), ACT.Copy
                           ).then_inc(S("turn_ev"), 1)

        def turn(pe, l, base, i):
            gi = (TILES if l else 0) + i
            pe.wait_ge(S("o_ev"), base + 16 * (i + 1))
            if gi:
                pe.wait_ge(S("turn_ev"), gi)
            for k in range(8):
                ins = pe.transpose(bank[5 + k // 4][:, (k % 4) * P:(k % 4 + 1) * P], ytm[:, i % 2, k * P:(k + 1) * P], ident)
            ins.then_inc(S("turn_mm"), 1)

        def post_out(l, which, m):
            w = qs(l).stop - qs(l).start
            if l % 2 and which:
                return bank[4 + m // 2][:, 256 * (m % 2):256 * (m % 2) + 256]
            return bank[4 + m % 4][:, 0:w]

        def post_bank_free(pe, l, which, m):
            if m >= 4:
                pe.wait_ge(S("po_sq"), KD * (2 * l + which) + m - 3)

        def post_norm(act, l, which):
            q, pc = qs(l), 2 * l + which
            dst = (yo, mid)[which]
            for m in range(KD):
                act.wait_ge(S("po_mm"), KD * pc + (m | 1 if l % 2 and which else m) + 1)
                act.activation(dst[:, m, q], post_out(l, which, m), ACT.Copy)
                act.activation(sqy[:, m, q], post_out(l, which, m), ACT.Square).then_inc(S("po_sq"), 1)
            act.wait_ge(S("po_ss"), pc + 1)
            act.activation(rstd[:, q], bank[0][:, 0:q.stop - q.start], ACT.Ln, bias=eps_col, scale=1.0 / D).then_inc(S("po_ln"), 1)
            act.wait_ge(S("po_ln"), pc + 1)
            act.activation(rstd[:, q], rstd[:, q], ACT.Exp, scale=-0.5).then_inc(S("po_rstd"), 1)

        def post_sum(pe, l, which):
            q, pc = qs(l), 2 * l + which
            for k in range(KD):
                pe.wait_ge(S("po_sq"), KD * pc + k + 1)
                ins = pe.matmul(bank[0][:, 0:q.stop - q.start], ones, sqy[:, k, q], start=k == 0, stop=k == KD - 1)
            ins.then_inc(S("po_ss"), 1)

        def residual(dve, V, l, which):
            q, pc = qs(l), 2 * l + which
            y = (yo, mid)[which]
            dve.wait_ge(S("po_rstd"), pc + 1)
            for k in range(KD):
                V.did(dve.tensor_tensor(y[:, k, q], y[:, k, q], rstd[:, q], ALU.mult))
            V.settle()
            for k in range(KD):
                for cc, jc in segs(l):
                    ins = dve.scalar_tensor_tensor(out=xT[:, k, cc], in0=y[:, k, cc], scalar=gmod[:, 2 * which + 1, k, jc:jc + 1],
                                                   in1=xT[:, k, cc], op0=ALU.mult, op1=ALU.add)
            name = f"xa{l}" if which == 0 else f"xb{l}"
            ins.then_inc(S(name), 1)
            dve.wait_ge(S(name), 1)

        RQ = 2 * 2
        ROUNDS = TILES
        LAYER_VEC_LOADS = 5
        block = ctx.enter_context(nc.Block())

        @block.sync
        def _(sp):
            sp.dma_start(cst, t["cst"]).then_inc(S("cst_in"), 16)
            sp.dma_start(scT, t["c2"]).then_inc(S("c_in"), 16)
            sp.dma_start(xT, t["x"]).then_inc(S("x_in"), 16)
            for n in range(sum(LAYER_SLABS)):
                if n >= RING:
                    sp.wait_ge(S("slab_used"), n - RING + 1)
                sp.dma_start(ring[:, n % RING], t["w"][n]).then_inc(S(f"slab_in{n % RING}"), 16)
            sp.wait_ge(S("xb1"), 1)
            sp.dma_start(t["out"], xT[:, :, CTX:TOK]).then_inc(S("out_done"), 16)
            sp.wait_ge(S("out_done"), 16)

        @block.gpsimd
        def _(pool):
            G = Steps(pool, S("pool_steps"))
            pool.dma_start(arena[0:32, 0:4096], t["sel"]).then_inc(S("rel_in"), 16)
            pool.dma_start(arena[0:32, 4096:4096 + 56], t["rpb"]).then_inc(S("rel_in"), 16)
            pool.dma_start(wrt, t["wr"]).then_inc(S("wr_in"), 16)
            pool.wait_ge(S("rel_ev"), 8)
            pool.dma_start(t["scratch"], hT.rearrange("p k t -> p (k t)")[0:56, :]).then_inc(S("rel_out"), 16)
            pool.wait_ge(S("rel_out"), 16)
            for l in range(DEPTH):
                if l:
                    pool.wait_ge(S(f"xb{l - 1}"), 1)
                pool.dma_start(vec, t["vec"][l]).then_inc(S("vec_in"), 16)
                pool.dma_start(mux, t["mux"][l]).then_inc(S("vec_in"), 16)
                pool.dma_start(rows, t["rows"][l:l + 1, :].broadcast_to([P, B_COLS])).then_inc(S("vec_in"), 16)
                pool.dma_start(lora2, t["lora2"][l]).then_inc(S("vec_in"), 16)
                pool.dma_start(lw, t["lw"][l]).then_inc(S("vec_in"), 16)
                pool.wait_ge(S("rkv_a"), TILES * (l + 1))
                pool.wait_ge(S("rkv_d"), TILES * (l + 1))
                for r in range(GRID_H):
                    for h in range(4):
                        first = (l * 4 + h) * 7 + GRID_H - 1 - r
                        pool.dma_start(bias[64 * (r % 2):64 * (r % 2) + 64, r // 2, h, :].rearrange("p (r c) -> p r c", r=GRID_H),
                                       t["scratch"][first:first + GRID_H, :].rearrange("r (q c) -> q r c", q=GRID_W)
                                       ).then_inc(S("bias_in"), 16)
                for j in range(ROUNDS):
                    rr = l * ROUNDS + j
                    for lev in range(1, LEVELS):
                        for d in range(2):
                            n = (lev - 1) % 2
                            if lev == 1 and d == 0:
                                pool.wait_ge(S("am_done"), 8 * (rr + 1))
                            if lev > 2:
                                pool.wait_ge(S("x_mm"), 10 * rr + 2 * (lev - 3) + d + 1)
                            pool.tensor_tensor(ct[:, n, 4 * d:4 * d + 4, :], am[:, 4 * d:4 * d + 4, 0, :],
                                               level(lev).unsqueeze(1).broadcast_to([P, 4, P]), ALU.mult
                                               ).then_inc(S("ct_done"), 1)
                    pool.wait_ge(S("yt_mm"), 10 * (rr + 1))
                    for d in range(2):
                        pool.tensor_copy(rhs2[:, 4 * d:4 * d + 4, 0:64],
                                         eX[:, d, :].rearrange("p (h c) -> p h c", h=4)).then_inc(S("rhs_left"), 1)

        @block.scalar
        def _(act):
            A = Steps(act, S("act_steps"))

            def rsqrt(out, src, scale, eps, sem):
                A.did(act.activation(out, src, ACT.Ln, bias=eps, scale=scale))
                A.settle()
                act.activation(out, out, ACT.Exp, scale=-0.5).then_inc(sem, 1)

            act.wait_ge(S("c_in"), 16)
            act.activation(scT, scT, ACT.Silu).then_inc(S("silu_c"), 1)
            act.wait_ge(S("cst_in"), 16)
            for l in range(DEPTH):
                q, n0 = qs(l), qs(l).start
                if l == 0:
                    act.wait_ge(S("x_in"), 16)
                    act.wait_ge(S("rel_out"), 16)
                else:
                    act.wait_ge(S(f"xb{l - 1}"), 1)
                for k in range(KD):
                    act.activation(hT[:, k, :], xT[:, k, :], ACT.Square).then_inc(S("na_sq"), 1)
                act.wait_ge(S("na_ss"), l + 1)
                rsqrt(rstd, bank[0], 1.0 / D, eps_col, S("na_rstd"))
                for i in range(0, Z_SLABS + 4, 2):
                    act.wait_ge(S("z_mm"), (Z_SLABS + 4) * l + i + 1)
                    if i < Z_SLABS:
                        c, qonly = Z_STREAM[i]
                        dst, cc = zT[:, c, :], (q if qonly else slice(0, TOK))
                    else:
                        g = i - Z_SLABS
                        dst, cc = (lor[:, g, :] if g < 2 else zT[:, Z_LMU + g - 2, :]), slice(0, TOK)
                    act.activation(dst[:, cc], bank[i % 4][:, 0:cc.stop - cc.start], ACT.Copy).then_inc(S("z_ev_a"), 1)
                for tt in range(TILES):
                    act.wait_ge(S("v_mm"), TILES * l + tt + 1)
                    act.activation(vT[:, tt, 0:384], bank[4 + tt][:, 0:384], ACT.Copy).then_inc(S("v_ev"), 1)
                act.wait_ge(S("shifted"), l + 1)
                act.activation(lor[0:64, 0, :], lor[0:64, 0, :], ACT.Tanh).then_inc(S("lor_ready"), 1)
                act.activation(lor[:, 1, :], lor[:, 1, :], ACT.Sigmoid).then_inc(S("lor_ready"), 1)
                for tt in range(TILES):
                    act.wait_ge(S("rkv_tr"), 2 * TILES * l + 2 * tt + 1)
                    act.activation(rkv[:, tt, 0:512], bank[2 * (tt % 2)], ACT.Copy).then_inc(S("rkv_a"), 1)
                act.wait_ge(S("kk_ss"), l + 1)
                A.did(act.activation(rt[:, 0:16], rt[:, 0:16], ACT.Ln))
                A.settle()
                act.activation(rt[:, 0:16], rt[:, 0:16], ACT.Exp, scale=-0.5).then_inc(S("kk_rs"), 1)
                for g, (chunks, _m, width, _g) in enumerate(NORMS):
                    gi, cc = len(NORMS) * l + g, norm_cols(l, g)
                    if g >= 2:
                        act.wait_ge(S("qk_ss"), gi - 1)
                    elif g == 0:
                        act.wait_ge(S("lor_ready"), 2 * (l + 1))
                    for i, c in enumerate(chunks):
                        last = act.activation(sq[:, g % 2, i, cc], zT[:, c, cc], ACT.Square)
                    last.then_inc(S("qk_sq"), 1)
                    act.wait_ge(S("qk_ss"), gi + 1)
                    if g >= 2:
                        act.wait_ge(S("qk_norm"), gi - 1)
                    w = cc.stop - cc.start
                    rsqrt(rsb[:, g % 2, cc], bank[g % 2][:, 0:w], 1.0 / width, eps_col, S("qk_rs"))
                for h in range(4):
                    act.wait_ge(S("uq_mm"), 4 * l + h + 1)
                    act.activation(mid[:, h, q], bank[4 + h % 2][:, 0:q.stop - n0], ACT.Copy).then_inc(S("uq_ev"), 1)
                for tt in range(TILES):
                    act.wait_ge(S("uv_mm"), TILES * l + tt + 1)
                    act.activation(vT[:, tt, 384:640], bank[6 + tt % 2][:, 0:256], ACT.Copy).then_inc(S("uv_ev"), 1)
                base = sum(len(units(i)) for i in range(l))
                U = units(l)
                for u, (tt, h) in enumerate(U):
                    n = unit_keys(tt)
                    act.wait_ge(S("smax"), base + u + 1)
                    src = bank[u % 2][:, 0:n]
                    if 8 <= h < 12 and n == TOK:
                        src = prob[:, u % 2, 0:n]
                        sc = 1.0
                    else:
                        sc = unit_scale(h)
                    if u >= 2:
                        act.wait_ge(S("pt_mm"), base + u - 1)
                        act.wait_ge(S("rinv"), base + u - 1)
                    act.activation(prob[:, u % 2, 0:n], src, ACT.Exp, bias=nmax[:, u % 2:u % 2 + 1], scale=sc,
                                   accum_out=rsum[:, u % 2:u % 2 + 1]).then_inc(S("exp"), 1)
                    if u % 16 == 3 and u > 16:
                        turned(act, l, u // 16 - 1)
                turned(act, l, len(U) // 16 - 1)
                for j in range(ROUNDS):
                    rr = l * ROUNDS + j
                    out = RW_ORDER[0][j] in qtiles(l)
                    act.wait_ge(S("w_pre"), 2 * rr + 1)
                    act.activation(sw, sw, ACT.Sigmoid).then_inc(S("w_sig"), 1)
                    act.wait_ge(S("w_pre"), 2 * rr + 2)
                    act.activation(aa, aa, ACT.Sigmoid).then_inc(S("w_sig"), 1)
                    act.wait_ge(S("w_mm"), 3 * rr + 3)
                    for d in range(2):
                        ins = act.activation(gg[:, d], bank[4 + d][:, 0:256], ACT.Copy)
                    ins.then_inc(S("gg"), 1)
                    act.wait_ge(S("cum"), rr + 1)
                    for dst, b, s in ((eL, 3, -DECAY), (eN, 3, DECAY), (eX, 4, -DECAY), (eA, 5, -DECAY)):
                        act.activation(dst, bank[b].rearrange("p (d c) -> p d c", d=2), ACT.Exp, scale=s
                                       ).then_inc(S("decays"), 1)
                    for c in range(2):
                        act.activation(ecol[:, 4 * c:4 * c + 4], bank[6 + c][:, 0:4], ACT.Exp, scale=-DECAY).then_inc(S("decays"), 1)
                    for i in range(0, RQ, 2):
                        act.wait_ge(S("fm_tr"), RQ * rr + i + 1)
                        act.activation(fmt[:, i], bank[i].rearrange("p (a t) -> p a t", a=4), ACT.Copy
                                       ).then_inc(S("fm_a"), 1)
                    for d in range(2):
                        act.wait_ge(S("t_tr"), 2 * rr + d + 1)
                        act.activation(Tm[:, 4 * d:4 * d + 4], bank[d].rearrange("p (u t) -> p u t", u=4), ACT.Copy
                                       ).then_inc(S("t_ev"), 1)
                    for lev in range(1, LEVELS):
                        for d in range(2):
                            act.wait_ge(S("x_mm"), 10 * rr + 2 * (lev - 1) + d + 1)
                            if lev > 1:
                                act.wait_ge(S("yt_mm"), 10 * rr + 2 * (lev - 2) + d + 1)
                            act.activation(Xs[:, 4 * d:4 * d + 4], bank[2 + d].rearrange("p (u t) -> p u t", u=4),
                                           ACT.Copy).then_inc(S("x_ev"), 1)
                    act.wait_ge(S("av_mm"), rr + 1)
                    act.activation(rhs2[:, :, 64:128], bank[0].rearrange("p (u c) -> p u c", u=8), ACT.Copy
                                   ).then_inc(S("av_ev"), 1)
                    for d in range(2):
                        act.wait_ge(S("wu_mm"), 2 * rr + d + 1)
                        act.activation(nwu[:, 4 * d:4 * d + 4], bank[2 + d].rearrange("p (u c) -> p u c", u=4),
                                       ACT.Copy, scale=-1.0).then_inc(S("nwu"), 1)
                    act.wait_ge(S("g0_mm"), rr + 1)
                    for c in range(2):
                        act.activation(gh[:, c], bank[(5, 1)[c]].rearrange("p (x q v) -> p x q v", x=2, q=4), ACT.Copy
                                       ).then_inc(S("g0_ev"), 1)
                    if out:
                        no = out_rounds_before(l, j)
                        act.wait_ge(S("o_var"), no + 1)
                        A.did(act.activation(rt[:, 16:24], rt[:, 16:24], ACT.Ln, scale=1.0 / HEAD, bias=gn_eps_col))
                        A.settle()
                        act.activation(rt[:, 16:24], rt[:, 16:24], ACT.Exp, scale=-0.5).then_inc(S("o_rs"), 1)
                for i, tt in enumerate(qtiles(l)):
                    act.wait_ge(S("yr_tr"), (TILES * l if l else 0) + i + 1)
                    act.activation(yT[:, 6:8, tt * P:(tt + 1) * P], bank[i % 2][:, 0:256].rearrange("p (k t) -> p k t", k=2),
                                   ACT.Copy).then_inc(S("yr_ev"), 1)
                w = q.stop - n0
                for i in range(4 * KD):
                    gi = 4 * KD * l + i
                    act.wait_ge(S("gate_mm"), gi + 1)
                    if i >= 2:
                        act.wait_ge(S("gated"), gi - 1)
                    act.activation(gate_sb[:, i % 2, 0:w], bank[i % 2][:, 0:w], ACT.Sigmoid).then_inc(S("gate"), 1)
                post_norm(act, l, 0)
                act.wait_ge(S(f"xa{l}"), 1)
                for k in range(KD):
                    act.activation(hT[:, k, q], xT[:, k, q], ACT.Square).then_inc(S("nb_sq"), 1)
                act.wait_ge(S("nb_ss"), l + 1)
                rsqrt(rstd[:, q], bank[0][:, 0:w], 1.0 / D, eps_col, S("nb_rstd"))
                if l % 2 == 0:
                    for j in range(FFC):
                        act.wait_ge(S("fg_mm"), j + 1)
                        if j >= 2:
                            act.wait_ge(S("hid"), j - 1)
                        act.activation(gate_sb[:, j % 2, 0:w], bank[j % 2][:, 0:w], ACT.Silu).then_inc(S("silu"), 1)
                else:
                    act.wait_ge(S("r_max"), 1)
                    for i in range(2):
                        act.activation(rt[:, 32 + 8 * i:40 + 8 * i], rt[:, 32 + 8 * i:40 + 8 * i], ACT.Exp,
                                       bias=rt[:, 48 + i:49 + i]).then_inc(S("r_exp"), 1)
                    for i in range(4):
                        act.wait_ge(S("cw_mm"), i + 1)
                        act.activation(cw[:, 2 * i:2 * i + 2], bank[i].rearrange("p (e t) -> p e t", e=2), ACT.Copy
                                       ).then_inc(S("cw_ev"), 1)
                    for e in range(EXPERTS):
                        for j in range(EFC):
                            i = e * EFC + j
                            act.wait_ge(S("eg_mm"), i + 1)
                            if i >= 2:
                                act.wait_ge(S("ehid"), i - 1)
                            act.activation(gate_sb[:, i % 2, 0:w], bank[i % 2][:, 0:w], ACT.Silu).then_inc(S("esilu"), 1)
                post_norm(act, l, 1)

        @block.tensor
        def _(pe):
            slabs, owed = [0], [0]

            def mm(out, lhsT, rhs, start=True, stop=True, skip=False):
                return pe.matmul(out, lhsT, rhs, start=start, stop=stop, skip_group_check=skip)

            def slab():
                n = slabs[0]
                slabs[0] += 1
                pe.wait_ge(S(f"slab_in{n % RING}"), 16 * (n // RING + 1))
                return ring[:, n % RING]

            blocks = [None, SLAB]

            def next_block():
                fresh = blocks[1] == SLAB
                if fresh:
                    blocks[0], blocks[1] = slab(), 0
                blocks[1] += 1
                return blocks[0][:, blocks[1] - 1, :], fresh

            def product(out, rhs_of, n, start=True, done=None):
                for k in range(n):
                    w, fresh = next_block()
                    ins = mm(out, w, rhs_of(k), start=(k == 0 and start), stop=(k == n - 1))
                    owed[0] += fresh and slabs[0] > 1
                    if owed[0] and k < n - 1:
                        ins.then_inc(S("slab_used"), owed[0])
                        owed[0] = 0
                if done:
                    ins.then_inc(S(done), 1)

            def slab_rest():
                out = [blocks[0][:, n, :] for n in range(blocks[1], SLAB)]
                blocks[1] = SLAB
                return out

            pe.wait_ge(S("rel_in"), 32)
            for i in range(8):
                mm(bank[i][0:56, :], arena[0:32, 4096:4152], arena[0:32, 512 * i:512 * i + 512]).then_inc(S("rel_mm"), 1)
            pe.wait_ge(S("rel_ev"), 8)
            pe.wait_ge(S("cst_in"), 16)
            pe.wait_ge(S("silu_c"), 1)
            for l in range(DEPTH):
                q, n0 = qs(l), qs(l).start
                w = q.stop - n0
                if l:
                    pe.wait_ge(S(f"xb{l - 1}"), 1)
                for n in range(6 * KD):
                    product(bank[7][:, 2 * n:2 * n + 2], lambda k: scT[:, k, :], KD, done="mod_mm" if n == 6 * KD - 1 else None)
                for k in range(KD):
                    pe.wait_ge(S("na_sq"), KD * l + k + 1)
                    last = mm(bank[0], ones, hT[:, k, :], k == 0, k == KD - 1)
                last.then_inc(S("na_ss"), 1)
                for i in range(Z_SLABS):
                    qonly = Z_STREAM[i][1]
                    cc = q if qonly else slice(0, TOK)
                    if i >= 4:
                        pe.wait_ge(S(("z_ev_a", "z_ev_d")[i % 2]), (Z_EVEN, Z_ODD)[i % 2] * l + (i - 4) // 2 + 1)
                    elif i == 0:
                        pe.wait_ge(S("ha"), l + 1)
                    product(bank[i % 4][:, 0:cc.stop - cc.start], lambda k: hT[:, k, cc], KD, done="z_mm")
                for g in range(4):
                    i = Z_SLABS + g
                    pe.wait_ge(S(("z_ev_a", "z_ev_d")[i % 2]), (Z_EVEN, Z_ODD)[i % 2] * l + (i - 4) // 2 + 1)
                    if g == 0:
                        pe.wait_ge(S("vec_in"), 16 * LAYER_VEC_LOADS * (l + 1))
                    if g == 2:
                        pe.wait_ge(S("lwm"), l + 1)
                    for k in range(KD):
                        ins = mm(bank[i % 4], (lw, lwm)[g // 2][:, g % 2, k, :], hT[:, k, :], k == 0, k == KD - 1)
                    ins.then_inc(S("z_mm"), 1)
                pe.wait_ge(S("mod_ready"), l + 1)
                for s in range(V_SLABS):
                    wv = slab()
                    for tt in range(TILES):
                        for k in range(KD):
                            ins = mm(bank[4 + tt][:, s * P:(s + 1) * P], hT[:, k, tt * P:(tt + 1) * P], wv[:, k, :],
                                     k == 0, k == KD - 1)
                            if tt == 0 and k == 0:
                                ins.then_inc(S("slab_used"), 1)
                        if s == V_SLABS - 1:
                            ins.then_inc(S("v_mm"), 1)
                pe.wait_ge(S("shifted"), l + 1)
                pe.wait_ge(S("z_ev_a"), Z_EVEN * (l + 1))
                for tt in range(TILES):
                    b = 2 * (tt % 2)
                    if tt >= 2:
                        pe.wait_ge(S("rkv_a"), TILES * l + tt - 1)
                        pe.wait_ge(S("rkv_d"), TILES * l + tt - 1)
                    for i in range(6):
                        ins = pe.transpose(bank[b + i // 4][:, (i % 4) * P:(i % 4 + 1) * P], zT[:, Z_R + i, tt * P:(tt + 1) * P], ident)
                        if i in (3, 5):
                            ins.then_inc(S("rkv_tr"), 1)
                pe.wait_ge(S("rkv_a"), TILES * (l + 1))
                pe.wait_ge(S("rkv_d"), TILES * (l + 1))
                for g, (chunks, ones_of, width, _g) in enumerate(NORMS):
                    gi, cc = len(NORMS) * l + g, norm_cols(l, g)
                    pe.wait_ge(S("qk_sq"), gi + 1)
                    if g >= 2:
                        pe.wait_ge(S("qk_rs"), gi - 1)
                    for i in range(len(chunks)):
                        ins = mm(bank[g % 2][:, 0:cc.stop - cc.start], ones_of, sq[:, g % 2, i, cc], i == 0, i == len(chunks) - 1)
                    ins.then_inc(S("qk_ss"), 1)
                pe.wait_ge(S("qk_norm"), len(NORMS) * (l + 1))
                pe.wait_ge(S("v_ev"), TILES * (l + 1))
                for h in range(4):
                    if h >= 2:
                        pe.wait_ge(S("uq_ev"), 4 * l + h - 1)
                    product(bank[4 + h % 2][:, 0:w], lambda k: zT[:, Z_CQ + k, q], 3, done="uq_mm")
                ROT = 2
                for i, (x, cc, kind) in enumerate(rotations(l)):
                    if i == 6:
                        for h in range(4):
                            if h == 0:
                                pe.wait_ge(S("uq_ev"), 4 * l + 4)
                            if h < 2:
                                pe.wait_ge(S("rot"), 10 * l + 6)
                            else:
                                pe.wait_ge(S("uk_ev"), 4 * l + h - 1)
                            product(bank[4 + h % 2], lambda k: zT[:, Z_CKV + k, :], 2, done="uk_mm")
                    if i >= 2:
                        pe.wait_ge(S("rot"), 10 * l + i - 1)
                    mm(bank[2 + i % 2][:, 0:cc.stop - cc.start], cst[:, C_ROT + kind * P:C_ROT + (kind + 1) * P],
                       x[:, cc]).then_inc(S("rot_mm"), 1)
                wuv = slab_rest()
                for tt in range(TILES):
                    if tt >= 2:
                        pe.wait_ge(S("uv_ev"), TILES * l + tt - 1)
                    for s in range(2):
                        for k in range(2):
                            ins = mm(bank[6 + tt % 2][:, s * P:(s + 1) * P], zT[:, Z_CKV + k, tt * P:(tt + 1) * P],
                                     wuv[2 * s + k], k == 0, k == 1)
                    ins.then_inc(S("uv_mm"), 1)
                pe.wait_ge(S("rot"), 10 * (l + 1))
                pe.wait_ge(S("uk_ev"), 4 * (l + 1))
                pe.wait_ge(S("uv_ev"), TILES * (l + 1))
                base, U = sum(len(units(i)) for i in range(l)), units(l)
                for step in range(len(U) + 2):
                    u = step
                    if u < len(U):
                        tt, h = U[u]
                        if u >= 2:
                            pe.wait_ge(S("exp"), base + u - 1)
                        mm(bank[u % 2][:, 0:unit_keys(tt)], unit_q(tt, h), unit_k(tt, h)).then_inc(S("s_mm"), 1)
                    u = step - 1
                    if 0 <= u < len(U):
                        pe.wait_ge(S("exp"), base + u + 1)
                        if u >= 2:
                            pe.wait_ge(S("pt_ev"), base + u - 1)
                        for j in range(unit_keys(U[u][0]) // P):
                            ins = pe.transpose(bank[2 + u % 2][:, j * P:(j + 1) * P], prob[:, u % 2, j * P:(j + 1) * P], ident)
                        ins.then_inc(S("pt_mm"), 1)
                    u = step - 2
                    if u >= 0:
                        pe.wait_ge(S("pt_ev"), base + u + 1)
                        if u >= 2:
                            pe.wait_ge(S("o_ev"), base + u - 1)
                        nk = unit_keys(U[u][0]) // P
                        for j in range(nk):
                            ins = mm(bank[(4, 7)[u % 2]][:, 0:HEAD], probT[:, u % 2, j * P:(j + 1) * P],
                                     unit_v(U[u][1], j), j == 0, j == nk - 1)
                        ins.then_inc(S("pv_mm"), 1)
                    if step % 16 == 3 and step > 16:
                        turn(pe, l, base, step // 16 - 1)
                turn(pe, l, base, len(U) // 16 - 1)
                pe.wait_ge(S("turn_ev"), (4 if l == 0 else 6))
                pe.wait_ge(S("lor_ready"), 2 * (l + 1))
                pe.wait_ge(S("kk_ready"), l + 1)
                for j in range(ROUNDS):
                    rr = l * ROUNDS + j
                    tau = [RW_ORDER[d][j] for d in range(2)]
                    out = RW_ORDER[0][j] in qtiles(l)
                    U8 = [(d, h, 4 * d + h, 2 * d + h // 2, slice(64 * (h % 2), 64 * (h % 2) + 64)) for d in range(2) for h in range(4)]

                    def v_of(d, h, rows_=slice(0, P)):
                        return rkv[rows_, tau[d], 512 + 64 * h:576 + 64 * h]

                    if out_rounds_before(l, j):
                        pe.wait_ge(S("o_read"), 2 * out_rounds_before(l, j))
                    for b in range(3):
                        for d in range(2):
                            if b < 2:
                                r0, g, c0, kr = 64 * b + 32 * d, 0, 0, 32
                            else:
                                r0, g, c0, kr = 64 * d, 1, 256, 64
                            ins = mm(bank[2 * b + d][:, 0:256], lor[r0:r0 + kr, g, tau[d] * P:(tau[d] + 1) * P],
                                     lora2[r0:r0 + kr, c0:c0 + 256])
                        ins.then_inc(S("w_mm"), 1)
                    pe.wait_ge(S("w_sig"), 2 * rr + 1)
                    pe.wait_ge(S("w_pre"), 2 * rr + 2)
                    pe.wait_ge(S("gg"), rr + 1)
                    for b, of in ((3, (1, 3)), (4, (0, 2)), (5, (2, 0))):
                        for d in range(2):
                            mm(bank[b][:, 256 * d:256 * d + 256], tri(of[d]), sw[:, d, :])
                    for d in range(2):
                        for hp in range(2):
                            for c in range(2):
                                ins = mm(bank[6 + c][:, 2 * d + hp:2 * d + hp + 1],
                                         sw[64 * c:64 * c + 64, d, P * hp:P * hp + P], ones[64 * c:64 * c + 64, 0:1])
                    ins.then_inc(S("cum"), 1)
                    for d in range(2):
                        pe.wait_ge(S("prod"), 2 * rr + d + 1)
                        for hp in range(2):
                            for a, x in enumerate((eX, eL, Bd, eN)):
                                ins = pe.transpose(bank[2 * d + hp][:, a * P:(a + 1) * P], x[:, d, P * hp:P * hp + P], ident)
                            ins.then_inc(S("fm_tr"), 1)
                    for d, h, u, qq, hh in U8:
                        if h % 2 == 0:
                            pe.wait_ge(S(("fm_a", "fm_d")[qq % 2]), 2 * rr + qq // 2 + 1)
                        if u >= 4:
                            pe.wait_ge(S("am_done"), 8 * rr + u - 3)
                        elif u == 0:
                            pe.wait_ge(S("decays"), 6 * (rr + 1))
                        b = bank[4 + u % 4]
                        mm(b[:, 0:256], fmt[hh, qq, 2], fmt[hh, qq, 0:2])
                        mm(b[:, 256:512], fmt[hh, qq, 3], fmt[hh, qq, 0:2]).then_inc(S("a_mm"), 1)
                    for d in range(2):
                        pe.wait_ge(S("tt0"), 2 * rr + d + 1)
                        for h in range(4):
                            ins = pe.transpose(bank[d][:, h * P:(h + 1) * P], TT[:, 4 * d + h], ident)
                        ins.then_inc(S("t_tr"), 1)
                    for lev in range(1, LEVELS):
                        for d in range(2):
                            pe.wait_ge(S("ct_done"), 10 * rr + 2 * (lev - 1) + d + 1)
                            if lev == 1:
                                pe.wait_ge(S("t_ev"), 2 * rr + d + 1)
                            else:
                                pe.wait_ge(S("inv"), 10 * rr + 2 * (lev - 2) + d + 1)
                            for h in range(4):
                                ins = mm(bank[2 + d][:, h * P:(h + 1) * P], ct[:, (lev - 1) % 2, 4 * d + h], Tm[:, 4 * d + h])
                            ins.then_inc(S("x_mm"), 1)
                        for d in range(2):
                            pe.wait_ge(S("x_ev"), 10 * rr + 2 * (lev - 1) + d + 1)
                            for h in range(4):
                                u = 4 * d + h
                                if lev < LEVELS - 1:
                                    mm(bank[4 + d][:, h * P:(h + 1) * P], TT[:, u], Xs[:, u])
                                ins = mm(bank[6 + d][:, h * P:(h + 1) * P], Xs[:, u], TT[:, u])
                            ins.then_inc(S("yt_mm"), 1)
                    for d, h, u, qq, hh in U8:
                        ins = mm(bank[0][:, 64 * u:64 * u + 64], am[:, u, 2], v_of(d, h))
                    ins.then_inc(S("av_mm"), 1)
                    pe.wait_ge(S("inv"), 10 * (rr + 1))
                    pe.wait_ge(S("av_ev"), rr + 1)
                    pe.wait_ge(S("rhs_left"), 2 * (rr + 1))
                    for d, h, u, qq, hh in U8:
                        ins = mm(bank[2 + d][:, h * P:(h + 1) * P], TT[:, u], rhs2[:, u])
                        if h == 3:
                            ins.then_inc(S("wu_mm"), 1)
                    pe.wait_ge(S("nwu"), 2 * (rr + 1))
                    for d, h, u, qq, hh in U8:
                        ins = mm(bank[4][hh, qq * P:(qq + 1) * P], nwu[:, u, 0:64], am[:, u, 1])
                    ins.then_inc(S("m1_mm"), 1)
                    pe.wait_ge(S("prod_end"), rr + 1)
                    for d, h, u, qq, hh in U8:
                        for c in range(2):
                            cs, b = slice(64 * c, 64 * c + 64), bank[(5, 1)[c]]
                            mm(b[hh, 64 * qq:64 * qq + 64], nwu[cs, u, 0:64], Be[cs, d, 64 * h:64 * h + 64])
                            o = b[hh, 256 + 64 * qq:320 + 64 * qq]
                            mm(o, Be[cs, d, 64 * h:64 * h + 64], nwu[cs, u, 64:128], True, False)
                            ins = mm(o, eA[cs, d, 64 * h:64 * h + 64], v_of(d, h, cs), False, True)
                    ins.then_inc(S("g0_mm"), 1)
                    pe.wait_ge(S("g0_ev"), 2 * (rr + 1))
                    for s in range(2):
                        pe.wait_ge(S("st"), 2 * rr + s + l + 1)
                        for d, h, u, qq, hh in U8:
                            ins = mm(bank[6][hh, 256 * s + 64 * qq:256 * s + 64 * qq + 64], g0[hh, CHUNK_ORDER[d][s], qq],
                                     state[hh, (2 * j + s) % 3, qq])
                        ins.then_inc(S("st_mm"), 1)
                    if out:
                        pe.wait_ge(S("m1"), rr + 1)
                        for d, h, u, qq, hh in U8:
                            o = bank[(7, 3)[h % 2]][:, 64 * qq:64 * qq + 64]
                            mm(o, am[:, u, 3], v_of(d, h), True, False, True)
                            mm(o, am[:, u, 1], nwu[:, u, 64:128], False, False, True)
                            for s in range(2):
                                c = CHUNK_ORDER[d][s]
                                cs = slice(64 * c, 64 * c + 64)
                                ins = mm(o[cs, :], m1[hh, qq, cs], state[hh, (2 * j + s) % 3, qq], False, s == 1, True)
                        ins.then_inc(S("o_mm"), 1)
                yb = TILES * l
                for i, tt in enumerate(qtiles(l)):
                    if i == 0:
                        pe.wait_ge(S("yr"), 4 if l == 0 else 6)
                    if i >= 2:
                        pe.wait_ge(S("yr_ev"), yb + i - 1)
                    for k in range(2):
                        ins = pe.transpose(bank[i % 2][:, k * P:(k + 1) * P], yr[:, tt, k * P:(k + 1) * P], ident)
                    ins.then_inc(S("yr_tr"), 1)
                pe.wait_ge(S("yr_ev"), yb + len(qtiles(l)))
                pe.wait_ge(S("st"), (2 * ROUNDS) * (l + 1) + l + 1)
                for i in range(4 * KD):
                    m, br = divmod(i, 4)
                    gi = 4 * KD * l + i
                    if i >= 2:
                        pe.wait_ge(S("gate"), gi - 1)
                    product(bank[i % 2][:, 0:w], lambda k: hT[:, k, q], KD, done="gate_mm")
                    if i >= 2:
                        pe.wait_ge(S("gated"), gi - 1)
                    product(bank[2 + i % 2][:, 0:w], lambda k: yT[:, BRANCH_FIRST[br] + k, q], BRANCH_CHUNKS[br], done="br_mm")
                pe.wait_ge(S("merged"), KD * (l + 1))
                for m in range(KD):
                    post_bank_free(pe, l, 0, m)
                    product(bank[4 + m % 4][:, 0:w], lambda k: merged[:, k, q], KD, done="po_mm")
                post_sum(pe, l, 0)
                for k in range(KD):
                    pe.wait_ge(S("nb_sq"), KD * l + k + 1)
                    if k == 0:
                        pe.wait_ge(S(f"xa{l}"), 1)
                    ins = mm(bank[0][:, 0:w], ones, hT[:, k, q], k == 0, k == KD - 1)
                ins.then_inc(S("nb_ss"), 1)
                pe.wait_ge(S("hb"), l + 1)
                if l % 2 == 0:
                    for j in range(FFC):
                        if j >= 2:
                            pe.wait_ge(S("silu"), j - 1)
                        product(bank[j % 2][:, 0:w], lambda k: hT[:, k, q], KD, done="fg_mm")
                        if j >= 2:
                            pe.wait_ge(S("hid"), j - 1)
                        product(bank[2 + j % 2][:, 0:w], lambda k: hT[:, k, q], KD, done="fu_mm")
                    pe.wait_ge(S("hid"), FFC)
                    for m in range(KD):
                        post_bank_free(pe, l, 1, m)
                        product(bank[4 + m % 4][:, 0:w], lambda k: hid[:, k, q], FFC, done="po_mm")
                else:
                    pe.wait_ge(S("wr_in"), 16)
                    for i in range(2):
                        for k in range(KD):
                            ins = mm(bank[0][:, 8 * i:8 * i + 8], hT[:, k, CTX + P * i:CTX + P * (i + 1)],
                                     wrt[:, 8 * k:8 * k + 8], k == 0, k == KD - 1)
                    ins.then_inc(S("r_mm"), 1)
                    pe.wait_ge(S("comb"), 1)
                    for e in range(EXPERTS):
                        for i in range(2):
                            ins = mm(bank[e // 2][:, 256 * (e % 2) + P * i:256 * (e % 2) + P * (i + 1)],
                                     rt[:, 64 + 8 * i + e:65 + 8 * i + e].broadcast_to([P, P]), ident)
                        if e % 2:
                            ins.then_inc(S("cw_mm"), 1)
                    pe.wait_ge(S("cw_ev"), 4)
                    for e in range(EXPERTS):
                        for j in range(EFC):
                            i = e * EFC + j
                            if i >= 2:
                                pe.wait_ge(S("esilu"), i - 1)
                            product(bank[i % 2][:, 0:w], lambda k: hT[:, k, q], KD, done="eg_mm")
                            if i >= 2:
                                pe.wait_ge(S("ehid"), i - 1)
                            product(bank[2 + i % 2][:, 0:w], lambda k: hT[:, k, q], KD, done="eu_mm")
                        pe.wait_ge(S("ehid"), EFC * (e + 1))
                        for m in range(KD):
                            for k in range(EFC):
                                wb, fresh = next_block()
                                ins = mm(bank[4 + m // 2][:, 256 * (m % 2):256 * (m % 2) + 256], wb, ehid[:, e % 2, k, :],
                                         e == 0 and k == 0 and m % 2 == 0, e == EXPERTS - 1 and k == EFC - 1, True)
                                owed[0] += fresh
                                if owed[0] and k < EFC - 1:
                                    ins.then_inc(S("slab_used"), owed[0])
                                    owed[0] = 0
                            if e == EXPERTS - 1:
                                ins.then_inc(S("po_mm"), 1)
                            elif m == KD - 1:
                                ins.then_inc(S("edown"), 1)
                post_sum(pe, l, 1)

        @block.vector
        def _(dve):
            V = Steps(dve, S("vec_steps"))
            vs = S("vec_steps")

            def bc(x, *shape):
                return x.broadcast_to(list(shape))

            for i in range(8):
                dve.wait_ge(S("rel_mm"), i + 1)
                if i == 0:
                    pass
                dve.tensor_copy(hT.rearrange("p k t -> p (k t)")[0:56, 512 * i:512 * i + 512], bank[i][0:56, :]).then_inc(S("rel_ev"), 1)
            dve.wait_ge(S("cst_in"), 16)
            for l in range(DEPTH):
                q, n0 = qs(l), qs(l).start
                w = q.stop - n0
                dve.wait_ge(S("vec_in"), 16 * LAYER_VEC_LOADS * (l + 1))
                for i, (g, c0, c1) in enumerate(((0, 0, 64), (0, 64, 128), (1, 0, 128))):
                    ins = dve.tensor_tensor(lwm[:, g, :, c0:c1], lw[:, g, :, c0:c1],
                                            bc(mux[:, 8 * i:8 * i + 8].unsqueeze(2), P, KD, c1 - c0), ALU.mult)
                ins.then_inc(S("lwm"), 1)
                dve.wait_ge(S("mod_mm"), l + 1)
                V.did(dve.tensor_tensor(mod, bank[7][:, 0:96].rearrange("p (n j) -> p n j", j=2),
                                        bc(vec[:, V_BMOD:V_BMOD + 48].unsqueeze(2), P, 48, 2), ALU.add))
                V.settle()
                for i, (sec, col) in enumerate(((1, V_NMPRE), (2, V_NMPOST), (4, V_NFPRE), (5, V_NFPOST))):
                    gain = bc(vec[:, col:col + KD].unsqueeze(2), P, KD, 2)
                    src = mod[:, 8 * sec:8 * sec + 8, :]
                    if sec in (1, 4):
                        ins = dve.scalar_tensor_tensor(out=gmod[:, i], in0=src, scalar=1.0, in1=gain, op0=ALU.add, op1=ALU.mult)
                    else:
                        ins = dve.tensor_tensor(gmod[:, i], src, gain, ALU.mult)
                ins.then_inc(S("mod_ready"), 1)
                dve.wait_ge(S("mod_ready"), l + 1)

                def modulated(which, shift, cols_segs):
                    for k in range(KD):
                        for cc, jc in cols_segs:
                            ins = V.did(dve.tensor_tensor(hT[:, k, cc], xT[:, k, cc], rstd[:, cc], ALU.mult))
                    V.settle()
                    for k in range(KD):
                        for cc, jc in cols_segs:
                            ins = dve.tensor_scalar(hT[:, k, cc], hT[:, k, cc], gmod[:, which, k, jc:jc + 1],
                                                    mod[:, 8 * shift + k, jc:jc + 1], ALU.mult, ALU.add)
                    return ins

                dve.wait_ge(S("na_rstd"), l + 1)
                modulated(0, 0, [(slice(CTX, TOK), 0), (slice(0, CTX), 1)]).then_inc(S("ha"), 1)
                for i in range(1, Z_SLABS + 4, 2):
                    dve.wait_ge(S("z_mm"), (Z_SLABS + 4) * l + i + 1)
                    if i < Z_SLABS:
                        c, qonly = Z_STREAM[i]
                        dst, cc = zT[:, c, :], (q if qonly else slice(0, TOK))
                    else:
                        g = i - Z_SLABS
                        dst, cc = (lor[:, g, :] if g < 2 else zT[:, Z_LMU + g - 2, :]), slice(0, TOK)
                    dve.tensor_copy(dst[:, cc], bank[i % 4][:, 0:cc.stop - cc.start]).then_inc(S("z_ev_d"), 1)
                dve.wait_ge(S("z_ev_a"), Z_EVEN * (l + 1))
                dve.wait_ge(S("z_ev_d"), Z_ODD * (l + 1))
                src = arena[:, Z_R * TOK:(Z_R + 8) * TOK].rearrange("p (s t) -> p s t", t=CTX)
                nb = arena[:, MID:MID + 8 * TOK].rearrange("p (s t) -> p s t", t=CTX)
                V.did(dve.tensor_tensor(nb[:, :, 1:CTX - 1], src[:, :, 0:CTX - 2], src[:, :, 2:CTX], ALU.add))
                V.did(dve.tensor_copy(nb[:, :, 0:1], src[:, :, 1:2]))
                V.did(dve.tensor_copy(nb[:, :, CTX - 1:CTX], src[:, :, CTX - 2:CTX - 1]))
                V.settle()
                V.did(dve.scalar_tensor_tensor(out=nb, in0=nb, scalar=0.5, in1=src, op0=ALU.mult, op1=ALU.subtract))
                V.settle()
                for i in range(6):
                    z = zT[:, Z_R + i, :]
                    dve.scalar_tensor_tensor(out=z, in0=mid[:, i, :], scalar=vec[:, V_MUP + i:V_MUP + i + 1], in1=z,
                                             op0=ALU.mult, op1=ALU.add)
                dve.tensor_tensor(lor, lor, mid[:, 6:8, :], ALU.add).then_inc(S("shifted"), 1)
                for tt in range(TILES):
                    dve.wait_ge(S("rkv_tr"), 2 * TILES * l + 2 * tt + 2)
                    dve.tensor_copy(rkv[:, tt, 512:768], bank[2 * (tt % 2) + 1][:, 0:256]).then_inc(S("rkv_d"), 1)
                dve.wait_ge(S("rkv_a"), TILES * (l + 1))
                hs = kk.rearrange("p t (h c) -> p (t h) c", h=4)
                V.did(dve.tensor_tensor(kk, rkv[:, :, 256:512], bc(rows[:, B_KK:B_KK + 256].unsqueeze(1), P, TILES, 256), ALU.mult))
                V.settle()
                scr = arena[:, MID:MID + 1024].rearrange("p (t c) -> p t c", t=TILES)
                V.did(dve.tensor_tensor(scr, kk, kk, ALU.mult))
                V.settle()
                V.did(dve.tensor_reduce(rt[:, 0:16], scr.rearrange("p t (h c) -> p (t h) c", h=4), AX.X, ALU.add))
                V.settle()
                dve.tensor_scalar(rt[:, 0:16], rt[:, 0:16], 1e-12, None, ALU.max).then_inc(S("kk_ss"), 1)
                dve.wait_ge(S("kk_rs"), l + 1)
                dve.tensor_tensor(hs, hs, bc(rt[:, 0:16].unsqueeze(2), P, 16, 64), ALU.mult).then_inc(S("kk_ready"), 1)
                for g, (chunks, _m, width, gains) in enumerate(NORMS):
                    cc = norm_cols(l, g)
                    dve.wait_ge(S("qk_rs"), len(NORMS) * l + g + 1)
                    for c, gcol in zip(chunks, gains):
                        ins = dve.scalar_tensor_tensor(out=zT[:, c, cc], in0=zT[:, c, cc], scalar=vec[:, gcol:gcol + 1],
                                                       in1=rsb[:, g % 2, cc], op0=ALU.mult, op1=ALU.mult)
                    ins.then_inc(S("qk_norm"), 1)
                dve.wait_ge(S("qk_norm"), len(NORMS) * (l + 1))
                for i, (x, cc, kind) in enumerate(rotations(l)):
                    if i == 6:
                        for h in range(4):
                            dve.wait_ge(S("uk_mm"), 4 * l + h + 1)
                            dve.tensor_tensor(mid[:, 4 + h, :], bank[4 + h % 2], zT[:, Z_KR, :], ALU.add).then_inc(S("uk_ev"), 1)
                    dve.wait_ge(S("rot_mm"), 10 * l + i + 1)
                    V.did(dve.tensor_tensor(rtmp[:, cc], bank[2 + i % 2][:, 0:cc.stop - cc.start], rope(2 * kind + 1)[:, cc], ALU.mult))
                    V.did(dve.tensor_tensor(x[:, cc], x[:, cc], rope(2 * kind)[:, cc], ALU.mult))
                    V.settle()
                    dve.tensor_tensor(x[:, cc], x[:, cc], rtmp[:, cc], ALU.add).then_inc(S("rot"), 1)
                    dve.wait_ge(S("rot"), 10 * l + i + 1)
                base, U = sum(len(units(i)) for i in range(l)), units(l)
                for step in range(len(U) + 2):
                    u = step
                    if u < len(U):
                        tt, h = U[u]
                        s2, n = u % 2, unit_keys(tt)
                        dve.wait_ge(S("s_mm"), base + u + 1)
                        if u >= 2:
                            dve.wait_ge(S("exp"), base + u - 1)
                        nm = nmax[:, s2:s2 + 1]
                        if 8 <= h < 12 and n == TOK:
                            if u >= 2:
                                dve.wait_ge(S("pt_mm"), base + u - 1)
                            dve.wait_ge(S("bias_in"), 16 * 16 * (l + 1))
                            V.did(dve.scalar_tensor_tensor(out=prob[:, s2, CTX:TOK], in0=bank[s2][:, CTX:TOK], scalar=unit_scale(h),
                                                           in1=bias[:, tt - T_LAT, h - 8, :], op0=ALU.mult, op1=ALU.add))
                            V.did(dve.tensor_scalar(prob[:, s2, 0:CTX], bank[s2][:, 0:CTX], unit_scale(h), None, ALU.mult))
                            V.settle()
                            dve.tensor_reduce(nm, prob[:, s2, 0:n], AX.X, ALU.max, negate=True).then_inc(S("smax"), 1)
                        else:
                            V.did(dve.tensor_reduce(bmax[:, s2:s2 + 1], bank[s2][:, 0:n], AX.X, ALU.max))
                            V.settle()
                            dve.tensor_scalar(nm, bmax[:, s2:s2 + 1], -unit_scale(h), None, ALU.mult).then_inc(S("smax"), 1)
                    u = step - 1
                    if 0 <= u < len(U):
                        n = unit_keys(U[u][0])
                        dve.wait_ge(S("exp"), base + u + 1)
                        dve.reciprocal(rinv[:, u % 4:u % 4 + 1], rsum[:, u % 2:u % 2 + 1]).then_inc(S("rinv"), 1)
                        dve.wait_ge(S("pt_mm"), base + u + 1)
                        if u >= 2:
                            dve.wait_ge(S("pv_mm"), base + u - 1)
                        dve.tensor_copy(probT[:, u % 2, 0:n], bank[2 + u % 2][:, 0:n]).then_inc(S("pt_ev"), 1)
                    u = step - 2
                    if u >= 0:
                        h = U[u][1]
                        dve.wait_ge(S("pv_mm"), base + u + 1)
                        dve.wait_ge(S("rinv"), base + u + 1)
                        if u % 16 == 0 and u >= 32:
                            dve.wait_ge(S("turn_mm"), u // 16 - 1)
                        dve.tensor_scalar(ytm[:, (u // 16) % 2, 64 * h:64 * h + 64], bank[(4, 7)[u % 2]][:, 0:HEAD],
                                          rinv[:, u % 4:u % 4 + 1], None, ALU.mult).then_inc(S("o_ev"), 1)
                pv_all = base + len(U)
                V.did(dve.memset(yr, 0.0))
                dve.memset(state[:, 0], 0.0).then_inc(S("st"), 1)
                dve.wait_ge(S("turn_ev"), 4 if l == 0 else 6)
                for j in range(ROUNDS):
                    rr = l * ROUNDS + j
                    tau = [RW_ORDER[d][j] for d in range(2)]
                    out = RW_ORDER[0][j] in qtiles(l)
                    for b, (dst, row) in enumerate(((sw, B_W0), (aa, B_A0))):
                        dve.wait_ge(S("w_mm"), 3 * rr + b + 1)
                        for d in range(2):
                            ins = dve.tensor_tensor(dst[:, d], bank[2 * b + d][:, 0:256], rows[:, row + 256 * d:row + 256 * d + 256], ALU.add)
                        ins.then_inc(S("w_pre"), 1)
                    dve.wait_ge(S("w_sig"), 2 * rr + 2)
                    ka = rows[:, B_KA:B_KA + 256]
                    V.did(dve.scalar_tensor_tensor(out=kd, in0=aa, scalar=-1.0, in1=bc(ka.unsqueeze(1), P, 2, 256), op0=ALU.add, op1=ALU.mult))
                    for d in range(2):
                        V.did(dve.tensor_tensor(bb[:, d], kk[:, tau[d]], aa[:, d], ALU.mult))
                    V.settle()
                    for d in range(2):
                        V.did(dve.scalar_tensor_tensor(out=kd[:, d], in0=kd[:, d], scalar=1.0, in1=rkv[:, tau[d], 256:512], op0=ALU.add, op1=ALU.mult))
                    V.settle()
                    dve.wait_ge(S("decays"), 6 * (rr + 1))
                    for d in range(2):
                        dve.tensor_tensor(eX[:, d], eX[:, d], kk[:, tau[d]], ALU.mult)
                        dve.tensor_tensor(eL[:, d], eL[:, d], rkv[:, tau[d], 0:256], ALU.mult)
                        dve.tensor_tensor(Bd[:, d], bb[:, d], eN[:, d], ALU.mult)
                        dve.tensor_tensor(eN[:, d], eN[:, d], kd[:, d], ALU.mult).then_inc(S("prod"), 1)
                    dve.tensor_tensor(Be, bb, eA, ALU.mult)
                    dve.tensor_tensor(eA, eA, kd, ALU.mult).then_inc(S("prod_end"), 1)
                    for i in range(1, RQ, 2):
                        dve.wait_ge(S("fm_tr"), RQ * rr + i + 1)
                        dve.tensor_copy(fmt[:, i], bank[i].rearrange("p (a t) -> p a t", a=4)).then_inc(S("fm_d"), 1)
                    for u in range(8):
                        d = u // 4
                        dve.wait_ge(S("a_mm"), 8 * rr + u + 1)
                        m2 = cst[:, C_TRI + 256 * d:C_TRI + 256 * d + 256]
                        dve.tensor_tensor(am[:, u].rearrange("p (x a) t -> p x (a t)", x=2), bank[4 + u % 4].rearrange("p (x t) -> p x t", x=2),
                                          bc(m2.unsqueeze(1), P, 2, 256), ALU.mult).then_inc(S("am_done"), 1)
                        if u % 4 == 3:
                            dve.wait_ge(S("am_done"), 8 * rr + u + 1)
                            half = slice(4 * d, 4 * d + 4)
                            V.did(dve.scalar_tensor_tensor(out=TT[:, half], in0=am[:, half, 0, :], scalar=-1.0,
                                                           in1=bc(level(0).unsqueeze(1), P, 4, P), op0=ALU.mult, op1=ALU.mult))
                            V.settle()
                            dve.tensor_tensor(TT[:, half], TT[:, half], bc(ident.unsqueeze(1), P, 4, P), ALU.add).then_inc(S("tt0"), 1)
                    dve.wait_ge(S("t_ev"), 2 * (rr + 1))
                    for lev in range(1, LEVELS):
                        for d in range(2):
                            half = slice(4 * d, 4 * d + 4)
                            dve.wait_ge(S("yt_mm"), 10 * rr + 2 * (lev - 1) + d + 1)
                            if lev > 1:
                                dve.wait_ge(S("inv"), 10 * rr + 2 * (lev - 2) + d + 1)
                            else:
                                dve.wait_ge(S("tt0"), 2 * rr + d + 1)
                            if lev < LEVELS - 1:
                                dve.tensor_tensor(Tm[:, half], Tm[:, half], bank[4 + d].rearrange("p (u t) -> p u t", u=4), ALU.subtract)
                            dve.tensor_tensor(TT[:, half], TT[:, half], bank[6 + d].rearrange("p (u t) -> p u t", u=4),
                                              ALU.subtract).then_inc(S("inv"), 1)
                    dve.wait_ge(S("m1_mm"), rr + 1)
                    dve.tensor_tensor(m1, bank[4].rearrange("p (q t) -> p q t", q=4), fmt[:, :, 1, :], ALU.add).then_inc(S("m1"), 1)
                    dve.wait_ge(S("g0_ev"), 2 * (rr + 1))
                    for s in range(2):
                        dve.wait_ge(S("st"), 2 * rr + s + l + 1)
                        new = state[:, (2 * j + s + 1) % 3]
                        for qq in range(RQ):
                            c = CHUNK_ORDER[qq // 2][s]
                            V.did(dve.scalar_tensor_tensor(out=new[:, qq], in0=state[:, (2 * j + s) % 3, qq],
                                                           scalar=ecol[:, 4 * c + qq:4 * c + qq + 1],
                                                           in1=h0[:, c, qq], op0=ALU.mult, op1=ALU.add))
                        V.settle()
                        dve.wait_ge(S("st_mm"), 2 * rr + s + 1)
                        dve.tensor_tensor(new, new, bank[6][:, 256 * s:256 * s + 256].rearrange("p (q v) -> p q v", q=4),
                                          ALU.add).then_inc(S("st"), 1)
                    if out:
                        no = out_rounds_before(l, j)
                        o3 = oo.rearrange("p (u c) -> p u c", u=8)
                        o2 = oo.rearrange("p (d c) -> p d c", d=2)
                        t13 = t1.rearrange("p d (h c) -> p (d h) c", h=4)
                        t23 = t2.rearrange("p d (h c) -> p (d h) c", h=4)
                        dve.wait_ge(S("o_mm"), no + 1)
                        dve.wait_ge(S("m1"), rr + 1)
                        o4 = oo.rearrange("p (q x c) -> p q x c", q=4, x=2)
                        for x, b in enumerate((7, 3)):
                            dve.tensor_copy(o4[:, :, x, :], bank[b][:, 0:256].rearrange("p (q c) -> p q c", q=4)).then_inc(S("o_read"), 1)
                        dve.wait_ge(S("o_read"), 2 * (no + 1))
                        V.did(dve.tensor_reduce(rt[:, 24:32], o3, AX.X, ALU.add))
                        V.settle()
                        V.did(dve.tensor_scalar(rt[:, 24:32], rt[:, 24:32], 1.0 / HEAD, None, ALU.mult))
                        V.settle()
                        V.did(dve.tensor_tensor(o3, o3, bc(rt[:, 24:32].unsqueeze(2), P, 8, 64), ALU.subtract))
                        V.settle()
                        V.did(dve.tensor_tensor(t13, o3, o3, ALU.mult))
                        V.settle()
                        dve.tensor_reduce(rt[:, 16:24], t13, AX.X, ALU.add).then_inc(S("o_var"), 1)
                        dve.wait_ge(S("o_rs"), no + 1)
                        V.did(dve.tensor_tensor(o3, o3, bc(rt[:, 16:24].unsqueeze(2), P, 8, 64), ALU.mult))
                        for d in range(2):
                            V.did(dve.tensor_tensor(t1[:, d], rkv[:, tau[d], 0:256], kd[:, d], ALU.mult))
                        V.settle()
                        V.did(dve.tensor_tensor(t1, t1, bc(rows[:, B_RK:B_RK + 256].unsqueeze(1), P, 2, 256), ALU.mult))
                        V.did(dve.tensor_tensor(o2, o2, bc(rows[:, B_LNW:B_LNW + 256].unsqueeze(1), P, 2, 256), ALU.mult))
                        V.settle()
                        V.did(dve.tensor_reduce(rt[:, 24:32], t13, AX.X, ALU.add))
                        V.did(dve.tensor_tensor(o2, o2, bc(rows[:, B_LNB:B_LNB + 256].unsqueeze(1), P, 2, 256), ALU.add))
                        V.settle()
                        for d in range(2):
                            V.did(dve.tensor_tensor(t2[:, d].rearrange("p (h c) -> p h c", h=4), rkv[:, tau[d], 512:768].rearrange("p (h c) -> p h c", h=4),
                                                    bc(rt[:, 24 + 4 * d:28 + 4 * d].unsqueeze(2), P, 4, 64), ALU.mult))
                        V.settle()
                        V.did(dve.tensor_tensor(o2, o2, t2, ALU.add))
                        V.settle()
                        V.did(dve.tensor_tensor(o2, o2, gg, ALU.mult))
                        V.settle()
                        for d in range(2):
                            ins = dve.tensor_tensor(yr[:, tau[d]], yr[:, tau[d]], o2[:, d], ALU.add)
                        ins.then_inc(S("yr"), 1)
                        dve.wait_ge(S("yr"), no + 1)
                for i in range(4 * KD):
                    m, br = divmod(i, 4)
                    gi = 4 * KD * l + i
                    dve.wait_ge(S("gate"), gi + 1)
                    dve.wait_ge(S("br_mm"), gi + 1)
                    dst = merged[:, m, q] if br == 0 else prod[:, i % 2, 0:w]
                    if br == 1 and KD * l + m:
                        dve.wait_ge(S("merged"), KD * l + m)
                    dve.tensor_tensor(dst, gate_sb[:, i % 2, 0:w], bank[2 + i % 2][:, 0:w], ALU.mult).then_inc(S("gated"), 1)
                    if br:
                        dve.wait_ge(S("gated"), gi + 1)
                        ins = dve.tensor_tensor(merged[:, m, q], merged[:, m, q], dst, ALU.add)
                        if br == 3:
                            ins.then_inc(S("merged"), 1)
                        else:
                            V.did(ins)
                            V.settle()
                residual(dve, V, l, 0)
                dve.wait_ge(S("nb_rstd"), l + 1)
                modulated(2, 3, segs(l)).then_inc(S("hb"), 1)
                if l % 2 == 0:
                    for j in range(FFC):
                        dve.wait_ge(S("silu"), j + 1)
                        dve.wait_ge(S("fu_mm"), j + 1)
                        dve.tensor_tensor(hid[:, j, q], gate_sb[:, j % 2, 0:w], bank[2 + j % 2][:, 0:w], ALU.mult).then_inc(S("hid"), 1)
                else:
                    dve.wait_ge(S("r_mm"), 1)
                    dve.wait_ge(S("wr_in"), 16)
                    lg = rt[:, 32:48].rearrange("p (i e) -> p i e", i=2)
                    V.did(dve.tensor_tensor(lg, bank[0][:, 0:16].rearrange("p (i e) -> p i e", i=2),
                                            bc(wrt[:, 64:72].unsqueeze(1), P, 2, EXPERTS), ALU.add))
                    V.settle()
                    dve.tensor_reduce(rt[:, 48:50], lg, AX.X, ALU.max, negate=True).then_inc(S("r_max"), 1)
                    dve.wait_ge(S("r_exp"), 2)
                    V.did(dve.tensor_reduce(rt[:, 50:52], lg, AX.X, ALU.add))
                    V.settle()
                    V.did(dve.reciprocal(rt[:, 50:52], rt[:, 50:52]))
                    V.settle()
                    V.did(dve.tensor_tensor(lg, lg, bc(rt[:, 50:52].unsqueeze(2), P, 2, EXPERTS), ALU.mult))
                    V.settle()
                    for i in range(2):
                        pi = lg[:, i, :].unsqueeze(2).broadcast_to([P, 8, 8])
                        pj = lg[:, i, :].unsqueeze(1).broadcast_to([P, 8, 8])
                        gt = prod[:, 0, 64 * i:64 * i + 64].rearrange("p (i j) -> p i j", i=8)
                        eq = prod[:, 1, 64 * i:64 * i + 64].rearrange("p (i j) -> p i j", i=8)
                        V.did(dve.tensor_tensor(gt, pj, pi, ALU.is_gt))
                        V.did(dve.tensor_tensor(eq, pj, pi, ALU.is_equal))
                        V.settle()
                        V.did(dve.tensor_tensor(eq, eq, cst[:, C_LOW:C_LOW + 64].rearrange("p (i j) -> p i j", i=8), ALU.mult))
                        V.settle()
                        V.did(dve.tensor_tensor(gt, gt, eq, ALU.add))
                        V.settle()
                        V.did(dve.tensor_reduce(rt[:, 64 + 8 * i:72 + 8 * i], gt, AX.X, ALU.add))
                    V.settle()
                    cm = rt[:, 64:80]
                    V.did(dve.tensor_scalar(cm, cm, 1.5, None, ALU.is_lt))
                    V.settle()
                    V.did(dve.tensor_tensor(cm, cm, rt[:, 32:48], ALU.mult))
                    V.settle()
                    V.did(dve.tensor_reduce(rt[:, 50:52], cm.rearrange("p (i e) -> p i e", i=2), AX.X, ALU.add))
                    V.settle()
                    V.did(dve.reciprocal(rt[:, 50:52], rt[:, 50:52]))
                    V.settle()
                    dve.tensor_tensor(cm.rearrange("p (i e) -> p i e", i=2), cm.rearrange("p (i e) -> p i e", i=2),
                                      bc(rt[:, 50:52].unsqueeze(2), P, 2, EXPERTS), ALU.mult).then_inc(S("comb"), 1)
                    dve.wait_ge(S("cw_ev"), 4)
                    dve.wait_ge(S("comb"), 1)
                    for e in range(EXPERTS):
                        for j in range(EFC):
                            i = e * EFC + j
                            dve.wait_ge(S("esilu"), i + 1)
                            dve.wait_ge(S("eu_mm"), i + 1)
                            if j == 0 and e >= 2:
                                dve.wait_ge(S("edown"), e - 1)
                            V.did(dve.tensor_tensor(prod[:, i % 2, 0:w], gate_sb[:, i % 2, 0:w], bank[2 + i % 2][:, 0:w], ALU.mult))
                            V.settle()
                            dve.tensor_tensor(ehid[:, e % 2, j, :], prod[:, i % 2, 0:w], cw[:, e, :], ALU.mult).then_inc(S("ehid"), 1)
                residual(dve, V, l, 1)


def constants():
    c = np.zeros((P, C_COLS), np.float32)
    i = np.arange(P)
    c[:, C_ID:C_ID + P] = np.eye(P)
    c[:, C_ONES:C_ONES + P] = 1
    c[:, C_BLK:C_BLK + P] = i[:, None] // HEAD == i[None, :] // HEAD
    for first, half in ((0, 32), (HEAD, 32)):
        for m in range(half):
            c[first + m + half, C_ROT + first + m] = -1
            c[first + m, C_ROT + first + m + half] = 1
    for m in range(16):
        c[HEAD + m + 16, C_ROTM + HEAD + m] = -1
        c[HEAD + m, C_ROTM + HEAD + m + 16] = 1
    same = i[:, None] // CHUNK == i[None, :] // CHUNK
    s, t = i[:, None], i[None, :]
    for n, m in enumerate((s < t, s <= t, s > t, s >= t)):
        c[:, C_TRI + n * P:C_TRI + (n + 1) * P] = m & same
    for lev in range(LEVELS):
        b = 1 << lev
        c[:, C_LEV + lev * P:C_LEV + (lev + 1) * P] = (s // (2 * b) == t // (2 * b)) & (s // b != t // b)
    pos = np.arange(SEQ)
    for kind, rot in enumerate((HEAD, 32)):
        pairs = rot // 4
        inv = (np.float32(10000.0) ** (-np.arange(pairs, dtype=np.float32) / np.float32(pairs))).astype(np.float32)
        ang = np.concatenate([(pos // GRID_W).astype(np.float32)[:, None] * inv, (pos % GRID_W).astype(np.float32)[:, None] * inv], 1)
        cos, sin = np.ones((P, TOK), np.float32), np.zeros((P, TOK), np.float32)
        for first in ((0, HEAD) if kind == 0 else (HEAD,)):
            for r in range(rot):
                cos[first + r, CTX:] = np.cos(ang[:, r % (rot // 2)])
                sin[first + r, CTX:] = np.sin(ang[:, r % (rot // 2)])
        c[:, C_ROPE + 2 * kind * TOK:C_ROPE + (2 * kind + 1) * TOK] = cos
        c[:, C_ROPE + (2 * kind + 1) * TOK:C_ROPE + (2 * kind + 2) * TOK] = sin
    c[:, C_EPS] = NORM_EPS
    c[:, C_EPS + 1] = GN_EPS
    e = np.arange(EXPERTS)
    c[:, C_LOW:C_LOW + 64] = (e[None, :] < e[:, None]).astype(np.float32).reshape(1, 64)
    sel = np.zeros((32, GRID_W * GRID_W), np.float32)
    for qc in range(GRID_W):
        start = min(max(qc - 8, 0), GRID_W - 16)
        for kc in range(GRID_W):
            if start <= kc < start + 16:
                sel[kc - qc + 15, qc * GRID_W + kc] = 1
            else:
                sel[31, qc * GRID_W + kc] = NEG
    return c, sel


def cut_blocks(w):
    r, c = w.shape
    return w.reshape(r // P, P, c // P, P).transpose(0, 2, 1, 3)


def by_output(w):
    b = cut_blocks(w)
    return b.transpose(1, 0, 2, 3).reshape(-1, P, P)


def columns(v):
    return np.ascontiguousarray(np.asarray(v).reshape(-1, P).T)


def padded(w, c):
    out = np.zeros((w.shape[0], c), w.dtype)
    out[:, :w.shape[1]] = w
    return out


def lay_out(i):
    i = {k: np.asarray(v) for k, v in i.items()}
    blocks, vecs, muxs, rows, lora2s, lws, rpbs = [], [], [], [], [], [], []
    for l in range(DEPTH):
        blocks.append(by_output(i["w_mod"][l]))
        w = i["w_in"][l]
        o = np.cumsum([0, 512, 128, 128, 256, 256, 256, 256, 256, 256, 384, 256, 32, 4096])
        part = [w[:, o[n]:o[n + 1]] for n in range(13)]
        heads = part[0].reshape(D, 8, HEAD)[:, [0, 4, 1, 5, 2, 6, 3, 7]].reshape(D, 512)
        kr = np.zeros((D, P), np.float32)
        kr[:, HEAD:HEAD + 32] = part[11]
        blocks.append(by_output(np.concatenate([heads, part[1], part[3], part[4], part[6], part[7], part[8], part[9], part[10], kr], 1)))
        blocks.append(by_output(np.concatenate([part[2], part[5]], 1)))
        uq = i["mla_w_uq"][l].reshape(384, 4, 96)
        blocks.append(by_output(np.concatenate([padded(uq[:, h], P) for h in range(4)], 1)))
        ukv = i["mla_w_ukv"][l].reshape(256, 4, 128)
        blocks.append(by_output(np.concatenate([padded(ukv[:, h, :64], P) for h in range(4)], 1)))
        blocks.append(by_output(np.ascontiguousarray(ukv[:, :, 64:]).reshape(256, 256)))
        gates, br = cut_blocks(part[12]), cut_blocks(i["w_branch"][l])
        for m in range(KD):
            for b in range(4):
                blocks.append(gates[:, b * KD + m])
                blocks.append(br[BRANCH_FIRST[b]:BRANCH_FIRST[b] + BRANCH_CHUNKS[b], m])
        blocks.append(by_output(i["w_out"][l]))
        if l % 2 == 0:
            g, u, d = (i[n][l // 2] for n in ("ffn_w_gate", "ffn_w_up", "ffn_w_down"))
            g, u = cut_blocks(g), cut_blocks(u)
            for j in range(FFC):
                blocks += [g[:, j], u[:, j]]
            blocks.append(by_output(d))
        else:
            for e in range(EXPERTS):
                g, u, d = (i[n][l // 2][e] for n in ("moe_w_gate", "moe_w_up", "moe_w_down"))
                g, u = cut_blocks(g), cut_blocks(u)
                for j in range(EFC):
                    blocks += [g[:, j], u[:, j]]
                blocks.append(by_output(d))
        two = lambda v: np.concatenate([v, v])
        vecs.append(np.concatenate([columns(i[n][l]) for n in ("b_mod", "norm_mix_pre", "norm_mix_post", "norm_ffn_pre", "norm_ffn_post")]
                                   + [columns(i["rwkv_mu_p"][l].reshape(-1)), columns(two(i["gqa_q_norm"][l])), columns(two(i["gqa_k_norm"][l])),
                                      columns(i["mla_q_norm"][l]), columns(i["mla_kv_norm"][l])], 1))
        muxs.append(columns(i["rwkv_mu_x"][l].reshape(-1)))
        rows.append(np.concatenate([i[n][l].reshape(-1) for n in ("rwkv_w0", "rwkv_a0", "rwkv_k_k", "rwkv_k_a", "rwkv_r_k", "rwkv_ln_w", "rwkv_ln_b")]))
        lora2s.append(np.concatenate([np.concatenate([i["rwkv_w2"][l].reshape(64, 256), i["rwkv_a2"][l].reshape(64, 256)]),
                                      i["rwkv_g2"][l].reshape(128, 256)], 1))
        one = np.concatenate([i["rwkv_w1"][l][0], i["rwkv_w1"][l][1], i["rwkv_a1"][l][0], i["rwkv_a1"][l][1]], 1)
        two_ = np.concatenate([i["rwkv_g1"][l][0], i["rwkv_g1"][l][1]], 1)
        lws.append(np.stack([x.reshape(KD, P, P).transpose(1, 0, 2) for x in (one, two_)], 1))
        r = i["na_rpb"][l][:, 8 - GRID_H:7 + GRID_H]
        rpbs.append(r.reshape(-1, NA_COLS).T)
    blocks = np.concatenate(blocks)
    slabs = np.ascontiguousarray(blocks.reshape(-1, SLAB, P, P).transpose(0, 2, 1, 3))
    rpb = np.concatenate([np.concatenate(rpbs, 1), np.ones((1, 56), np.float32)])
    cst, sel = constants()
    fm = np.concatenate([i["ctx"][0], i["x"][0]]).T.reshape(KD, P, TOK).transpose(1, 0, 2)
    c2 = np.stack([columns(i["c"][0]), columns(i["c_ctx"])], 2)
    wr = np.concatenate([i["moe_w_router"][0].reshape(KD, P, EXPERTS).transpose(1, 0, 2).reshape(P, KD * EXPERTS),
                         np.tile(i["moe_b_router"][0][None, :], (P, 1))], 1)
    return {"w": slabs, "vec": np.stack(vecs), "mux": np.stack(muxs), "rows": np.stack(rows), "lora2": np.stack(lora2s), "lw": np.stack(lws),
            "rpb": rpb, "sel": sel, "cst": cst, "x": fm, "c2": c2, "wr": wr}


def program(nc, arrays):
    t = {name: nc.dram_tensor(f"in_{name}", a.shape, mybir.dt.from_np(a.dtype), kind="ExternalInput").ap() for name, a in arrays.items()}
    t["scratch"] = nc.dram_tensor("rel_bias", [DEPTH * 4 * 7, GRID_W * GRID_W], F32, kind="Internal").ap()
    t["out"] = nc.dram_tensor("out_0", [P, KD, SEQ], F32, kind="ExternalOutput").ap()
    build(nc, t)


def kernel(**inputs):
    import concourse.bacc as bacc
    from concourse.bass_utils import run_bass_kernel_spmd as run

    nc = bacc.Bacc("TRN2", target_bir_lowering=False, num_devices=1)
    arrays = {name: np.ascontiguousarray(a) for name, a in lay_out(inputs).items()}
    program(nc, arrays)
    r = run(nc, [{f"in_{name}": a for name, a in arrays.items()}], core_ids=[0])
    got = r.results[0]["out_0"]
    return np.ascontiguousarray(got.transpose(2, 1, 0).reshape(1, SEQ, D))
```

```python
import math
from contextlib import ExitStack

import numpy as np
import concourse.bass as bass
from concourse import mybir

F32 = mybir.dt.float32
F16 = mybir.dt.float16
ALU = mybir.AluOpType
ACT = mybir.ActivationFunctionType
AX = mybir.AxisListType

P = 128
D = 1024
SEQ = 256
CTX = 256
TOK = CTX + SEQ
DEPTH = 2
GRID_W = 64
GRID_H = SEQ // GRID_W
KD = D // P
TILES = TOK // P
HEAD = 64
NORM_EPS = 1e-6
GN_EPS = 64e-5
FF = 2816
FFC = FF // P
EXPERTS = 8
EFF = 1408
EFC = EFF // P
CHUNK = 64
LEVELS = 6
DECAY = math.exp(-0.5)
NA_ROWS = 2 * 8 - 1
NA_COLS = 2 * 16 - 1
NEG = -1e30

BRANCH_CHUNKS = (4, 2, 2, 2)
BRANCH_FIRST = (0, 4, 6, 8)

Z_Q, Z_K, Z_NQ, Z_NK, Z_R, Z_RK, Z_RV, Z_LMU, Z_CQ, Z_CKV, Z_KR = 0, 4, 5, 7, 9, 11, 13, 15, 17, 20, 22
Z_CHUNKS = 23
Z_STREAM = ([(Z_Q + i, True) for i in range(4)] + [(Z_K, False)]
            + [(Z_NQ + i, True) for i in range(2)] + [(Z_NK + i, False) for i in range(2)]
            + [(Z_R + i, False) for i in range(6)]
            + [(Z_CQ + i, True) for i in range(3)] + [(Z_CKV + i, False) for i in range(2)] + [(Z_KR, False)])

SLAB = 8
RING = 4
PARTS = 3
WSCALE = 64.0
UNSCALE = 1.0 / WSCALE
MOD_SLABS = 6 * KD
Z_SLABS = len(Z_STREAM)
Z_EVEN, Z_ODD = (Z_SLABS + 5) // 2, (Z_SLABS + 4) // 2
V_SLABS = 3
MLA_SLABS = 3
MERGE_SLABS = (4 * KD * KD + 10 * KD) // SLAB
OUT_SLABS = KD
FFN_SLABS = 2 * FFC + FFC * KD // SLAB
MOE_SLABS = EXPERTS * (2 * EFC + EFC * KD // SLAB)
LAYER_Z = []
SLABS = 0
for _l in range(DEPTH):
    LAYER_Z.append(SLABS + MOD_SLABS + Z_SLABS + V_SLABS + MLA_SLABS)
    SLABS = LAYER_Z[-1] + MERGE_SLABS + OUT_SLABS + (FFN_SLABS, MOE_SLABS)[_l]

V_BMOD, V_NMPRE, V_NMPOST, V_NFPRE, V_NFPOST = 0, 48, 56, 64, 72
V_MUP, V_QG, V_KG, V_MQ, V_MKV = 80, 86, 87, 88, 91
V_COLS = 93
B_W0, B_A0, B_KK, B_KA, B_RK, B_LNW, B_LNB = 0, 512, 1024, 1280, 1536, 1792, 2048
B_COLS = 2304
C_ID, C_ONES, C_BLK, C_ROT, C_ROTM, C_TRI, C_LEV, C_ROPE, C_EPS, C_LOW, C_FOLD = 0, 128, 256, 384, 512, 640, 1152, 1920, 2944, 2946, 3010
C_COLS = 3012

RW_ORDER = ((0, 1, 2, 3), (1, 0, 3, 2))
CHUNK_ORDER = ((0, 1), (1, 0))


class Steps:

    def __init__(self, eng, sem):
        self.eng, self.sem, self.n = eng, sem, 0

    def did(self, ins):
        ins.then_inc(self.sem, 1)
        self.n += 1
        return ins

    def settle(self):
        if self.n:
            self.eng.wait_ge(self.sem, self.n)


def build(nc, t):
    ctx = ExitStack()
    with ctx:
        def sb(name, cols, dt=F32):
            return ctx.enter_context(nc.sbuf_tensor(name, [P, cols], dt))

        sems = {}

        def S(name):
            if name not in sems:
                sems[name] = ctx.enter_context(nc.semaphore(name))
            return sems[name]

        xT = sb("xT", KD * TOK)[:, :].rearrange("p (k t) -> p k t", k=KD)
        h16 = sb("h16", 2 * KD * TOK, F16)[:, :].rearrange("p (x k t) -> p x k t", x=2, k=KD)
        ring = sb("ring", RING * SLAB * P)[:, :].rearrange("p (r b c) -> p r b c", r=RING, b=SLAB)
        parts = sb("parts", 2 * PARTS * SLAB * P, F16)[:, :].rearrange("p (r x b c) -> p r x b c", r=PARTS, x=2, b=SLAB)
        yflat = sb("yT", 10 * TOK)[:, :]
        y16 = yflat.bitcast(F16).rearrange("p (x k t) -> p x k t", x=2, k=10)
        arena = sb("arena", Z_CHUNKS * TOK + KD * TOK + TILES * 640)[:, :]
        rkv = sb("rkv", TILES * 768)[:, :].rearrange("p (t c) -> p t c", t=TILES)
        kk = sb("kk", TILES * 256)[:, :].rearrange("p (t c) -> p t c", t=TILES)
        state = sb("state", 3 * 256)[:, :].rearrange("p (s j v) -> p s j v", s=3, j=4)
        lor = sb("lor", 2 * TOK)[:, :].rearrange("p (k t) -> p k t", k=2)
        yr = sb("yr", TILES * 256)[:, :].rearrange("p (t c) -> p t c", t=TILES)
        rows = sb("rows", B_COLS)[:, :]
        lora2 = sb("lora2", 512)[:, :]
        cst = sb("cst", C_COLS)[:, :]
        vecs = sb("vec", DEPTH * V_COLS)[:, :].rearrange("p (l c) -> p l c", l=DEPTH)
        mux = sb("mux", 3 * KD)[:, :]
        wrt = sb("wrt", KD * EXPERTS + EXPERTS)[:, :]
        rstd = sb("rstd", TOK)[:, :]
        scT = sb("scT", KD * 2)[:, :].rearrange("p (k j) -> p k j", j=2)
        sc16 = sb("sc16", KD * 8, F16)[:, :].rearrange("p (k x j) -> p k x j", x=4, j=2)
        mods = sb("mod", DEPTH * 96)[:, :].rearrange("p (l n j) -> p l n j", l=DEPTH, j=2)
        gmods = sb("gmod", DEPTH * 64)[:, :].rearrange("p (l w k j) -> p l w k j", l=DEPTH, w=4, j=2)
        wr16 = sb("wr16", 2 * KD * EXPERTS, F16)[:, :].rearrange("p (x c) -> p x c", x=2)
        small = sb("small", 108)[:, :]
        bank = [ctx.enter_context(nc.psum_tensor(f"bank{i}", [P, 512], F32))[:, :] for i in range(8)]

        ident = cst[:, C_ID:C_ID + P]
        ones = cst[:, C_ONES:C_ONES + P]
        blk = cst[:, C_BLK:C_BLK + P]
        eps_col = cst[:, C_EPS:C_EPS + 1]
        gn_eps_col = cst[:, C_EPS + 1:C_EPS + 2]

        def tri(i):
            return cst[:, C_TRI + i * P:C_TRI + (i + 1) * P]

        def level(i):
            return cst[:, C_LEV + i * P:C_LEV + (i + 1) * P]

        def rope(i):
            return cst[:, C_ROPE + i * SEQ:C_ROPE + (i + 1) * SEQ]

        zT = arena[:, 0:Z_CHUNKS * TOK].rearrange("p (k t) -> p k t", k=Z_CHUNKS)
        MID = Z_CHUNKS * TOK
        mid = arena[:, MID:MID + KD * TOK].rearrange("p (k t) -> p k t", k=KD)
        VT = MID + KD * TOK
        vT = arena[:, VT:VT + TILES * 640].rearrange("p (t c) -> p t c", t=TILES)
        lw = arena[:, MID:MID + 2048].rearrange("p (g k c) -> p g k c", g=2, k=KD)
        lwm = arena[:, MID + 2048:MID + 4096].rearrange("p (g k c) -> p g k c", g=2, k=KD)
        l16 = yflat[:, 0:4096].bitcast(F16).rearrange("p (x s g k c) -> p x s g k c", x=2, s=2, g=2, k=KD)
        wide = arena[:, 0:KD * TOK].rearrange("p (k t) -> p k t", k=KD)
        relrow = arena[:, 4608:4608 + 4096]
        modrow = arena[:, (Z_CHUNKS - 4) * TOK:Z_CHUNKS * TOK].rearrange("p (s c) -> p s c", s=2)
        z16 = [arena[:, c * TOK:(c + 1) * TOK].bitcast(F16).rearrange("p (x t) -> p x t", x=2) for c in range(Z_CHUNKS)]
        sq = yflat[:, 0:6 * TOK].rearrange("p (g k t) -> p g k t", g=2, k=3)
        rsb = yflat[:, 6 * TOK:8 * TOK].rearrange("p (g t) -> p g t", g=2)
        rtmp = yflat[:, 8 * TOK:10 * TOK].rearrange("p (s t) -> p s t", s=2)
        bias = arena[:, Z_R * TOK:Z_R * TOK + 2048].rearrange("p (j h c) -> p j h c", j=2, h=4)
        diag = arena[:, Z_RV * TOK:Z_RV * TOK + 3 * P].rearrange("p (s c) -> p s c", s=3)
        probT = arena[:, Z_LMU * TOK:Z_LMU * TOK + 2 * TOK].rearrange("p (s c) -> p s c", s=2)
        prob = arena[:, Z_CQ * TOK:Z_CQ * TOK + 3 * TOK].rearrange("p (s c) -> p s c", s=3)
        nmax, bmax, rsum, rinv = (small[:, 3 * i:3 * i + 3] for i in range(4))
        rt_ = small[:, 12:]
        at = [0]

        def cut(n):
            at[0] += n
            return arena[:, at[0] - n:at[0]]

        sw, aa, gg, kd, bb, eL, eN, eX, eA, Bd, Be = (cut(512).rearrange("p (d c) -> p d c", d=2) for _ in range(11))
        fmt_flat = cut(2048)
        fmt = fmt_flat.rearrange("p (q a t) -> p q a t", q=4, a=4)
        am = cut(4096).rearrange("p (u a t) -> p u a t", u=8, a=4)
        ct = cut(2048).rearrange("p (s u t) -> p s u t", s=2, u=8)
        Tm = cut(1024).rearrange("p (u t) -> p u t", u=8)
        TT = cut(1024).rearrange("p (u t) -> p u t", u=8)
        Xs = cut(1024).rearrange("p (u t) -> p u t", u=8)
        m1 = cut(512).rearrange("p (q t) -> p q t", q=4)
        gh = cut(1024).rearrange("p (c x q v) -> p c x q v", c=2, x=2, q=4)
        g0, h0 = gh[:, :, 0], gh[:, :, 1]
        ecol = small[:, 100:108]
        assert at[0] <= VT + TILES * 640
        rhs2, nwu = ct[:, 1], Tm
        RATE_BANKS = (1, 5, 0, 7)
        oo = gg.rearrange("p d c -> p (d c)")
        bonus = rt_[:, 80:88]
        t1, t2 = eN, Bd
        merged = arena[:, 0:KD * TOK].rearrange("p (k t) -> p k t", k=KD)
        m16 = arena[:, 2 * KD * TOK:3 * KD * TOK].bitcast(F16).rearrange("p (x k t) -> p x k t", x=2, k=KD)
        yo = arena[:, KD * TOK:2 * KD * TOK].rearrange("p (k t) -> p k t", k=KD)
        gate_sb = vT.rearrange("p t c -> p (t c)")[:, 0:1024].rearrange("p (s t) -> p s t", s=2)
        prod = vT.rearrange("p t c -> p (t c)")[:, 1024:2048].rearrange("p (s t) -> p s t", s=2)
        hid = arena[:, 0:FFC * TOK].bitcast(F16).rearrange("p (x k t) -> p x k t", x=2, k=FFC)
        ehid = arena[:, 0:2 * EFC * SEQ].bitcast(F16).rearrange("p (s x k t) -> p s x k t", s=2, x=2, k=EFC)
        cw = arena[:, 2 * EFC * SEQ:2 * EFC * SEQ + EXPERTS * SEQ].rearrange("p (e t) -> p e t", e=EXPERTS)
        sqy = yflat[:, 0:KD * TOK].rearrange("p (k t) -> p k t", k=KD)
        rt = small[:, 12:]

        def qs(l):
            return slice(0, TOK) if l < DEPTH - 1 else slice(CTX, TOK)

        def segs(l):
            return [(slice(CTX, TOK), 0)] + ([(slice(0, CTX), 1)] if l < DEPTH - 1 else [])

        def qtiles(l):
            return range(TILES) if l < DEPTH - 1 else range(CTX // P, TILES)

        def units(l):
            return [(tt, h) for tt in qtiles(l) for h in range(16)]

        def unit_q(tt, h):
            c = slice(tt * P, (tt + 1) * P)
            if h < 8:
                return zT[64 * (h // 4):64 * (h // 4) + 64, Z_Q + h % 4, c]
            if h < 12:
                return zT[64 * (h % 2):64 * (h % 2) + 64, Z_NQ + (h - 8) // 2, c]
            return mid[:, h - 12, c]

        def unit_keys(tt):
            return CTX if tt < CTX // P else TOK

        def unit_k(tt, h):
            c = slice(0, unit_keys(tt))
            if h < 8:
                return zT[64 * (h // 4):64 * (h // 4) + 64, Z_K, c]
            if h < 12:
                return zT[64 * (h % 2):64 * (h % 2) + 64, Z_NK + (h - 8) // 2, c]
            return mid[:, 4 + h - 12, c]

        def unit_v(h, j):
            col = 64 * (h // 4) if h < 8 else 128 + 64 * (h - 8) if h < 12 else 384 + 64 * (h - 12)
            return vT[:, j, col:col + 64]

        def scores(u):
            return bank[(0, 1, 5)[u % 3]]

        def attended(u):
            return bank[(4, 7, 6)[u % 3]]

        def unit_scale(h):
            return HEAD ** -0.5 if h < 12 else 96 ** -0.5

        NORMS = [([Z_Q + i], blk, HEAD, [V_QG]) for i in range(4)] + [([Z_K], blk, HEAD, [V_KG]),
                 ([Z_CQ + i for i in range(3)], ones, 384, [V_MQ + i for i in range(3)]),
                 ([Z_CKV + i for i in range(2)], ones, 256, [V_MKV + i for i in range(2)])]

        def norm_cols(l, g):
            return qs(l) if g < 4 or g == 5 else slice(0, TOK)

        def rotations(l):
            gq = [(zT[:, Z_Q + i, CTX:TOK], 0) for i in range(4)] + [(zT[:, Z_K, CTX:TOK], 0)]
            return gq + [(zT[:, Z_KR, CTX:TOK], 1)] + [(mid[:, i, CTX:TOK], 1) for i in range(4)]

        T_LAT = CTX // P

        def out_rounds_before(l, j):
            return j if l == 0 else TILES + max(0, j - CTX // P)

        def has_out(l, j):
            return RW_ORDER[0][j] in qtiles(l)

        def unit_out(tt, h):
            chunk = h // 2 if h < 12 else 8 + (h - 12) // 2
            return slice(64 * (h % 2), 64 * (h % 2) + 64), chunk, slice(tt * P, (tt + 1) * P)

        def fresh_slab(seen, split, blocks):
            seen[0] += blocks
            first = split[0]
            split[0] = max(first, min((seen[0] - 1) // SLAB + PARTS, SLABS))
            return range(first, split[0])

        def post_out(l, which, m):
            w = qs(l).stop - qs(l).start
            if l % 2 and which:
                return bank[4 + m // 2][:, 256 * (m % 2):256 * (m % 2) + 256]
            return bank[4 + m % 4][:, 0:w]

        def post_bank_free(pe, l, which, m):
            if m >= 4:
                pe.wait_ge(S("po_sq"), KD * (2 * l + which) + m - 3)

        def post_norm(act, highs, l, which):
            q, pc = qs(l), 2 * l + which
            dst = (yo, mid)[which]
            for m in range(KD):
                if not (l % 2 and which):
                    highs((KD, FFC)[which])
                act.wait_ge(S("po_mm"), KD * pc + (m | 1 if l % 2 and which else m) + 1)
                act.activation(dst[:, m, q], post_out(l, which, m), ACT.Copy, scale=UNSCALE)
                act.activation(sqy[:, m, q], post_out(l, which, m), ACT.Square, scale=UNSCALE).then_inc(S("po_sq"), 1)
            act.wait_ge(S("po_ss"), pc + 1)
            act.activation(rstd[:, q], bank[0][:, 0:q.stop - q.start], ACT.Ln, bias=eps_col, scale=1.0 / D).then_inc(S("po_ln"), 1)
            act.wait_ge(S("po_ln"), pc + 1)
            act.activation(rstd[:, q], rstd[:, q], ACT.Exp, scale=-0.5).then_inc(S("po_rstd"), 1)

        def post_sum(pe, l, which):
            q, pc = qs(l), 2 * l + which
            for k in range(KD):
                pe.wait_ge(S("po_sq"), KD * pc + k + 1)
                ins = pe.matmul(bank[0][:, 0:q.stop - q.start], ones, sqy[:, k, q], start=k == 0, stop=k == KD - 1)
            ins.then_inc(S("po_ss"), 1)

        def residual(dve, V, lows, l, which):
            q, pc = qs(l), 2 * l + which
            y = (yo, mid)[which]
            lows(KD * (KD, (FFC, EFC)[l % 2])[which])
            dve.wait_ge(S("po_rstd"), pc + 1)
            for k in range(KD):
                V.did(dve.tensor_tensor(y[:, k, q], y[:, k, q], rstd[:, q], ALU.mult))
            V.settle()
            for k in range(KD):
                for cc, jc in segs(l):
                    ins = dve.scalar_tensor_tensor(out=xT[:, k, cc], in0=y[:, k, cc], scalar=gmods[:, l, 2 * which + 1, k, jc:jc + 1],
                                                   in1=xT[:, k, cc], op0=ALU.mult, op1=ALU.add)
            name = f"xa{l}" if which == 0 else f"xb{l}"
            ins.then_inc(S(name), 1)
            dve.wait_ge(S(name), 1)

        RQ = 2 * 2
        ROUNDS = TILES
        LAYER_VEC_LOADS = 4
        block = ctx.enter_context(nc.Block())

        @block.sync
        def _(sp):
            sp.dma_start(cst, t["cst"]).then_inc(S("cst_in"), 16)
            sp.dma_start(scT, t["c2"]).then_inc(S("c_in"), 16)
            sp.dma_start(xT, t["x"]).then_inc(S("x_in"), 16)
            for n in range(SLABS):
                if n in LAYER_Z:
                    l = LAYER_Z.index(n)
                    if l == 0:
                        sp.wait_ge(S("rel_out"), 16)
                    sp.wait_ge(S("rkv_a"), TILES * (l + 1))
                    sp.wait_ge(S("rkv_d"), TILES * (l + 1))
                    for r in range(GRID_H):
                        for h in range(4):
                            first = (l * 4 + h) * 7 + GRID_H - 1 - r
                            sp.dma_start(bias[64 * (r % 2):64 * (r % 2) + 64, r // 2, h, :].rearrange("p (r c) -> p r c", r=GRID_H),
                                         t["scratch"][first:first + GRID_H, :].rearrange("r (q c) -> q r c", q=GRID_W)
                                         ).then_inc(S("bias_in"), 16)
                if n >= RING:
                    sp.wait_ge(S("split_lo"), n - RING + 1)
                sp.dma_start(ring[:, n % RING], t["w"][n]).then_inc(S(f"slab_in{n % RING}"), 16)
            sp.wait_ge(S("xb1"), 1)
            sp.dma_start(t["out"], xT[:, :, CTX:TOK]).then_inc(S("out_done"), 16)
            sp.wait_ge(S("out_done"), 16)

        @block.gpsimd
        def _(pool):
            pool.dma_start(arena[0:32, 0:4096], t["sel"]).then_inc(S("rel_in"), 16)
            pool.dma_start(arena[0:32, 4096:4096 + 56], t["rpb"]).then_inc(S("rel_in"), 16)
            pool.dma_start(wrt, t["wr"]).then_inc(S("wr_in"), 16)
            pool.dma_start(vecs.rearrange("p l c -> p (l c)"), t["vec"]).then_inc(S("vecs_in"), 16)
            pool.wait_ge(S("rel_ev"), 8)
            pool.dma_start(t["scratch"], relrow[0:56, :]).then_inc(S("rel_out"), 16)
            pool.wait_ge(S("rel_out"), 16)
            for l in range(DEPTH):
                if l:
                    pool.wait_ge(S(f"xb{l - 1}"), 1)
                pool.dma_start(mux, t["mux"][l]).then_inc(S("vec_in"), 16)
                pool.dma_start(rows, t["rows"][l:l + 1, :].broadcast_to([P, B_COLS])).then_inc(S("vec_in"), 16)
                pool.dma_start(lora2, t["lora2"][l]).then_inc(S("vec_in"), 16)
                pool.dma_start(lw, t["lw"][l]).then_inc(S("vec_in"), 16)
                for j in range(ROUNDS):
                    rr = l * ROUNDS + j
                    for lev in range(1, LEVELS):
                        for d in range(2):
                            n = (lev - 1) % 2
                            if lev == 1:
                                pool.wait_ge(S("am_done"), 8 * rr + 4 * (d + 1))
                            if lev > 2:
                                pool.wait_ge(S("x_mm"), 10 * rr + 2 * (lev - 3) + d + 1)
                            pool.tensor_tensor(ct[:, n, 4 * d:4 * d + 4, :], am[:, 4 * d:4 * d + 4, 0, :],
                                               level(lev).unsqueeze(1).broadcast_to([P, 4, P]), ALU.mult
                                               ).then_inc(S("ct_done"), 1)
                    pool.wait_ge(S("x_mm"), 10 * rr + 8)
                    for d in range(2):
                        pool.tensor_copy(rhs2[:, 4 * d:4 * d + 4, 0:64],
                                         eX[:, d, :].rearrange("p (h c) -> p h c", h=4)).then_inc(S("rhs_left"), 1)

        @block.scalar
        def _(act):
            A = Steps(act, S("act_steps"))

            def rsqrt(out, src, scale, eps, sem):
                A.did(act.activation(out, src, ACT.Ln, bias=eps, scale=scale))
                A.settle()
                act.activation(out, out, ACT.Exp, scale=-0.5).then_inc(sem, 1)

            def rates(rr):
                for n, x in enumerate((sw, aa)):
                    act.wait_ge(S("w_pre"), 2 * rr + n + 1)
                    act.activation(x, x, ACT.Sigmoid).then_inc(S("w_sig"), 1)

            def deviation(no):
                act.wait_ge(S("o_var"), no + 1)
                A.did(act.activation(rt[:, 16:24], rt[:, 16:24], ACT.Ln, scale=1.0 / HEAD, bias=gn_eps_col))
                A.settle()
                act.activation(rt[:, 16:24], rt[:, 16:24], ACT.Exp, scale=-0.5).then_inc(S("o_rs"), 1)

            seen, high = [0], [0]

            def highs(blocks):
                for c in fresh_slab(seen, high, blocks):
                    act.wait_ge(S(f"slab_in{c % RING}"), 16 * (c // RING + 1))
                    if c >= PARTS:
                        act.wait_ge(S("slab_used"), c - PARTS + 1)
                    act.activation(parts[:, c % PARTS, 0], ring[:, c % RING], ACT.Copy, scale=WSCALE).then_inc(S("split_hi"), 1)

            act.wait_ge(S("c_in"), 16)
            A.did(act.activation(scT, scT, ACT.Silu))
            A.settle()
            act.activation(sc16[:, :, 0], scT, ACT.Copy).then_inc(S("silu_c"), 1)
            act.activation(sc16[:, :, 2], scT, ACT.Copy).then_inc(S("silu_c"), 1)
            highs(0)
            act.wait_ge(S("wr_in"), 16)
            act.activation(wr16[:, 0], wrt[:, 0:KD * EXPERTS], ACT.Copy, scale=WSCALE).then_inc(S("wr_hi"), 1)
            act.wait_ge(S("cst_in"), 16)
            for l in range(DEPTH):
                q, n0 = qs(l), qs(l).start
                if l == 0:
                    act.wait_ge(S("x_in"), 16)
                    act.wait_ge(S("rel_mm"), 8)
                else:
                    act.wait_ge(S(f"xb{l - 1}"), 1)
                for k in range(KD):
                    act.activation(wide[:, k, :], xT[:, k, :], ACT.Square).then_inc(S("na_sq"), 1)
                for s in range(6):
                    i = 6 * l + s
                    highs(KD * SLAB)
                    act.wait_ge(S("mod_mm"), i + 1)
                    if i >= 2:
                        act.wait_ge(S("mod_tr"), i - 1)
                    for x in range(2):
                        act.activation(modrow[0:4, s % 2, 512 * x:512 * x + 512], bank[2 * (s % 2) + x][0:4, :], ACT.Copy,
                                       scale=UNSCALE).then_inc(S("mod_ev"), 1)
                act.wait_ge(S("na_ss"), l + 1)
                rsqrt(rstd, bank[0], 1.0 / D, eps_col, S("na_rstd"))
                act.wait_ge(S("vec_in"), 16 * LAYER_VEC_LOADS * (l + 1))
                act.activation(l16[:, 0, 0], lw, ACT.Copy, scale=WSCALE).then_inc(S("l_hi"), 1)
                act.wait_ge(S("lwm"), l + 1)
                act.activation(l16[:, 0, 1], lwm, ACT.Copy, scale=WSCALE).then_inc(S("l_hi"), 1)
                if l == 0:
                    act.wait_ge(S("rel_out"), 16)
                for i in range(0, Z_SLABS + 4, 2):
                    for n in (i, i + 1):
                        if n < Z_SLABS:
                            highs(SLAB)
                    act.wait_ge(S("z_mm"), (Z_SLABS + 4) * l + i + 1)
                    if i < Z_SLABS:
                        c, qonly = Z_STREAM[i]
                        dst, cc = zT[:, c, :], (q if qonly else slice(0, TOK))
                    else:
                        g = i - Z_SLABS
                        dst, cc = (lor[:, g, :] if g < 2 else zT[:, Z_LMU + g - 2, :]), slice(0, TOK)
                    act.activation(dst[:, cc], bank[i % 4][:, 0:cc.stop - cc.start], ACT.Copy, scale=UNSCALE).then_inc(S("z_ev_a"), 1)
                highs(V_SLABS * SLAB)
                for tt in range(TILES):
                    act.wait_ge(S("v_mm"), TILES * l + tt + 1)
                    act.activation(vT[:, tt, 0:384], bank[4 + tt][:, 0:384], ACT.Copy, scale=UNSCALE).then_inc(S("v_ev"), 1)
                act.wait_ge(S("shifted"), l + 1)
                act.activation(lor[0:64, 0, :], lor[0:64, 0, :], ACT.Tanh).then_inc(S("lor_ready"), 1)
                act.activation(lor[:, 1, :], lor[:, 1, :], ACT.Sigmoid).then_inc(S("lor_ready"), 1)
                for tt in range(TILES):
                    act.wait_ge(S("rkv_tr"), 2 * TILES * l + 2 * tt + 1)
                    act.activation(rkv[:, tt, 0:512], bank[2 * (tt % 2)], ACT.Copy).then_inc(S("rkv_a"), 1)
                act.wait_ge(S("kk_ss"), l + 1)
                A.did(act.activation(rt[:, 0:16], rt[:, 0:16], ACT.Ln))
                A.settle()
                act.activation(rt[:, 0:16], rt[:, 0:16], ACT.Exp, scale=-0.5).then_inc(S("kk_rs"), 1)
                for g, (chunks, _m, width, _g) in enumerate(NORMS):
                    gi, cc = len(NORMS) * l + g, norm_cols(l, g)
                    if g >= 2:
                        act.wait_ge(S("qk_ss"), gi - 1)
                    elif g == 0:
                        act.wait_ge(S("lor_ready"), 2 * (l + 1))
                    for i, c in enumerate(chunks):
                        last = act.activation(sq[:, g % 2, i, cc], zT[:, c, cc], ACT.Square)
                    last.then_inc(S("qk_sq"), 1)
                    act.wait_ge(S("qk_ss"), gi + 1)
                    if g >= 2:
                        act.wait_ge(S("qk_norm"), gi - 1)
                    w = cc.stop - cc.start
                    rsqrt(rsb[:, g % 2, cc], bank[g % 2][:, 0:w], 1.0 / width, eps_col, S("qk_rs"))
                for h in range(4):
                    highs(3)
                    act.wait_ge(S("uq_mm"), 4 * l + h + 1)
                    act.activation(mid[:, h, q], bank[4 + h % 2][:, 0:q.stop - n0], ACT.Copy, scale=UNSCALE).then_inc(S("uq_ev"), 1)
                highs(4 * 2 + 4)
                for tt in range(TILES):
                    act.wait_ge(S("uv_mm"), TILES * l + tt + 1)
                    act.activation(vT[:, tt, 384:640], bank[6 + tt % 2][:, 0:256], ACT.Copy, scale=UNSCALE).then_inc(S("uv_ev"), 1)
                base = sum(len(units(i)) for i in range(l))
                U = units(l)
                for step in range(len(U) + 4):
                    u = step
                    if u < len(U):
                        tt, h = U[u]
                        n, s3 = unit_keys(tt), u % 3
                        act.wait_ge(S("smax"), base + u + 1)
                        src, sc = scores(u)[:, 0:n], unit_scale(h)
                        if 8 <= h < 12 and n == TOK:
                            src, sc = prob[:, s3, 0:n], 1.0
                        if u >= 3:
                            act.wait_ge(S("pt_mm"), base + u - 2)
                            act.wait_ge(S("diag"), base + u - 2)
                        act.activation(prob[:, s3, 0:n], src, ACT.Exp, bias=nmax[:, s3:s3 + 1], scale=sc,
                                       accum_out=rsum[:, s3:s3 + 1]).then_inc(S("exp"), 1)
                    u = step - 4
                    if u >= 0:
                        rows_, chunk, cols = unit_out(*U[u])
                        act.wait_ge(S("pv_mm"), base + u + 1)
                        act.activation(y16[rows_, 0, chunk, cols], attended(u)[rows_, 0:P], ACT.Copy).then_inc(S("o_hi"), 1)
                    u = step - 2
                    if 0 <= u < len(U):
                        n = unit_keys(U[u][0])
                        act.wait_ge(S("pt_mm"), base + u + 1)
                        if u >= 2:
                            act.wait_ge(S("pv_mm"), base + u - 1)
                        act.activation(probT[:, u % 2, 0:n], bank[2 + u % 2][:, 0:n], ACT.Copy).then_inc(S("pt_ev"), 1)
                def outputs(j):
                    no = out_rounds_before(l, j)
                    act.wait_ge(S("o_mm"), no + 1)
                    if no:
                        act.wait_ge(S("yr"), no)
                    o4 = oo.rearrange("p (q x c) -> p q x c", q=4, x=2)
                    for x, b in enumerate((7, 3)):
                        act.activation(o4[:, :, x, :], bank[b][:, 0:256].rearrange("p (q c) -> p q c", q=4), ACT.Copy).then_inc(S("o_read"), 1)

                for j in range(ROUNDS):
                    rr = l * ROUNDS + j
                    if j == 0:
                        rates(rr)
                    act.wait_ge(S("cum"), 2 * rr + 1)
                    for dst, b, s in ((eX, 0, -DECAY), (eL, 2, -DECAY), (eN, 2, DECAY), (eA, 4, -DECAY)):
                        act.activation(dst, bank[b].rearrange("p (d c) -> p d c", d=2), ACT.Exp, scale=s
                                       ).then_inc(S("decays"), 1)
                    act.wait_ge(S("st"), 2 * rr + l + 1)
                    act.wait_ge(S("cum"), 2 * rr + 2)
                    act.activation(ecol, bank[1][:, 0:8], ACT.Exp, scale=-DECAY).then_inc(S("decays"), 1)
                    if j and has_out(l, j - 1):
                        outputs(j - 1)
                    for i in range(0, RQ, 2):
                        act.wait_ge(S("fm_tr"), RQ * rr + i + 1)
                        act.activation(fmt[:, i], bank[i].rearrange("p (a t) -> p a t", a=4), ACT.Copy
                                       ).then_inc(S("fm_a"), 1)
                    for d in range(2):
                        act.wait_ge(S("t_tr"), 2 * rr + d + 1)
                        act.activation(Tm[:, 4 * d:4 * d + 4], bank[d].rearrange("p (u t) -> p u t", u=4), ACT.Copy
                                       ).then_inc(S("t_ev"), 1)
                    for lev in range(1, LEVELS):
                        for d in range(2):
                            act.wait_ge(S("x_mm"), 10 * rr + 2 * (lev - 1) + d + 1)
                            if lev > 1:
                                act.wait_ge(S("yt_mm"), 10 * rr + 2 * (lev - 2) + d + 1)
                            act.activation(Xs[:, 4 * d:4 * d + 4], bank[2 + d].rearrange("p (u t) -> p u t", u=4),
                                           ACT.Copy).then_inc(S("x_ev"), 1)
                        if lev == 3 and j and has_out(l, j - 1):
                            deviation(out_rounds_before(l, j - 1))
                    act.wait_ge(S("av_mm"), rr + 1)
                    act.activation(rhs2[:, :, 64:128], bank[0].rearrange("p (u c) -> p u c", u=8), ACT.Copy
                                   ).then_inc(S("av_ev"), 1)
                    for d in range(2):
                        act.wait_ge(S("wu_mm"), 2 * rr + d + 1)
                        act.activation(nwu[:, 4 * d:4 * d + 4], bank[2 + d].rearrange("p (u c) -> p u c", u=4),
                                       ACT.Copy, scale=-1.0).then_inc(S("nwu"), 1)
                    if j < ROUNDS - 1:
                        rates(rr + 1)
                    act.wait_ge(S("g0_mm"), rr + 1)
                    for c in range(2):
                        act.activation(gh[:, c], bank[(5, 1)[c]].rearrange("p (x q v) -> p x q v", x=2, q=4), ACT.Copy
                                       ).then_inc(S("g0_ev"), 1)
                outputs(ROUNDS - 1)
                deviation(out_rounds_before(l, ROUNDS - 1))
                for i, tt in enumerate(qtiles(l)):
                    act.wait_ge(S("yr_tr"), (TILES * l if l else 0) + i + 1)
                    act.activation(y16[:, 0, 6:8, tt * P:(tt + 1) * P], bank[i % 2][:, 0:256].rearrange("p (k t) -> p k t", k=2),
                                   ACT.Copy).then_inc(S("yr_hi"), 1)
                w = q.stop - n0
                for i in range(4 * KD):
                    gi = 4 * KD * l + i
                    highs(KD)
                    act.wait_ge(S("gate_mm"), gi + 1)
                    if i >= 2:
                        act.wait_ge(S("gated"), gi - 1)
                    act.activation(gate_sb[:, i % 2, 0:w], bank[i % 2][:, 0:w], ACT.Sigmoid, scale=UNSCALE).then_inc(S("gate"), 1)
                    highs(BRANCH_CHUNKS[i % 4])
                post_norm(act, highs, l, 0)
                act.wait_ge(S(f"xa{l}"), 1)
                for k in range(KD):
                    act.activation(wide[:, k, q], xT[:, k, q], ACT.Square).then_inc(S("nb_sq"), 1)
                act.wait_ge(S("nb_ss"), l + 1)
                rsqrt(rstd[:, q], bank[0][:, 0:w], 1.0 / D, eps_col, S("nb_rstd"))
                if l % 2 == 0:
                    for j in range(FFC):
                        highs(KD)
                        act.wait_ge(S("fg_mm"), j + 1)
                        if j >= 2:
                            act.wait_ge(S("hid"), j - 1)
                        act.activation(gate_sb[:, j % 2, 0:w], bank[j % 2][:, 0:w], ACT.Silu, scale=UNSCALE).then_inc(S("silu"), 1)
                        highs(KD)
                else:
                    act.wait_ge(S("r_max"), 1)
                    for i in range(2):
                        act.activation(rt[:, 32 + 8 * i:40 + 8 * i], rt[:, 32 + 8 * i:40 + 8 * i], ACT.Exp,
                                       bias=rt[:, 48 + i:49 + i]).then_inc(S("r_exp"), 1)
                    for i in range(4):
                        act.wait_ge(S("cw_mm"), i + 1)
                        act.activation(cw[:, 2 * i:2 * i + 2], bank[i].rearrange("p (e t) -> p e t", e=2), ACT.Copy
                                       ).then_inc(S("cw_ev"), 1)
                    for e in range(EXPERTS):
                        for j in range(EFC):
                            i = e * EFC + j
                            highs(KD)
                            act.wait_ge(S("eg_mm"), i + 1)
                            if i >= 2:
                                act.wait_ge(S("ehid"), i - 1)
                            act.activation(gate_sb[:, i % 2, 0:w], bank[i % 2][:, 0:w], ACT.Silu, scale=UNSCALE).then_inc(S("esilu"), 1)
                            highs(KD)
                        highs(EFC * KD)
                post_norm(act, highs, l, 1)

        @block.tensor
        def _(pe):
            slabs = [0]

            def mm(out, lhsT, rhs, start=True, stop=True, skip=False):
                return pe.matmul(out, lhsT, rhs, start=start, stop=stop, skip_group_check=skip)

            def slab():
                n = slabs[0]
                slabs[0] += 1
                pe.wait_ge(S("split_lo"), n + 1)
                return parts[:, n % PARTS]

            def frees_last(ins):
                if slabs[0] > 1:
                    ins.then_inc(S("slab_used"), 1)

            blocks = [None, SLAB]

            def product(out, rhs_of, n, start=True, stop=True, done=None, skip=False):
                for k in range(n):
                    fresh = blocks[1] == SLAB
                    if fresh:
                        blocks[0], blocks[1] = slab(), 0
                    wh, wl = (blocks[0][:, x, blocks[1], :] for x in range(2))
                    blocks[1] += 1
                    ins = mm(out, wh, rhs_of(0, k), k == 0 and start, False, skip)
                    if fresh:
                        frees_last(ins)
                    mm(out, wh, rhs_of(1, k), False, False, skip)
                    ins = mm(out, wl, rhs_of(0, k), False, k == n - 1 and stop, skip)
                if done:
                    ins.then_inc(S(done), 1)

            def by_token(out, x_of, w_of, n):
                for k in range(n):
                    mm(out, x_of(0, k), w_of(0, k), k == 0, False)
                    mm(out, x_of(1, k), w_of(0, k), False, False)
                    ins = mm(out, x_of(0, k), w_of(1, k), False, k == n - 1)
                return ins

            pe.wait_ge(S("rel_in"), 32)
            for i in range(8):
                mm(bank[i][0:56, :], arena[0:32, 4096:4152], arena[0:32, 512 * i:512 * i + 512]).then_inc(S("rel_mm"), 1)
            pe.wait_ge(S("rel_ev"), 8)
            pe.wait_ge(S("cst_in"), 16)
            pe.wait_ge(S("silu_c"), 1)
            for l in range(DEPTH):
                q, n0 = qs(l), qs(l).start
                w = q.stop - n0
                if l:
                    pe.wait_ge(S(f"xb{l - 1}"), 1)
                for s in range(6):
                    i = 6 * l + s
                    b = 2 * (s % 2)
                    if s >= 2:
                        pe.wait_ge(S("mod_ev"), 2 * (i - 1))
                    for k in range(KD):
                        sl = slab()
                        for x in range(2):
                            for part in range(2):
                                ins = mm(bank[b + x][0:4, :], sc16[:, k, 2 * part:2 * part + 2].rearrange("p x j -> p (x j)"),
                                         sl[:, part, 4 * x:4 * x + 4].rearrange("p b c -> p (b c)"), k == 0 and part == 0, k == KD - 1 and part == 1)
                                if x == 0 and part == 0:
                                    frees_last(ins)
                    ins.then_inc(S("mod_mm"), 1)
                    for o in ([s - 1] if s else []) + ([s] if s == 5 else []):
                        pe.wait_ge(S("mod_ev"), 2 * (6 * l + o + 1))
                        for c in range(KD):
                            ins = mm(bank[7][:, 2 * (KD * o + c):2 * (KD * o + c) + 2], modrow[0:4, o % 2, P * c:P * c + P],
                                     cst[0:4, C_FOLD:C_FOLD + 2])
                        ins.then_inc(S("mod_tr"), 1)
                for k in range(KD):
                    pe.wait_ge(S("na_sq"), KD * l + k + 1)
                    last = mm(bank[0], ones, wide[:, k, :], k == 0, k == KD - 1)
                last.then_inc(S("na_ss"), 1)
                for i in range(Z_SLABS):
                    qonly = Z_STREAM[i][1]
                    cc = q if qonly else slice(0, TOK)
                    if i >= 4:
                        pe.wait_ge(S(("z_ev_a", "z_ev_d")[i % 2]), (Z_EVEN, Z_ODD)[i % 2] * l + (i - 4) // 2 + 1)
                    elif i == 0:
                        pe.wait_ge(S("ha"), l + 1)
                    product(bank[i % 4][:, 0:cc.stop - cc.start], lambda x, k: h16[:, x, k, cc], KD, done="z_mm")
                for g in range(4):
                    i = Z_SLABS + g
                    pe.wait_ge(S(("z_ev_a", "z_ev_d")[i % 2]), (Z_EVEN, Z_ODD)[i % 2] * l + (i - 4) // 2 + 1)
                    pe.wait_ge(S("l_lo"), 2 * l + g // 2 + 1)
                    by_token(bank[i % 4], lambda x, k: l16[:, x, g // 2, g % 2, k, :], lambda x, k: h16[:, x, k, :], KD).then_inc(S("z_mm"), 1)
                pe.wait_ge(S("mod_ready"), l + 1)
                for s in range(V_SLABS):
                    wv = slab()
                    for tt in range(TILES):
                        for k in range(KD):
                            o, c = bank[4 + tt][:, s * P:(s + 1) * P], slice(tt * P, (tt + 1) * P)
                            ins = mm(o, h16[:, 0, k, c], wv[:, 0, k, :], k == 0, False)
                            if tt == 0 and k == 0:
                                frees_last(ins)
                            mm(o, h16[:, 1, k, c], wv[:, 0, k, :], False, False)
                            ins = mm(o, h16[:, 0, k, c], wv[:, 1, k, :], False, k == KD - 1)
                        if s == V_SLABS - 1:
                            ins.then_inc(S("v_mm"), 1)
                pe.wait_ge(S("shifted"), l + 1)
                pe.wait_ge(S("z_ev_a"), Z_EVEN * (l + 1))
                for tt in range(TILES):
                    b = 2 * (tt % 2)
                    if tt >= 2:
                        pe.wait_ge(S("rkv_a"), TILES * l + tt - 1)
                        pe.wait_ge(S("rkv_d"), TILES * l + tt - 1)
                    for i in range(6):
                        ins = pe.transpose(bank[b + i // 4][:, (i % 4) * P:(i % 4 + 1) * P], zT[:, Z_R + i, tt * P:(tt + 1) * P], ident)
                        if i in (3, 5):
                            ins.then_inc(S("rkv_tr"), 1)
                pe.wait_ge(S("rkv_a"), TILES * (l + 1))
                pe.wait_ge(S("rkv_d"), TILES * (l + 1))
                for g, (chunks, ones_of, width, _g) in enumerate(NORMS):
                    gi, cc = len(NORMS) * l + g, norm_cols(l, g)
                    pe.wait_ge(S("qk_sq"), gi + 1)
                    if g >= 2:
                        pe.wait_ge(S("qk_rs"), gi - 1)
                    for i in range(len(chunks)):
                        ins = mm(bank[g % 2][:, 0:cc.stop - cc.start], ones_of, sq[:, g % 2, i, cc], i == 0, i == len(chunks) - 1)
                    ins.then_inc(S("qk_ss"), 1)
                pe.wait_ge(S("qk_norm"), len(NORMS) * (l + 1))
                pe.wait_ge(S("v_ev"), TILES * (l + 1))
                for h in range(4):
                    if h >= 2:
                        pe.wait_ge(S("uq_ev"), 4 * l + h - 1)
                    product(bank[4 + h % 2][:, 0:w], lambda x, k: z16[Z_CQ + k][:, x, q], 3, done="uq_mm")
                ROT = 2
                for i, (x, kind) in enumerate(rotations(l)):
                    if i == 6:
                        for h in range(4):
                            if h == 0:
                                pe.wait_ge(S("uq_ev"), 4 * l + 4)
                            if h < 2:
                                pe.wait_ge(S("rot"), 10 * l + 6)
                            else:
                                pe.wait_ge(S("uk_ev"), 4 * l + h - 1)
                            product(bank[4 + h % 2], lambda x, k: z16[Z_CKV + k][:, x, :], 2, done="uk_mm")
                    if i >= 2:
                        pe.wait_ge(S("rot"), 10 * l + i - 1)
                    mm(bank[2 + i % 2][:, 0:SEQ], cst[:, C_ROT + kind * P:C_ROT + (kind + 1) * P], x).then_inc(S("rot_mm"), 1)
                wuv = blocks[0][:, :, blocks[1]:SLAB, :]
                blocks[1] = SLAB
                for tt in range(TILES):
                    if tt >= 2:
                        pe.wait_ge(S("uv_ev"), TILES * l + tt - 1)
                    for s in range(2):
                        ins = by_token(bank[6 + tt % 2][:, s * P:(s + 1) * P], lambda x, k: z16[Z_CKV + k][:, x, tt * P:(tt + 1) * P],
                                       lambda x, k: wuv[:, x, 2 * s + k, :], 2)
                    ins.then_inc(S("uv_mm"), 1)
                pe.wait_ge(S("rot"), 10 * (l + 1))
                pe.wait_ge(S("uk_ev"), 4 * (l + 1))
                pe.wait_ge(S("uv_ev"), TILES * (l + 1))
                base, U = sum(len(units(i)) for i in range(l)), units(l)
                for step in range(len(U) + 3):
                    u = step
                    if u < len(U):
                        tt, h = U[u]
                        if u >= 3:
                            pe.wait_ge(S("exp"), base + u - 2)
                        mm(scores(u)[:, 0:unit_keys(tt)], unit_q(tt, h), unit_k(tt, h)).then_inc(S("s_mm"), 1)
                    u = step - 2
                    if 0 <= u < len(U):
                        pe.wait_ge(S("exp"), base + u + 1)
                        if u >= 2:
                            pe.wait_ge(S("pt_ev"), base + u - 1)
                        pe.wait_ge(S("diag"), base + u + 1)
                        for j in range(unit_keys(U[u][0]) // P):
                            ins = mm(bank[2 + u % 2][:, j * P:(j + 1) * P], prob[:, u % 3, j * P:(j + 1) * P], diag[:, u % 3])
                        ins.then_inc(S("pt_mm"), 1)
                    u = step - 3
                    if u >= 0:
                        pe.wait_ge(S("pt_ev"), base + u + 1)
                        if u >= 3:
                            pe.wait_ge(S("o_ev"), base + u - 2)
                        nk = unit_keys(U[u][0]) // P
                        for j in range(nk):
                            ins = mm(attended(u)[unit_out(*U[u])[0], 0:P], unit_v(U[u][1], j), probT[:, u % 2, j * P:(j + 1) * P],
                                     j == 0, j == nk - 1)
                        ins.then_inc(S("pv_mm"), 1)
                pe.wait_ge(S("o_ev"), base + len(U))
                pe.wait_ge(S("lor_ready"), 2 * (l + 1))
                pe.wait_ge(S("kk_ready"), l + 1)

                def rates(j):
                    for n in range(2):
                        for d in range(2):
                            r0 = 64 * n + 32 * d
                            tile = RW_ORDER[d][j]
                            ins = mm(bank[RATE_BANKS[2 * n + d]][:, 0:256], lor[r0:r0 + 32, 0, tile * P:(tile + 1) * P], lora2[r0:r0 + 32, 0:256])
                        ins.then_inc(S("w_mm"), 1)

                U8 = [(d, h, 4 * d + h, 2 * d + h // 2, slice(64 * (h % 2), 64 * (h % 2) + 64)) for d in range(2) for h in range(4)]

                def sums(j):
                    rr = l * ROUNDS + j
                    pe.wait_ge(S("w_pre"), 2 * rr + 2)
                    pe.wait_ge(S("w_sig"), 2 * rr + 1)
                    for b, of in ((0, (0, 2)), (2, (1, 3)), (4, (2, 0))):
                        for d in range(2):
                            ins = mm(bank[b][:, 256 * d:256 * d + 256], tri(of[d]), sw[:, d, :])
                    ins.then_inc(S("cum"), 1)
                    if j:
                        pe.wait_ge(S("g0_ev"), 2 * rr)
                    for qq in range(RQ):
                        ins = mm(bank[1][:, 2 * qq:2 * qq + 2], sw[:, qq // 2, P * (qq % 2):P * (qq % 2) + P],
                                 blk.rearrange("p (c x) -> p c x", c=2)[:, :, 0])
                    ins.then_inc(S("cum"), 1)

                def outputs(j):
                    for d, h, u, qq, hh in U8:
                        o = bank[(7, 3)[h % 2]][:, 64 * qq:64 * qq + 64]
                        mm(o, am[:, u, 3], rkv[:, RW_ORDER[d][j], 512 + 64 * h:576 + 64 * h], True, False, True)
                        mm(o, am[:, u, 1], nwu[:, u, 64:128], False, False, True)
                        for s in range(2):
                            c = CHUNK_ORDER[d][s]
                            cs = slice(64 * c, 64 * c + 64)
                            ins = mm(o[cs, :], m1[hh, qq, cs], state[hh, (2 * j + s) % 3, qq], False, s == 1, True)
                    ins.then_inc(S("o_mm"), 1)

                def gates(j):
                    for d in range(2):
                        tile = RW_ORDER[d][j]
                        ins = mm(bank[d][:, 0:256], lor[64 * d:64 * d + 64, 1, tile * P:(tile + 1) * P], lora2[64 * d:64 * d + 64, 256:512])
                    ins.then_inc(S("g_mm"), 1)

                for j in range(ROUNDS):
                    rr = l * ROUNDS + j
                    tau = [RW_ORDER[d][j] for d in range(2)]
                    out = RW_ORDER[0][j] in qtiles(l)

                    def v_of(d, h, rows_=slice(0, P)):
                        return rkv[rows_, tau[d], 512 + 64 * h:576 + 64 * h]

                    if j == 0:
                        rates(j)
                        sums(j)
                    if j and has_out(l, j - 1):
                        pe.wait_ge(S("m1"), rr)
                        outputs(j - 1)
                    for d in range(2):
                        pe.wait_ge(S("prod"), 2 * rr + d + 1)
                        for hp in range(2):
                            if d and hp and out_rounds_before(l, j):
                                pe.wait_ge(S("o_read"), 2 * out_rounds_before(l, j))
                            for a, x in enumerate((eX, eL, Bd, eN)):
                                ins = pe.transpose(bank[2 * d + hp][:, a * P:(a + 1) * P], x[:, d, P * hp:P * hp + P], ident)
                            ins.then_inc(S("fm_tr"), 1)
                    for d, h, u, qq, hh in U8:
                        if h % 2 == 0:
                            pe.wait_ge(S(("fm_a", "fm_d")[qq % 2]), 2 * rr + qq // 2 + 1)
                        if u >= 4:
                            pe.wait_ge(S("am_done"), 8 * rr + u - 3)
                        elif u == 0:
                            pe.wait_ge(S("decays"), 5 * (rr + 1))
                        b = bank[4 + u % 4]
                        mm(b[:, 0:256], fmt[hh, qq, 2], fmt[hh, qq, 0:2])
                        mm(b[:, 256:512], fmt[hh, qq, 3], fmt[hh, qq, 0:2]).then_inc(S("a_mm"), 1)
                    for lev in range(1, LEVELS):
                        for d in range(2):
                            if lev == 1:
                                pe.wait_ge(S("tt0"), 2 * rr + d + 1)
                                for h in range(4):
                                    ins = pe.transpose(bank[d][:, h * P:(h + 1) * P], TT[:, 4 * d + h], ident)
                                ins.then_inc(S("t_tr"), 1)
                            pe.wait_ge(S("ct_done"), 10 * rr + 2 * (lev - 1) + d + 1)
                            if lev == 1:
                                pe.wait_ge(S("t_ev"), 2 * rr + d + 1)
                            else:
                                pe.wait_ge(S("inv"), 10 * rr + 2 * (lev - 2) + d + 1)
                            for h in range(4):
                                ins = mm(bank[2 + d][:, h * P:(h + 1) * P], ct[:, (lev - 1) % 2, 4 * d + h], Tm[:, 4 * d + h])
                            ins.then_inc(S("x_mm"), 1)
                        if lev == LEVELS - 1:
                            if j and has_out(l, j - 1):
                                pe.wait_ge(S("g_read"), out_rounds_before(l, j - 1) + 1)
                            for d, h, u, qq, hh in U8:
                                ins = mm(bank[0][:, 64 * u:64 * u + 64], am[:, u, 2], v_of(d, h))
                            ins.then_inc(S("av_mm"), 1)
                        for d in range(2):
                            pe.wait_ge(S("x_ev"), 10 * rr + 2 * (lev - 1) + d + 1)
                            for h in range(4):
                                u = 4 * d + h
                                if lev < LEVELS - 1:
                                    mm(bank[4 + d][:, h * P:(h + 1) * P], TT[:, u], Xs[:, u])
                                ins = mm(bank[6 + d][:, h * P:(h + 1) * P], Xs[:, u], TT[:, u])
                            ins.then_inc(S("yt_mm"), 1)
                        if lev == 2 and j and has_out(l, j - 1):
                            gates(j - 1)
                    pe.wait_ge(S("inv"), 10 * (rr + 1))
                    pe.wait_ge(S("av_ev"), rr + 1)
                    pe.wait_ge(S("rhs_left"), 2 * (rr + 1))
                    for d, h, u, qq, hh in U8:
                        ins = mm(bank[2 + d][:, h * P:(h + 1) * P], TT[:, u], rhs2[:, u])
                        if h == 3:
                            ins.then_inc(S("wu_mm"), 1)
                    if j < ROUNDS - 1:
                        rates(j + 1)
                    for d, h, u, qq, hh in U8:
                        if h == 0:
                            pe.wait_ge(S("nwu"), 2 * rr + d + 1)
                        ins = mm(bank[4][hh, qq * P:(qq + 1) * P], nwu[:, u, 0:64], am[:, u, 1])
                    ins.then_inc(S("m1_mm"), 1)
                    pe.wait_ge(S("prod_end"), rr + 1)
                    if j < ROUNDS - 1:
                        pe.wait_ge(S("w_pre"), 2 * rr + 3)
                    for d, h, u, qq, hh in U8:
                        for c in range(2):
                            cs, b = slice(64 * c, 64 * c + 64), bank[(5, 1)[c]]
                            mm(b[hh, 64 * qq:64 * qq + 64], nwu[cs, u, 0:64], Be[cs, d, 64 * h:64 * h + 64])
                            o = b[hh, 256 + 64 * qq:320 + 64 * qq]
                            mm(o, Be[cs, d, 64 * h:64 * h + 64], nwu[cs, u, 64:128], True, False)
                            ins = mm(o, eA[cs, d, 64 * h:64 * h + 64], v_of(d, h, cs), False, True)
                    ins.then_inc(S("g0_mm"), 1)
                    if j < ROUNDS - 1:
                        pe.wait_ge(S("m1"), rr + 1)
                        sums(j + 1)
                    pe.wait_ge(S("g0_ev"), 2 * (rr + 1))
                    for s in range(2):
                        pe.wait_ge(S("st"), 2 * rr + s + l + 1)
                        for d, h, u, qq, hh in U8:
                            ins = mm(bank[6][hh, 256 * s + 64 * qq:256 * s + 64 * qq + 64], g0[hh, CHUNK_ORDER[d][s], qq],
                                     state[hh, (2 * j + s) % 3, qq])
                        ins.then_inc(S("st_mm"), 1)
                pe.wait_ge(S("m1"), ROUNDS * (l + 1))
                outputs(ROUNDS - 1)
                gates(ROUNDS - 1)
                yb = TILES * l
                for i, tt in enumerate(qtiles(l)):
                    if i == 0:
                        pe.wait_ge(S("yr"), 4 if l == 0 else 6)
                    if i >= 2:
                        pe.wait_ge(S("yr_ev"), yb + i - 1)
                    for k in range(2):
                        ins = pe.transpose(bank[i % 2][:, k * P:(k + 1) * P], yr[:, tt, k * P:(k + 1) * P], ident)
                    ins.then_inc(S("yr_tr"), 1)
                pe.wait_ge(S("yr_ev"), yb + len(qtiles(l)))
                pe.wait_ge(S("st"), (2 * ROUNDS) * (l + 1) + l + 1)
                for i in range(4 * KD):
                    m, br = divmod(i, 4)
                    gi = 4 * KD * l + i
                    if i >= 2:
                        pe.wait_ge(S("gate"), gi - 1)
                    product(bank[i % 2][:, 0:w], lambda x, k: h16[:, x, k, q], KD, done="gate_mm")
                    if i >= 2:
                        pe.wait_ge(S("gated"), gi - 1)
                    product(bank[2 + i % 2][:, 0:w], lambda x, k: y16[:, x, BRANCH_FIRST[br] + k, q], BRANCH_CHUNKS[br], done="br_mm")
                pe.wait_ge(S("merged"), KD * (l + 1))
                for m in range(KD):
                    post_bank_free(pe, l, 0, m)
                    product(bank[4 + m % 4][:, 0:w], lambda x, k: m16[:, x, k, q], KD, done="po_mm")
                post_sum(pe, l, 0)
                for k in range(KD):
                    pe.wait_ge(S("nb_sq"), KD * l + k + 1)
                    if k == 0:
                        pe.wait_ge(S(f"xa{l}"), 1)
                    ins = mm(bank[0][:, 0:w], ones, wide[:, k, q], k == 0, k == KD - 1)
                ins.then_inc(S("nb_ss"), 1)
                pe.wait_ge(S("hb"), l + 1)
                if l % 2 == 0:
                    for j in range(FFC):
                        if j >= 2:
                            pe.wait_ge(S("silu"), j - 1)
                        product(bank[j % 2][:, 0:w], lambda x, k: h16[:, x, k, q], KD, done="fg_mm")
                        if j >= 2:
                            pe.wait_ge(S("hid"), j - 1)
                        product(bank[2 + j % 2][:, 0:w], lambda x, k: h16[:, x, k, q], KD, done="fu_mm")
                    pe.wait_ge(S("hid"), FFC)
                    for m in range(KD):
                        post_bank_free(pe, l, 1, m)
                        product(bank[4 + m % 4][:, 0:w], lambda x, k: hid[:, x, k, q], FFC, done="po_mm")
                else:
                    pe.wait_ge(S("wr_lo"), 1)
                    for i in range(2):
                        ins = by_token(bank[0][:, 8 * i:8 * i + 8], lambda x, k: h16[:, x, k, CTX + P * i:CTX + P * (i + 1)],
                                       lambda x, k: wr16[:, x, 8 * k:8 * k + 8], KD)
                    ins.then_inc(S("r_mm"), 1)
                    pe.wait_ge(S("comb"), 1)
                    for e in range(EXPERTS):
                        for i in range(2):
                            ins = mm(bank[e // 2][:, 256 * (e % 2) + P * i:256 * (e % 2) + P * (i + 1)],
                                     rt[:, 64 + 8 * i + e:65 + 8 * i + e].broadcast_to([P, P]), ident)
                        if e % 2:
                            ins.then_inc(S("cw_mm"), 1)
                    pe.wait_ge(S("cw_ev"), 4)
                    for e in range(EXPERTS):
                        for j in range(EFC):
                            i = e * EFC + j
                            if i >= 2:
                                pe.wait_ge(S("esilu"), i - 1)
                            product(bank[i % 2][:, 0:w], lambda x, k: h16[:, x, k, q], KD, done="eg_mm")
                            if i >= 2:
                                pe.wait_ge(S("ehid"), i - 1)
                            product(bank[2 + i % 2][:, 0:w], lambda x, k: h16[:, x, k, q], KD, done="eu_mm")
                        pe.wait_ge(S("ehid"), EFC * (e + 1))
                        for m in range(KD):
                            product(bank[4 + m // 2][:, 256 * (m % 2):256 * (m % 2) + 256], lambda x, k: ehid[:, e % 2, x, k, :], EFC,
                                    start=e == 0 and m % 2 == 0, stop=e == EXPERTS - 1, skip=True,
                                    done="po_mm" if e == EXPERTS - 1 else "edown" if m == KD - 1 else None)
                post_sum(pe, l, 1)

        @block.vector
        def _(dve):
            V = Steps(dve, S("vec_steps"))
            vs = S("vec_steps")

            def bc(x, *shape):
                return x.broadcast_to(list(shape))

            seen, low = [0], [0]

            def lows(blocks):
                for c in fresh_slab(seen, low, blocks):
                    dve.wait_ge(S("split_hi"), c + 1)
                    dve.scalar_tensor_tensor(out=parts[:, c % PARTS, 1], in0=ring[:, c % RING], scalar=WSCALE, in1=parts[:, c % PARTS, 0],
                                             op0=ALU.mult, op1=ALU.subtract).then_inc(S("split_lo"), 1)

            for i in range(8):
                dve.wait_ge(S("rel_mm"), i + 1)
                dve.tensor_copy(relrow[0:56, 512 * i:512 * i + 512], bank[i][0:56, :]).then_inc(S("rel_ev"), 1)
            dve.wait_ge(S("silu_c"), 2)
            dve.memset(sc16[:, :, 3], 0.0).then_inc(S("c_low"), 1)
            dve.tensor_tensor(sc16[:, :, 1], scT, sc16[:, :, 0], ALU.subtract).then_inc(S("c_low"), 1)
            lows(0)
            dve.wait_ge(S("wr_hi"), 1)
            dve.scalar_tensor_tensor(out=wr16[:, 1], in0=wrt[:, 0:KD * EXPERTS], scalar=WSCALE, in1=wr16[:, 0],
                                     op0=ALU.mult, op1=ALU.subtract).then_inc(S("wr_lo"), 1)
            dve.wait_ge(S("cst_in"), 16)
            dve.wait_ge(S("vecs_in"), 16)
            for l in range(DEPTH):
                q, n0 = qs(l), qs(l).start
                w = q.stop - n0
                vec, mod, gmod = vecs[:, l], mods[:, l], gmods[:, l]
                lows(3 * SLAB)
                dve.wait_ge(S("vec_in"), 16 * LAYER_VEC_LOADS * (l + 1))
                for i, (g, c0, c1) in enumerate(((0, 0, 64), (0, 64, 128), (1, 0, 128))):
                    ins = dve.tensor_tensor(lwm[:, g, :, c0:c1], lw[:, g, :, c0:c1],
                                            bc(mux[:, 8 * i:8 * i + 8].unsqueeze(2), P, KD, c1 - c0), ALU.mult)
                ins.then_inc(S("lwm"), 1)
                lows(MOD_SLABS * SLAB - 3 * SLAB)
                dve.wait_ge(S("mod_tr"), 6 * (l + 1))
                V.did(dve.tensor_tensor(mod, bank[7][:, 0:96].rearrange("p (n j) -> p n j", j=2),
                                        bc(vec[:, V_BMOD:V_BMOD + 48].unsqueeze(2), P, 48, 2), ALU.add))
                V.settle()
                for i, (sec, col) in enumerate(((1, V_NMPRE), (2, V_NMPOST), (4, V_NFPRE), (5, V_NFPOST))):
                    gain = bc(vec[:, col:col + KD].unsqueeze(2), P, KD, 2)
                    src = mod[:, 8 * sec:8 * sec + 8, :]
                    if sec in (1, 4):
                        ins = dve.scalar_tensor_tensor(out=gmod[:, i], in0=src, scalar=1.0, in1=gain, op0=ALU.add, op1=ALU.mult)
                    else:
                        ins = dve.tensor_tensor(gmod[:, i], src, gain, ALU.mult)
                ins.then_inc(S("mod_ready"), 1)
                dve.wait_ge(S("mod_ready"), l + 1)

                def modulated(which, shift, cols_segs):
                    for k in range(KD):
                        for cc, jc in cols_segs:
                            V.did(dve.tensor_tensor(wide[:, k, cc], xT[:, k, cc], rstd[:, cc], ALU.mult))
                    V.settle()
                    for k in range(KD):
                        for cc, jc in cols_segs:
                            V.did(dve.tensor_scalar(wide[:, k, cc], wide[:, k, cc], gmod[:, which, k, jc:jc + 1],
                                                    mod[:, 8 * shift + k, jc:jc + 1], ALU.mult, ALU.add))
                    V.settle()
                    cc = slice(min(c.start for c, _j in cols_segs), TOK)
                    for k in range(KD):
                        V.did(dve.tensor_copy(h16[:, 0, k, cc], wide[:, k, cc]))
                    V.settle()
                    for k in range(KD):
                        ins = dve.tensor_tensor(h16[:, 1, k, cc], wide[:, k, cc], h16[:, 0, k, cc], ALU.subtract)
                    return ins

                dve.wait_ge(S("na_rstd"), l + 1)
                modulated(0, 0, [(slice(CTX, TOK), 0), (slice(0, CTX), 1)]).then_inc(S("ha"), 1)
                for n, of in enumerate((lw, lwm)):
                    dve.wait_ge(S("l_hi"), 2 * l + n + 1)
                    dve.scalar_tensor_tensor(out=l16[:, 1, n], in0=of, scalar=WSCALE, in1=l16[:, 0, n],
                                             op0=ALU.mult, op1=ALU.subtract).then_inc(S("l_lo"), 1)
                if l == 0:
                    dve.wait_ge(S("rel_out"), 16)
                for i in range(1, Z_SLABS + 4, 2):
                    for n in (i - 1, i):
                        if n < Z_SLABS:
                            lows(SLAB)
                    dve.wait_ge(S("z_mm"), (Z_SLABS + 4) * l + i + 1)
                    if i < Z_SLABS:
                        c, qonly = Z_STREAM[i]
                        dst, cc = zT[:, c, :], (q if qonly else slice(0, TOK))
                    else:
                        g = i - Z_SLABS
                        dst, cc = (lor[:, g, :] if g < 2 else zT[:, Z_LMU + g - 2, :]), slice(0, TOK)
                    dve.tensor_scalar(dst[:, cc], bank[i % 4][:, 0:cc.stop - cc.start], UNSCALE, None, ALU.mult).then_inc(S("z_ev_d"), 1)
                lows(V_SLABS * SLAB)
                dve.wait_ge(S("z_ev_a"), Z_EVEN * (l + 1))
                dve.wait_ge(S("z_ev_d"), Z_ODD * (l + 1))
                src = arena[:, Z_R * TOK:(Z_R + 8) * TOK].rearrange("p (s t) -> p s t", t=CTX)
                nb = arena[:, MID:MID + 8 * TOK].rearrange("p (s t) -> p s t", t=CTX)
                V.did(dve.tensor_tensor(nb[:, :, 1:CTX - 1], src[:, :, 0:CTX - 2], src[:, :, 2:CTX], ALU.add))
                V.did(dve.tensor_copy(nb[:, :, 0:1], src[:, :, 1:2]))
                V.did(dve.tensor_copy(nb[:, :, CTX - 1:CTX], src[:, :, CTX - 2:CTX - 1]))
                V.settle()
                V.did(dve.scalar_tensor_tensor(out=nb, in0=nb, scalar=0.5, in1=src, op0=ALU.mult, op1=ALU.subtract))
                V.settle()
                for i in range(6):
                    z = zT[:, Z_R + i, :]
                    dve.scalar_tensor_tensor(out=z, in0=mid[:, i, :], scalar=vec[:, V_MUP + i:V_MUP + i + 1], in1=z,
                                             op0=ALU.mult, op1=ALU.add)
                dve.tensor_tensor(lor, lor, mid[:, 6:8, :], ALU.add).then_inc(S("shifted"), 1)
                for tt in range(TILES):
                    dve.wait_ge(S("rkv_tr"), 2 * TILES * l + 2 * tt + 2)
                    dve.tensor_copy(rkv[:, tt, 512:768], bank[2 * (tt % 2) + 1][:, 0:256]).then_inc(S("rkv_d"), 1)
                dve.wait_ge(S("rkv_a"), TILES * (l + 1))
                hs = kk.rearrange("p t (h c) -> p (t h) c", h=4)
                V.did(dve.tensor_tensor(kk, rkv[:, :, 256:512], bc(rows[:, B_KK:B_KK + 256].unsqueeze(1), P, TILES, 256), ALU.mult))
                V.settle()
                scr = arena[:, MID:MID + 1024].rearrange("p (t c) -> p t c", t=TILES)
                V.did(dve.tensor_tensor(scr, kk, kk, ALU.mult))
                V.settle()
                V.did(dve.tensor_reduce(rt[:, 0:16], scr.rearrange("p t (h c) -> p (t h) c", h=4), AX.X, ALU.add))
                V.settle()
                dve.tensor_scalar(rt[:, 0:16], rt[:, 0:16], 1e-12, None, ALU.max).then_inc(S("kk_ss"), 1)
                dve.wait_ge(S("kk_rs"), l + 1)
                dve.tensor_tensor(hs, hs, bc(rt[:, 0:16].unsqueeze(2), P, 16, 64), ALU.mult).then_inc(S("kk_ready"), 1)
                for g, (chunks, _m, width, gains) in enumerate(NORMS):
                    cc = norm_cols(l, g)
                    dve.wait_ge(S("qk_rs"), len(NORMS) * l + g + 1)
                    if g == 6:
                        dve.wait_ge(S("qk_norm"), len(NORMS) * l + g)
                    for n, (c, gcol) in enumerate(zip(chunks, gains)):
                        to = zT[:, c, cc] if g < 5 else rtmp[:, n % 2, cc]
                        ins = dve.scalar_tensor_tensor(out=to, in0=zT[:, c, cc], scalar=vec[:, gcol:gcol + 1],
                                                       in1=rsb[:, g % 2, cc], op0=ALU.mult, op1=ALU.mult)
                        if g >= 5:
                            V.did(ins)
                            V.settle()
                            V.did(dve.tensor_copy(z16[c][:, 0, cc], to))
                            V.settle()
                            ins = dve.tensor_tensor(z16[c][:, 1, cc], to, z16[c][:, 0, cc], ALU.subtract)
                            if n < len(chunks) - 1:
                                V.did(ins)
                                V.settle()
                    ins.then_inc(S("qk_norm"), 1)
                dve.wait_ge(S("qk_norm"), len(NORMS) * (l + 1))
                lows(4 * 3)
                for i, (x, kind) in enumerate(rotations(l)):
                    if i == 6:
                        dve.wait_ge(S("rot"), 10 * l + 6)
                        for h in range(4):
                            lows(2)
                            dve.wait_ge(S("uk_mm"), 4 * l + h + 1)
                            dve.scalar_tensor_tensor(out=mid[:, 4 + h, :], in0=bank[4 + h % 2], scalar=UNSCALE, in1=zT[:, Z_KR, :],
                                                     op0=ALU.mult, op1=ALU.add).then_inc(S("uk_ev"), 1)
                        lows(4)
                    dve.wait_ge(S("rot_mm"), 10 * l + i + 1)
                    r = rtmp[:, i % 2, 0:SEQ]
                    if i >= 2:
                        dve.wait_ge(S("rot"), 10 * l + i - 1)
                    V.did(dve.tensor_tensor(r, bank[2 + i % 2][:, 0:SEQ], rope(2 * kind + 1), ALU.mult))
                    V.did(dve.tensor_tensor(x, x, rope(2 * kind), ALU.mult))
                    V.settle()
                    dve.tensor_tensor(x, x, r, ALU.add).then_inc(S("rot"), 1)
                dve.wait_ge(S("rot"), 10 * (l + 1))
                base, U = sum(len(units(i)) for i in range(l)), units(l)
                for step in range(len(U) + 4):
                    u = step
                    if u < len(U):
                        tt, h = U[u]
                        s3, n = u % 3, unit_keys(tt)
                        src = scores(u)
                        dve.wait_ge(S("s_mm"), base + u + 1)
                        if u >= 3:
                            dve.wait_ge(S("exp"), base + u - 2)
                        nm = nmax[:, s3:s3 + 1]
                        if 8 <= h < 12 and n == TOK:
                            if u >= 3:
                                dve.wait_ge(S("pt_mm"), base + u - 2)
                            dve.wait_ge(S("bias_in"), 16 * 16 * (l + 1))
                            V.did(dve.scalar_tensor_tensor(out=prob[:, s3, CTX:TOK], in0=src[:, CTX:TOK], scalar=unit_scale(h),
                                                           in1=bias[:, tt - T_LAT, h - 8, :], op0=ALU.mult, op1=ALU.add))
                            V.did(dve.tensor_scalar(prob[:, s3, 0:CTX], src[:, 0:CTX], unit_scale(h), None, ALU.mult))
                            V.settle()
                            dve.tensor_reduce(nm, prob[:, s3, 0:n], AX.X, ALU.max, negate=True).then_inc(S("smax"), 1)
                        else:
                            V.did(dve.tensor_reduce(bmax[:, s3:s3 + 1], src[:, 0:n], AX.X, ALU.max))
                            V.settle()
                            dve.tensor_scalar(nm, bmax[:, s3:s3 + 1], -unit_scale(h), None, ALU.mult).then_inc(S("smax"), 1)
                    u = step - 1
                    if 0 <= u < len(U):
                        s3 = u % 3
                        dve.wait_ge(S("exp"), base + u + 1)
                        V.did(dve.reciprocal(rinv[:, s3:s3 + 1], rsum[:, s3:s3 + 1]))
                        V.settle()
                        if u >= 3:
                            dve.wait_ge(S("pt_mm"), base + u - 2)
                        dve.tensor_scalar(diag[:, s3], ident, rinv[:, s3:s3 + 1], None, ALU.mult).then_inc(S("diag"), 1)
                    u = step - 4
                    if u >= 0:
                        rows_, chunk, cols = unit_out(*U[u])
                        dve.wait_ge(S("o_hi"), base + u + 1)
                        dve.tensor_tensor(y16[rows_, 1, chunk, cols], attended(u)[rows_, 0:P], y16[rows_, 0, chunk, cols],
                                          ALU.subtract).then_inc(S("o_ev"), 1)
                V.did(dve.memset(yr, 0.0))
                dve.memset(state[:, 0], 0.0).then_inc(S("st"), 1)
                o3 = oo.rearrange("p (u c) -> p u c", u=8)
                o2 = oo.rearrange("p (d c) -> p d c", d=2)
                t13 = t1.rearrange("p d (h c) -> p (d h) c", h=4)

                def rates(j):
                    rr = l * ROUNDS + j
                    for n, (dst, row) in enumerate(((sw, B_W0), (aa, B_A0))):
                        dve.wait_ge(S("w_mm"), 2 * rr + n + 1)
                        for d in range(2):
                            ins = dve.tensor_tensor(dst[:, d], bank[RATE_BANKS[2 * n + d]][:, 0:256], rows[:, row + 256 * d:row + 256 * d + 256], ALU.add)
                        ins.then_inc(S("w_pre"), 1)

                def keys(j):
                    rr = l * ROUNDS + j
                    dve.wait_ge(S("w_sig"), 2 * rr + 2)
                    if rr:
                        dve.wait_ge(S("prod_end"), rr)
                    V.did(dve.scalar_tensor_tensor(out=kd, in0=aa, scalar=-1.0, in1=bc(rows[:, B_KA:B_KA + 256].unsqueeze(1), P, 2, 256),
                                                   op0=ALU.add, op1=ALU.mult))
                    for d in range(2):
                        V.did(dve.tensor_tensor(bb[:, d], kk[:, RW_ORDER[d][j]], aa[:, d], ALU.mult))
                    V.settle()
                    for d in range(2):
                        V.did(dve.scalar_tensor_tensor(out=kd[:, d], in0=kd[:, d], scalar=1.0, in1=rkv[:, RW_ORDER[d][j], 256:512],
                                                       op0=ALU.add, op1=ALU.mult))
                    V.settle()

                def bonus_of(j):
                    for d in range(2):
                        V.did(dve.tensor_tensor(t2[:, d], rkv[:, RW_ORDER[d][j], 0:256], kd[:, d], ALU.mult))
                    V.settle()
                    V.did(dve.tensor_tensor(t2, t2, bc(rows[:, B_RK:B_RK + 256].unsqueeze(1), P, 2, 256), ALU.mult))
                    V.settle()
                    V.did(dve.tensor_reduce(bonus, t2.rearrange("p d (h c) -> p (d h) c", h=4), AX.X, ALU.add))
                    V.settle()

                def readout(j, part):
                    no = out_rounds_before(l, j)
                    if part == 0:
                        dve.wait_ge(S("o_read"), 2 * (no + 1))
                        V.did(dve.tensor_reduce(rt[:, 24:32], o3, AX.X, ALU.add))
                        V.settle()
                        V.did(dve.scalar_tensor_tensor(out=o3, in0=bc(rt[:, 24:32].unsqueeze(2), P, 8, 64), scalar=-1.0 / HEAD, in1=o3,
                                                       op0=ALU.mult, op1=ALU.add))
                        V.settle()
                    elif part == 1:
                        V.did(dve.tensor_tensor(t13, o3, o3, ALU.mult))
                        V.settle()
                        dve.tensor_reduce(rt[:, 16:24], t13, AX.X, ALU.add).then_inc(S("o_var"), 1)
                    elif part == 2:
                        dve.wait_ge(S("o_rs"), no + 1)
                        V.did(dve.tensor_tensor(o3, o3, bc(rt[:, 16:24].unsqueeze(2), P, 8, 64), ALU.mult))
                        V.settle()
                        V.did(dve.tensor_tensor(o2, o2, bc(rows[:, B_LNW:B_LNW + 256].unsqueeze(1), P, 2, 256), ALU.mult))
                        for d in range(2):
                            V.did(dve.tensor_tensor(t2[:, d].rearrange("p (h c) -> p h c", h=4),
                                                    rkv[:, RW_ORDER[d][j], 512:768].rearrange("p (h c) -> p h c", h=4),
                                                    bc(bonus[:, 4 * d:4 * d + 4].unsqueeze(2), P, 4, 64), ALU.mult))
                        V.settle()
                    elif part == 3:
                        V.did(dve.tensor_tensor(o2, o2, bc(rows[:, B_LNB:B_LNB + 256].unsqueeze(1), P, 2, 256), ALU.add))
                        V.settle()
                        V.did(dve.tensor_tensor(o2, o2, t2, ALU.add))
                        V.settle()
                        dve.wait_ge(S("g_mm"), no + 1)
                        for d in range(2):
                            ins = dve.tensor_tensor(o2[:, d], o2[:, d], bank[d][:, 0:256], ALU.mult)
                        ins.then_inc(S("g_read"), 1)
                    else:
                        dve.wait_ge(S("g_read"), no + 1)
                        for d in range(2):
                            tile = RW_ORDER[d][j]
                            ins = dve.tensor_tensor(yr[:, tile], yr[:, tile], o2[:, d], ALU.add)
                        ins.then_inc(S("yr"), 1)
                        dve.wait_ge(S("yr"), no + 1)

                for j in range(ROUNDS):
                    rr = l * ROUNDS + j
                    tau = [RW_ORDER[d][j] for d in range(2)]
                    out = RW_ORDER[0][j] in qtiles(l)
                    if j == 0:
                        rates(j)
                        keys(j)
                    dve.wait_ge(S("decays"), 5 * (rr + 1))
                    for d in range(2):
                        dve.tensor_tensor(eX[:, d], eX[:, d], kk[:, tau[d]], ALU.mult)
                        dve.tensor_tensor(eL[:, d], eL[:, d], rkv[:, tau[d], 0:256], ALU.mult)
                        dve.tensor_tensor(Bd[:, d], bb[:, d], eN[:, d], ALU.mult)
                        dve.tensor_tensor(eN[:, d], eN[:, d], kd[:, d], ALU.mult).then_inc(S("prod"), 1)
                    dve.tensor_tensor(Be, bb, eA, ALU.mult)
                    dve.tensor_tensor(eA, eA, kd, ALU.mult).then_inc(S("prod_end"), 1)
                    for i in range(1, RQ, 2):
                        dve.wait_ge(S("fm_tr"), RQ * rr + i + 1)
                        dve.tensor_copy(fmt[:, i], bank[i].rearrange("p (a t) -> p a t", a=4)).then_inc(S("fm_d"), 1)
                    for u in range(8):
                        d = u // 4
                        dve.wait_ge(S("a_mm"), 8 * rr + u + 1)
                        m2 = cst[:, C_TRI + 256 * d:C_TRI + 256 * d + 256]
                        dve.tensor_tensor(am[:, u].rearrange("p (x a) t -> p x (a t)", x=2), bank[4 + u % 4].rearrange("p (x t) -> p x t", x=2),
                                          bc(m2.unsqueeze(1), P, 2, 256), ALU.mult).then_inc(S("am_done"), 1)
                        if u % 4 == 3:
                            dve.wait_ge(S("am_done"), 8 * rr + u + 1)
                            half = slice(4 * d, 4 * d + 4)
                            V.did(dve.scalar_tensor_tensor(out=TT[:, half], in0=am[:, half, 0, :], scalar=-1.0,
                                                           in1=bc(level(0).unsqueeze(1), P, 4, P), op0=ALU.mult, op1=ALU.mult))
                            V.settle()
                            dve.tensor_tensor(TT[:, half], TT[:, half], bc(ident.unsqueeze(1), P, 4, P), ALU.add).then_inc(S("tt0"), 1)
                    dve.wait_ge(S("t_ev"), 2 * (rr + 1))
                    for lev in range(1, LEVELS):
                        for d in range(2):
                            half = slice(4 * d, 4 * d + 4)
                            dve.wait_ge(S("yt_mm"), 10 * rr + 2 * (lev - 1) + d + 1)
                            if lev > 1:
                                dve.wait_ge(S("inv"), 10 * rr + 2 * (lev - 2) + d + 1)
                            else:
                                dve.wait_ge(S("tt0"), 2 * rr + d + 1)
                            if lev < LEVELS - 1:
                                dve.tensor_tensor(Tm[:, half], Tm[:, half], bank[4 + d].rearrange("p (u t) -> p u t", u=4), ALU.subtract)
                            dve.tensor_tensor(TT[:, half], TT[:, half], bank[6 + d].rearrange("p (u t) -> p u t", u=4),
                                              ALU.subtract).then_inc(S("inv"), 1)
                        if j and has_out(l, j - 1) and lev < LEVELS - 1:
                            readout(j - 1, lev - 1)
                    if j < ROUNDS - 1:
                        rates(j + 1)
                    dve.wait_ge(S("m1_mm"), rr + 1)
                    dve.tensor_tensor(m1, bank[4].rearrange("p (q t) -> p q t", q=4), fmt[:, :, 1, :], ALU.add).then_inc(S("m1"), 1)
                    if j and has_out(l, j - 1):
                        readout(j - 1, LEVELS - 2)
                    if out:
                        bonus_of(j)
                    if j < ROUNDS - 1:
                        keys(j + 1)
                    dve.wait_ge(S("g0_ev"), 2 * (rr + 1))
                    for s in range(2):
                        dve.wait_ge(S("st"), 2 * rr + s + l + 1)
                        new = state[:, (2 * j + s + 1) % 3]
                        for qq in range(RQ):
                            c = CHUNK_ORDER[qq // 2][s]
                            V.did(dve.scalar_tensor_tensor(out=new[:, qq], in0=state[:, (2 * j + s) % 3, qq],
                                                           scalar=ecol[:, 2 * qq + c:2 * qq + c + 1],
                                                           in1=h0[:, c, qq], op0=ALU.mult, op1=ALU.add))
                        V.settle()
                        dve.wait_ge(S("st_mm"), 2 * rr + s + 1)
                        dve.tensor_tensor(new, new, bank[6][:, 256 * s:256 * s + 256].rearrange("p (q v) -> p q v", q=4),
                                          ALU.add).then_inc(S("st"), 1)
                for part in range(5):
                    readout(ROUNDS - 1, part)
                for i, tt in enumerate(qtiles(l)):
                    dve.wait_ge(S("yr_hi"), TILES * l + i + 1)
                    c = slice(tt * P, (tt + 1) * P)
                    dve.tensor_tensor(y16[:, 1, 6:8, c], bank[i % 2][:, 0:256].rearrange("p (k t) -> p k t", k=2), y16[:, 0, 6:8, c],
                                      ALU.subtract).then_inc(S("yr_ev"), 1)
                for i in range(4 * KD):
                    m, br = divmod(i, 4)
                    gi = 4 * KD * l + i
                    lows(KD)
                    lows(BRANCH_CHUNKS[br])
                    dve.wait_ge(S("gate"), gi + 1)
                    dve.wait_ge(S("br_mm"), gi + 1)
                    dst = merged[:, m, q] if br == 0 else prod[:, i % 2, 0:w]
                    if br == 1 and KD * l + m:
                        dve.wait_ge(S("merged"), KD * l + m)
                    dve.scalar_tensor_tensor(out=dst, in0=bank[2 + i % 2][:, 0:w], scalar=UNSCALE, in1=gate_sb[:, i % 2, 0:w],
                                             op0=ALU.mult, op1=ALU.mult).then_inc(S("gated"), 1)
                    if br:
                        dve.wait_ge(S("gated"), gi + 1)
                        ins = dve.tensor_tensor(merged[:, m, q], merged[:, m, q], dst, ALU.add)
                        V.did(ins)
                        V.settle()
                        if br == 3:
                            V.did(dve.tensor_copy(m16[:, 0, m, q], merged[:, m, q]))
                            V.settle()
                            dve.tensor_tensor(m16[:, 1, m, q], merged[:, m, q], m16[:, 0, m, q], ALU.subtract).then_inc(S("merged"), 1)
                residual(dve, V, lows, l, 0)
                dve.wait_ge(S("nb_rstd"), l + 1)
                modulated(2, 3, segs(l)).then_inc(S("hb"), 1)
                if l % 2 == 0:
                    for j in range(FFC):
                        lows(2 * KD)
                        dve.wait_ge(S("silu"), j + 1)
                        dve.wait_ge(S("fu_mm"), j + 1)
                        if j >= 2:
                            dve.wait_ge(S("hid"), j - 1)
                        V.did(dve.scalar_tensor_tensor(out=prod[:, j % 2, 0:w], in0=bank[2 + j % 2][:, 0:w], scalar=UNSCALE,
                                                       in1=gate_sb[:, j % 2, 0:w], op0=ALU.mult, op1=ALU.mult))
                        V.settle()
                        V.did(dve.tensor_copy(hid[:, 0, j, q], prod[:, j % 2, 0:w]))
                        V.settle()
                        dve.tensor_tensor(hid[:, 1, j, q], prod[:, j % 2, 0:w], hid[:, 0, j, q], ALU.subtract).then_inc(S("hid"), 1)
                else:
                    dve.wait_ge(S("r_mm"), 1)
                    dve.wait_ge(S("wr_in"), 16)
                    lg = rt[:, 32:48].rearrange("p (i e) -> p i e", i=2)
                    V.did(dve.scalar_tensor_tensor(out=lg, in0=bank[0][:, 0:16].rearrange("p (i e) -> p i e", i=2), scalar=UNSCALE,
                                                   in1=bc(wrt[:, 64:72].unsqueeze(1), P, 2, EXPERTS), op0=ALU.mult, op1=ALU.add))
                    V.settle()
                    dve.tensor_reduce(rt[:, 48:50], lg, AX.X, ALU.max, negate=True).then_inc(S("r_max"), 1)
                    dve.wait_ge(S("r_exp"), 2)
                    V.did(dve.tensor_reduce(rt[:, 50:52], lg, AX.X, ALU.add))
                    V.settle()
                    V.did(dve.reciprocal(rt[:, 50:52], rt[:, 50:52]))
                    V.settle()
                    V.did(dve.tensor_tensor(lg, lg, bc(rt[:, 50:52].unsqueeze(2), P, 2, EXPERTS), ALU.mult))
                    V.settle()
                    for i in range(2):
                        pi = lg[:, i, :].unsqueeze(2).broadcast_to([P, 8, 8])
                        pj = lg[:, i, :].unsqueeze(1).broadcast_to([P, 8, 8])
                        gt = prod[:, 0, 64 * i:64 * i + 64].rearrange("p (i j) -> p i j", i=8)
                        eq = prod[:, 1, 64 * i:64 * i + 64].rearrange("p (i j) -> p i j", i=8)
                        V.did(dve.tensor_tensor(gt, pj, pi, ALU.is_gt))
                        V.did(dve.tensor_tensor(eq, pj, pi, ALU.is_equal))
                        V.settle()
                        V.did(dve.tensor_tensor(eq, eq, cst[:, C_LOW:C_LOW + 64].rearrange("p (i j) -> p i j", i=8), ALU.mult))
                        V.settle()
                        V.did(dve.tensor_tensor(gt, gt, eq, ALU.add))
                        V.settle()
                        V.did(dve.tensor_reduce(rt[:, 64 + 8 * i:72 + 8 * i], gt, AX.X, ALU.add))
                    V.settle()
                    cm = rt[:, 64:80]
                    V.did(dve.tensor_scalar(cm, cm, 1.5, None, ALU.is_lt))
                    V.settle()
                    V.did(dve.tensor_tensor(cm, cm, rt[:, 32:48], ALU.mult))
                    V.settle()
                    V.did(dve.tensor_reduce(rt[:, 50:52], cm.rearrange("p (i e) -> p i e", i=2), AX.X, ALU.add))
                    V.settle()
                    V.did(dve.reciprocal(rt[:, 50:52], rt[:, 50:52]))
                    V.settle()
                    dve.tensor_tensor(cm.rearrange("p (i e) -> p i e", i=2), cm.rearrange("p (i e) -> p i e", i=2),
                                      bc(rt[:, 50:52].unsqueeze(2), P, 2, EXPERTS), ALU.mult).then_inc(S("comb"), 1)
                    dve.wait_ge(S("cw_ev"), 4)
                    dve.wait_ge(S("comb"), 1)
                    for e in range(EXPERTS):
                        for j in range(EFC):
                            i = e * EFC + j
                            lows(2 * KD)
                            dve.wait_ge(S("esilu"), i + 1)
                            dve.wait_ge(S("eu_mm"), i + 1)
                            if j == 0 and e >= 2:
                                dve.wait_ge(S("edown"), e - 1)
                            if i >= 2:
                                dve.wait_ge(S("ehid"), i - 1)
                            p = prod[:, i % 2, 0:w]
                            V.did(dve.scalar_tensor_tensor(out=p, in0=bank[2 + i % 2][:, 0:w], scalar=UNSCALE, in1=gate_sb[:, i % 2, 0:w],
                                                           op0=ALU.mult, op1=ALU.mult))
                            V.settle()
                            V.did(dve.tensor_tensor(p, p, cw[:, e, :], ALU.mult))
                            V.settle()
                            V.did(dve.tensor_copy(ehid[:, e % 2, 0, j, :], p))
                            V.settle()
                            dve.tensor_tensor(ehid[:, e % 2, 1, j, :], p, ehid[:, e % 2, 0, j, :], ALU.subtract).then_inc(S("ehid"), 1)
                        if e < EXPERTS - 1:
                            lows(EFC * KD)
                residual(dve, V, lows, l, 1)


def constants():
    c = np.zeros((P, C_COLS), np.float32)
    i = np.arange(P)
    c[:, C_ID:C_ID + P] = np.eye(P)
    c[:, C_ONES:C_ONES + P] = 1
    c[:, C_BLK:C_BLK + P] = i[:, None] // HEAD == i[None, :] // HEAD
    for first, half in ((0, 32), (HEAD, 32)):
        for m in range(half):
            c[first + m + half, C_ROT + first + m] = -1
            c[first + m, C_ROT + first + m + half] = 1
    for m in range(16):
        c[HEAD + m + 16, C_ROTM + HEAD + m] = -1
        c[HEAD + m, C_ROTM + HEAD + m + 16] = 1
    same = i[:, None] // CHUNK == i[None, :] // CHUNK
    s, t = i[:, None], i[None, :]
    for n, m in enumerate((s < t, s <= t, s > t, s >= t)):
        c[:, C_TRI + n * P:C_TRI + (n + 1) * P] = m & same
    for lev in range(LEVELS):
        b = 1 << lev
        c[:, C_LEV + lev * P:C_LEV + (lev + 1) * P] = (s // (2 * b) == t // (2 * b)) & (s // b != t // b)
    pos = np.arange(SEQ)
    for kind, rot in enumerate((HEAD, 32)):
        pairs = rot // 4
        inv = (np.float32(10000.0) ** (-np.arange(pairs, dtype=np.float32) / np.float32(pairs))).astype(np.float32)
        ang = np.concatenate([(pos // GRID_W).astype(np.float32)[:, None] * inv, (pos % GRID_W).astype(np.float32)[:, None] * inv], 1)
        cos, sin = np.ones((P, SEQ), np.float32), np.zeros((P, SEQ), np.float32)
        for first in ((0, HEAD) if kind == 0 else (HEAD,)):
            for r in range(rot):
                cos[first + r] = np.cos(ang[:, r % (rot // 2)])
                sin[first + r] = np.sin(ang[:, r % (rot // 2)])
        c[:, C_ROPE + 2 * kind * SEQ:C_ROPE + (2 * kind + 1) * SEQ] = cos
        c[:, C_ROPE + (2 * kind + 1) * SEQ:C_ROPE + (2 * kind + 2) * SEQ] = sin
    c[:, C_EPS] = NORM_EPS
    c[:, C_EPS + 1] = GN_EPS
    for r in range(4):
        c[r, C_FOLD + r % 2] = 1
    e = np.arange(EXPERTS)
    c[:, C_LOW:C_LOW + 64] = (e[None, :] < e[:, None]).astype(np.float32).reshape(1, 64)
    sel = np.zeros((32, GRID_W * GRID_W), np.float32)
    for qc in range(GRID_W):
        start = min(max(qc - 8, 0), GRID_W - 16)
        for kc in range(GRID_W):
            if start <= kc < start + 16:
                sel[kc - qc + 15, qc * GRID_W + kc] = 1
            else:
                sel[31, qc * GRID_W + kc] = NEG
    return c, sel


def cut_blocks(w):
    r, c = w.shape
    return w.reshape(r // P, P, c // P, P).transpose(0, 2, 1, 3)


def by_output(w):
    b = cut_blocks(w)
    return b.transpose(1, 0, 2, 3).reshape(-1, P, P)


def columns(v):
    return np.ascontiguousarray(np.asarray(v).reshape(-1, P).T)


def padded(w, c):
    out = np.zeros((w.shape[0], c), w.dtype)
    out[:, :w.shape[1]] = w
    return out


def lay_out(i):
    i = {k: np.asarray(v) for k, v in i.items()}
    blocks, vecs, muxs, rows, lora2s, lws, rpbs = [], [], [], [], [], [], []
    for l in range(DEPTH):
        blocks.append(cut_blocks(i["w_mod"][l]).reshape(KD, 6, KD, P, P).transpose(1, 0, 2, 3, 4).reshape(-1, P, P))
        w = i["w_in"][l]
        o = np.cumsum([0, 512, 128, 128, 256, 256, 256, 256, 256, 256, 384, 256, 32, 4096])
        part = [w[:, o[n]:o[n + 1]] for n in range(13)]
        heads = part[0].reshape(D, 8, HEAD)[:, [0, 4, 1, 5, 2, 6, 3, 7]].reshape(D, 512)
        kr = np.zeros((D, P), np.float32)
        kr[:, HEAD:HEAD + 32] = part[11]
        blocks.append(by_output(np.concatenate([heads, part[1], part[3], part[4], part[6], part[7], part[8], part[9], part[10], kr], 1)))
        blocks.append(by_output(np.concatenate([part[2], part[5]], 1)))
        uq = i["mla_w_uq"][l].reshape(384, 4, 96)
        blocks.append(by_output(np.concatenate([padded(uq[:, h], P) for h in range(4)], 1)))
        ukv = i["mla_w_ukv"][l].reshape(256, 4, 128)
        blocks.append(by_output(np.concatenate([padded(ukv[:, h, :64], P) for h in range(4)], 1)))
        blocks.append(by_output(np.ascontiguousarray(ukv[:, :, 64:]).reshape(256, 256)))
        gates, br = cut_blocks(part[12]), cut_blocks(i["w_branch"][l])
        for m in range(KD):
            for b in range(4):
                blocks.append(gates[:, b * KD + m])
                blocks.append(br[BRANCH_FIRST[b]:BRANCH_FIRST[b] + BRANCH_CHUNKS[b], m])
        blocks.append(by_output(i["w_out"][l]))
        if l % 2 == 0:
            g, u, d = (i[n][l // 2] for n in ("ffn_w_gate", "ffn_w_up", "ffn_w_down"))
            g, u = cut_blocks(g), cut_blocks(u)
            for j in range(FFC):
                blocks += [g[:, j], u[:, j]]
            blocks.append(by_output(d))
        else:
            for e in range(EXPERTS):
                g, u, d = (i[n][l // 2][e] for n in ("moe_w_gate", "moe_w_up", "moe_w_down"))
                g, u = cut_blocks(g), cut_blocks(u)
                for j in range(EFC):
                    blocks += [g[:, j], u[:, j]]
                blocks.append(by_output(d))
        two = lambda v: np.concatenate([v, v])
        vecs.append(np.concatenate([columns(i[n][l]) for n in ("b_mod", "norm_mix_pre", "norm_mix_post", "norm_ffn_pre", "norm_ffn_post")]
                                   + [columns(i["rwkv_mu_p"][l].reshape(-1)), columns(two(i["gqa_q_norm"][l])), columns(two(i["gqa_k_norm"][l])),
                                      columns(i["mla_q_norm"][l]), columns(i["mla_kv_norm"][l])], 1))
        muxs.append(columns(i["rwkv_mu_x"][l].reshape(-1)))
        rows.append(np.concatenate([i[n][l].reshape(-1) for n in ("rwkv_w0", "rwkv_a0", "rwkv_k_k", "rwkv_k_a", "rwkv_r_k", "rwkv_ln_w", "rwkv_ln_b")]))
        lora2s.append(np.concatenate([np.concatenate([i["rwkv_w2"][l].reshape(64, 256), i["rwkv_a2"][l].reshape(64, 256)]),
                                      i["rwkv_g2"][l].reshape(128, 256)], 1))
        one = np.concatenate([i["rwkv_w1"][l][0], i["rwkv_w1"][l][1], i["rwkv_a1"][l][0], i["rwkv_a1"][l][1]], 1)
        two_ = np.concatenate([i["rwkv_g1"][l][0], i["rwkv_g1"][l][1]], 1)
        lws.append(np.stack([x.reshape(KD, P, P).transpose(1, 0, 2) for x in (one, two_)], 1))
        r = i["na_rpb"][l][:, 8 - GRID_H:7 + GRID_H]
        rpbs.append(r.reshape(-1, NA_COLS).T)
    blocks = np.concatenate(blocks)
    slabs = np.ascontiguousarray(blocks.reshape(-1, SLAB, P, P).transpose(0, 2, 1, 3))
    rpb = np.concatenate([np.concatenate(rpbs, 1), np.ones((1, 56), np.float32)])
    cst, sel = constants()
    fm = np.concatenate([i["ctx"][0], i["x"][0]]).T.reshape(KD, P, TOK).transpose(1, 0, 2)
    c2 = np.stack([columns(i["c"][0]), columns(i["c_ctx"])], 2)
    wr = np.concatenate([i["moe_w_router"][0].reshape(KD, P, EXPERTS).transpose(1, 0, 2).reshape(P, KD * EXPERTS),
                         np.tile(i["moe_b_router"][0][None, :], (P, 1))], 1)
    return {"w": slabs, "vec": np.concatenate(vecs, 1), "mux": np.stack(muxs), "rows": np.stack(rows), "lora2": np.stack(lora2s), "lw": np.stack(lws),
            "rpb": rpb, "sel": sel, "cst": cst, "x": fm, "c2": c2, "wr": wr}


def program(nc, arrays):
    t = {name: nc.dram_tensor(f"in_{name}", a.shape, mybir.dt.from_np(a.dtype), kind="ExternalInput").ap() for name, a in arrays.items()}
    t["scratch"] = nc.dram_tensor("rel_bias", [DEPTH * 4 * 7, GRID_W * GRID_W], F32, kind="Internal").ap()
    t["out"] = nc.dram_tensor("out_0", [P, KD, SEQ], F32, kind="ExternalOutput").ap()
    build(nc, t)


def kernel(**inputs):
    import concourse.bacc as bacc
    from concourse.bass_utils import run_bass_kernel_spmd as run

    nc = bacc.Bacc("TRN2", target_bir_lowering=False, num_devices=1)
    arrays = {name: np.ascontiguousarray(a) for name, a in lay_out(inputs).items()}
    program(nc, arrays)
    r = run(nc, [{f"in_{name}": a for name, a in arrays.items()}], core_ids=[0])
    got = r.results[0]["out_0"]
    return np.ascontiguousarray(got.transpose(2, 1, 0).reshape(1, SEQ, D))
```

```python
import math
from contextlib import ExitStack

import numpy as np
import concourse.bass as bass
from concourse import mybir

F32 = mybir.dt.float32
F16 = mybir.dt.float16
ALU = mybir.AluOpType
ACT = mybir.ActivationFunctionType
AX = mybir.AxisListType

P = 128
D = 1024
SEQ = 256
CTX = 256
TOK = CTX + SEQ
DEPTH = 2
GRID_W = 64
GRID_H = SEQ // GRID_W
KD = D // P
TILES = TOK // P
HEAD = 64
NORM_EPS = 1e-6
GN_EPS = 64e-5
FF = 2816
FFC = FF // P
EXPERTS = 8
EFF = 1408
EFC = EFF // P
CHUNK = 64
LEVELS = 6
DECAY = math.exp(-0.5)
NA_ROWS = 2 * 8 - 1
NA_COLS = 2 * 16 - 1
NEG = -1e30

BRANCH_CHUNKS = (4, 2, 2, 2)
BRANCH_FIRST = (0, 4, 6, 8)

Z_Q, Z_K, Z_NQ, Z_NK, Z_R, Z_RK, Z_RV, Z_LMU, Z_CQ, Z_CKV, Z_KR = 0, 4, 5, 7, 9, 11, 13, 15, 17, 20, 22
Z_CHUNKS = 23
Z_STREAM = ([(Z_Q + i, True) for i in range(4)] + [(Z_K, False)]
            + [(Z_NQ + i, True) for i in range(2)] + [(Z_NK + i, False) for i in range(2)]
            + [(Z_CQ + i, True) for i in range(3)] + [(Z_CKV + i, False) for i in range(2)] + [(Z_KR, False)]
            + [(Z_R + i, False) for i in range(6)])
NORM_STEP = (1, 3, 5, 7, 9, 13, 15)
ROT_STEP = (5, 7, 9, 11, 13, 17)

SLAB = 8
RING = 4
PARTS = 4
WSCALE = 64.0
UNSCALE = 1.0 / WSCALE
MOD_SLABS = 6 * KD
Z_SLABS = len(Z_STREAM)
Z_EVEN, Z_ODD = (Z_SLABS + 5) // 2, (Z_SLABS + 4) // 2
V_SLABS = 3
MLA_SLABS = 3
MERGE_SLABS = (4 * KD * KD + 10 * KD) // SLAB
OUT_SLABS = KD
FFN_SLABS = 2 * FFC + FFC * KD // SLAB
MOE_SLABS = EXPERTS * (2 * EFC + EFC * KD // SLAB)
MOD_FIRST = 2
MOD_BESIDE = 2
MOD_PERIOD = KD // MOD_BESIDE
MOD_STEPS = (6 - MOD_FIRST) * MOD_PERIOD
SLABS = sum(MOD_SLABS + Z_SLABS + V_SLABS + MLA_SLABS + MERGE_SLABS + OUT_SLABS + (FFN_SLABS, MOE_SLABS)[_l] for _l in range(DEPTH))

V_BMOD, V_NMPRE, V_NMPOST, V_NFPRE, V_NFPOST = 0, 48, 56, 64, 72
V_MUP, V_QG, V_KG, V_MQ, V_MKV = 80, 86, 87, 88, 91
V_COLS = 93
B_W0, B_A0, B_KK, B_KA, B_RK, B_LNW, B_LNB = 0, 512, 1024, 1280, 1536, 1792, 2048
B_COLS = 2304
C_ID, C_ONES, C_BLK, C_ROT, C_ROTM, C_TRI, C_LEV, C_ROPE, C_EPS, C_LOW, C_FOLD = 0, 128, 256, 384, 512, 640, 1152, 1920, 2944, 2946, 3010
C_COLS = 3012

RW_ORDER = ((0, 1, 2, 3), (1, 0, 3, 2))
CHUNK_ORDER = ((0, 1), (1, 0))


class Steps:

    def __init__(self, eng, sem):
        self.eng, self.sem, self.n = eng, sem, 0

    def did(self, ins):
        ins.then_inc(self.sem, 1)
        self.n += 1
        return ins

    def settle(self):
        if self.n:
            self.eng.wait_ge(self.sem, self.n)


def build(nc, t):
    ctx = ExitStack()
    with ctx:
        def sb(name, cols, dt=F32):
            return ctx.enter_context(nc.sbuf_tensor(name, [P, cols], dt))

        sems = {}

        def S(name):
            if name not in sems:
                sems[name] = ctx.enter_context(nc.semaphore(name))
            return sems[name]

        xT = sb("xT", KD * TOK)[:, :].rearrange("p (k t) -> p k t", k=KD)
        h16 = sb("h16", 2 * KD * TOK, F16)[:, :].rearrange("p (x k t) -> p x k t", x=2, k=KD)
        ring = sb("ring", RING * SLAB * P)[:, :].rearrange("p (r b c) -> p r b c", r=RING, b=SLAB)
        parts = sb("parts", 2 * PARTS * SLAB * P, F16)[:, :].rearrange("p (r x b c) -> p r x b c", r=PARTS, x=2, b=SLAB)
        yflat = sb("yT", 10 * TOK)[:, :]
        y16 = yflat.bitcast(F16).rearrange("p (x k t) -> p x k t", x=2, k=10)
        arena = sb("arena", Z_CHUNKS * TOK + KD * TOK + TILES * 640)[:, :]
        rkv = sb("rkv", TILES * 768)[:, :].rearrange("p (t c) -> p t c", t=TILES)
        kk = sb("kk", TILES * 256)[:, :].rearrange("p (t c) -> p t c", t=TILES)
        state = sb("state", 3 * 256)[:, :].rearrange("p (s j v) -> p s j v", s=3, j=4)
        lor = sb("lor", 2 * TOK)[:, :].rearrange("p (k t) -> p k t", k=2)
        yr = [yflat[:, c:c + 256] for c in (6 * 256, 7 * 256, 16 * 256, 17 * 256)]
        rows = sb("rows", B_COLS)[:, :]
        lora2 = sb("lora2", 512)[:, :]
        cst = sb("cst", C_COLS)[:, :]
        vecs = sb("vec", DEPTH * V_COLS)[:, :].rearrange("p (l c) -> p l c", l=DEPTH)
        mux = sb("mux", 3 * KD)[:, :]
        wrt = sb("wrt", KD * EXPERTS + EXPERTS)[:, :]
        rstd = sb("rstd", TOK)[:, :]
        scT = sb("scT", KD * 2)[:, :].rearrange("p (k j) -> p k j", j=2)
        sc16 = sb("sc16", KD * 8, F16)[:, :].rearrange("p (k x j) -> p k x j", x=4, j=2)
        mods = sb("mod", DEPTH * 96)[:, :].rearrange("p (l n j) -> p l n j", l=DEPTH, j=2)
        gmods = sb("gmod", DEPTH * 64)[:, :].rearrange("p (l w k j) -> p l w k j", l=DEPTH, w=4, j=2)
        wr16 = sb("wr16", 2 * KD * EXPERTS, F16)[:, :].rearrange("p (x c) -> p x c", x=2)
        small = sb("small", 108)[:, :]
        bank = [ctx.enter_context(nc.psum_tensor(f"bank{i}", [P, 512], F32))[:, :] for i in range(8)]

        ident = cst[:, C_ID:C_ID + P]
        ones = cst[:, C_ONES:C_ONES + P]
        blk = cst[:, C_BLK:C_BLK + P]
        eps_col = cst[:, C_EPS:C_EPS + 1]
        gn_eps_col = cst[:, C_EPS + 1:C_EPS + 2]

        def tri(i):
            return cst[:, C_TRI + i * P:C_TRI + (i + 1) * P]

        def level(i):
            return cst[:, C_LEV + i * P:C_LEV + (i + 1) * P]

        def rope(i):
            return cst[:, C_ROPE + i * SEQ:C_ROPE + (i + 1) * SEQ]

        zT = arena[:, 0:Z_CHUNKS * TOK].rearrange("p (k t) -> p k t", k=Z_CHUNKS)
        MID = Z_CHUNKS * TOK
        mid = arena[:, MID:MID + KD * TOK].rearrange("p (k t) -> p k t", k=KD)
        VT = MID + KD * TOK
        vT = arena[:, VT:VT + TILES * 640].rearrange("p (t c) -> p t c", t=TILES)
        lw = arena[:, MID:MID + 2048].rearrange("p (g k c) -> p g k c", g=2, k=KD)
        lwm = arena[:, MID + 2048:MID + 4096].rearrange("p (g k c) -> p g k c", g=2, k=KD)
        l16 = yflat[:, 0:4096].bitcast(F16).rearrange("p (x s g k c) -> p x s g k c", x=2, s=2, g=2, k=KD)
        wide = arena[:, 0:KD * TOK].rearrange("p (k t) -> p k t", k=KD)
        wider = arena[:, KD * TOK:2 * KD * TOK].rearrange("p (k t) -> p k t", k=KD)
        relrow = arena[:, 4608:4608 + 4096]
        modrow = arena[:, VT:VT + 2 * D].rearrange("p (s c) -> p s c", s=2)
        z16 = [arena[:, c * TOK:(c + 1) * TOK].bitcast(F16).rearrange("p (x t) -> p x t", x=2) for c in range(Z_CHUNKS)]
        sq = arena[:, MID:MID + 6 * TOK].rearrange("p (g k t) -> p g k t", g=2, k=3)
        rsb = arena[:, MID + 6 * TOK:MID + 8 * TOK].rearrange("p (g t) -> p g t", g=2)
        rtmp = yflat[:, 8 * TOK:10 * TOK].rearrange("p (s t) -> p s t", s=2)
        bias = arena[:, Z_R * TOK:Z_R * TOK + 2048].rearrange("p (j h c) -> p j h c", j=2, h=4)
        diag = arena[:, Z_RV * TOK:Z_RV * TOK + 3 * P].rearrange("p (s c) -> p s c", s=3)
        probT = arena[:, Z_LMU * TOK:Z_LMU * TOK + 2 * TOK].rearrange("p (s c) -> p s c", s=2)
        prob = arena[:, Z_CQ * TOK:Z_CQ * TOK + 3 * TOK].rearrange("p (s c) -> p s c", s=3)
        nmax, bmax, rsum, rinv = (small[:, 3 * i:3 * i + 3] for i in range(4))
        rt = small[:, 12:]
        at = [0]

        def cut(n):
            at[0] += n
            return arena[:, at[0] - n:at[0]]

        sw, aa, gg, kd, bb, eL, eN, eX, eA, Bd, Be = (cut(512).rearrange("p (d c) -> p d c", d=2) for _ in range(11))
        fmt_flat = cut(2048)
        fmt = fmt_flat.rearrange("p (q a t) -> p q a t", q=4, a=4)
        am = cut(4096).rearrange("p (u a t) -> p u a t", u=8, a=4)
        ct = cut(2048).rearrange("p (s u t) -> p s u t", s=2, u=8)
        Tm = cut(1024).rearrange("p (u t) -> p u t", u=8)
        TT = cut(1024).rearrange("p (u t) -> p u t", u=8)
        Xs = cut(1024).rearrange("p (u t) -> p u t", u=8)
        m1 = cut(512).rearrange("p (q t) -> p q t", q=4)
        gh = cut(1024).rearrange("p (c x q v) -> p c x q v", c=2, x=2, q=4)
        g0, h0 = gh[:, :, 0], gh[:, :, 1]
        ecol = small[:, 100:108]
        assert at[0] <= VT + TILES * 640
        rhs2, nwu = ct[:, 1], Tm
        RATE_BANKS = (1, 5, 0, 7)
        oo = gg.rearrange("p d c -> p (d c)")
        bonus = rt[:, 80:88]
        t1, t2 = eN, Bd
        merged = arena[:, 0:KD * TOK].rearrange("p (k t) -> p k t", k=KD)
        m16 = arena[:, 2 * KD * TOK:3 * KD * TOK].bitcast(F16).rearrange("p (x k t) -> p x k t", x=2, k=KD)
        yo = arena[:, KD * TOK:2 * KD * TOK].rearrange("p (k t) -> p k t", k=KD)
        gate_sb = vT.rearrange("p t c -> p (t c)")[:, 0:1024].rearrange("p (s t) -> p s t", s=2)
        prod = vT.rearrange("p t c -> p (t c)")[:, 1024:2048].rearrange("p (s t) -> p s t", s=2)
        hid = arena[:, 0:FFC * TOK].bitcast(F16).rearrange("p (x k t) -> p x k t", x=2, k=FFC)
        ehid = arena[:, 0:2 * EFC * SEQ].bitcast(F16).rearrange("p (s x k t) -> p s x k t", s=2, x=2, k=EFC)
        cw = arena[:, 2 * EFC * SEQ:2 * EFC * SEQ + EXPERTS * SEQ].rearrange("p (e t) -> p e t", e=EXPERTS)
        sqy = yflat[:, 0:KD * TOK].rearrange("p (k t) -> p k t", k=KD)

        def qs(l):
            return slice(0, TOK) if l < DEPTH - 1 else slice(CTX, TOK)

        def segs(l):
            return [(slice(CTX, TOK), 0)] + ([(slice(0, CTX), 1)] if l < DEPTH - 1 else [])

        def qtiles(l):
            return range(TILES) if l < DEPTH - 1 else range(CTX // P, TILES)

        def units(l):
            return [(tt, h) for tt in qtiles(l) for h in range(16)]

        def unit_q(tt, h):
            c = slice(tt * P, (tt + 1) * P)
            if h < 8:
                return zT[64 * (h // 4):64 * (h // 4) + 64, Z_Q + h % 4, c]
            if h < 12:
                return zT[64 * (h % 2):64 * (h % 2) + 64, Z_NQ + (h - 8) // 2, c]
            return mid[:, h - 12, c]

        def unit_keys(tt):
            return CTX if tt < CTX // P else TOK

        def unit_k(tt, h):
            c = slice(0, unit_keys(tt))
            if h < 8:
                return zT[64 * (h // 4):64 * (h // 4) + 64, Z_K, c]
            if h < 12:
                return zT[64 * (h % 2):64 * (h % 2) + 64, Z_NK + (h - 8) // 2, c]
            return mid[:, 4 + h - 12, c]

        def unit_v(h, j):
            col = 64 * (h // 4) if h < 8 else 128 + 64 * (h - 8) if h < 12 else 384 + 64 * (h - 12)
            return vT[:, j, col:col + 64]

        def scores(u):
            return bank[(0, 1, 5)[u % 3]]

        def attended(u):
            return bank[(4, 7, 6)[u % 3]]

        def unit_scale(h):
            return HEAD ** -0.5 if h < 12 else 96 ** -0.5

        NORMS = [([Z_Q + i], blk, HEAD, [V_QG]) for i in range(4)] + [([Z_K], blk, HEAD, [V_KG]),
                 ([Z_CQ + i for i in range(3)], ones, 384, [V_MQ + i for i in range(3)]),
                 ([Z_CKV + i for i in range(2)], ones, 256, [V_MKV + i for i in range(2)])]

        def norm_cols(l, g):
            return qs(l) if g < 4 or g == 5 else slice(0, TOK)

        def section_at(step, lag):
            done, rest = divmod(step - lag + 1, MOD_PERIOD)
            return [MOD_FIRST + done - 1] if rest == 0 and 1 <= done <= 6 - MOD_FIRST else []

        def norms_at(step, lag):
            return [g for g, s in enumerate(NORM_STEP) if s + lag == step]

        def rotations(l):
            gq = [(zT[:, Z_Q + i, CTX:TOK], 0) for i in range(4)] + [(zT[:, Z_K, CTX:TOK], 0)]
            return gq + [(zT[:, Z_KR, CTX:TOK], 1)] + [(mid[:, i, CTX:TOK], 1) for i in range(4)]

        T_LAT = CTX // P

        def out_rounds_before(l, j):
            return j if l == 0 else TILES + max(0, j - CTX // P)

        def has_out(l, j):
            return RW_ORDER[0][j] in qtiles(l)

        def unit_out(tt, h):
            chunk = h // 2 if h < 12 else 8 + (h - 12) // 2
            return slice(64 * (h % 2), 64 * (h % 2) + 64), chunk, slice(tt * P, (tt + 1) * P)

        def fresh_slab(seen, split, blocks):
            seen[0] += blocks
            first = split[0]
            split[0] = max(first, min((seen[0] - 1) // SLAB + PARTS, SLABS))
            return range(first, split[0])

        def post_out(l, which, m):
            w = qs(l).stop - qs(l).start
            if l % 2 and which:
                return bank[4 + m // 2][:, 256 * (m % 2):256 * (m % 2) + 256]
            return bank[4 + m % 4][:, 0:w]

        def post_bank_free(pe, l, which, m):
            if m >= 4:
                pe.wait_ge(S("po_sq"), KD * (2 * l + which) + m - 3)

        def post_norm(act, highs, l, which):
            q, pc = qs(l), 2 * l + which
            dst = (yo, mid)[which]
            for m in range(KD):
                if not (l % 2 and which):
                    highs((KD, FFC)[which])
                act.wait_ge(S("po_mm"), KD * pc + (m | 1 if l % 2 and which else m) + 1)
                act.activation(dst[:, m, q], post_out(l, which, m), ACT.Copy, scale=UNSCALE)
                act.activation(sqy[:, m, q], post_out(l, which, m), ACT.Square, scale=UNSCALE).then_inc(S("po_sq"), 1)
            act.wait_ge(S("po_ss"), pc + 1)
            act.activation(rstd[:, q], bank[0][:, 0:q.stop - q.start], ACT.Ln, bias=eps_col, scale=1.0 / D).then_inc(S("po_ln"), 1)
            act.wait_ge(S("po_ln"), pc + 1)
            act.activation(rstd[:, q], rstd[:, q], ACT.Exp, scale=-0.5).then_inc(S("po_rstd"), 1)

        def post_sum(pe, l, which, k):
            q, pc = qs(l), 2 * l + which
            pe.wait_ge(S("po_sq"), KD * pc + k + 1)
            ins = pe.matmul(bank[0][:, 0:q.stop - q.start], ones, sqy[:, k, q], start=k == 0, stop=k == KD - 1)
            if k == KD - 1:
                ins.then_inc(S("po_ss"), 1)

        def residual(dve, V, lows, l, which):
            q, pc = qs(l), 2 * l + which
            y = (yo, mid)[which]
            lows(KD * (KD, (FFC, EFC)[l % 2])[which])
            dve.wait_ge(S("po_rstd"), pc + 1)
            at = []
            for k in range(KD + 1):
                if k < KD:
                    V.did(dve.tensor_tensor(y[:, k, q], y[:, k, q], rstd[:, q], ALU.mult))
                    at.append(V.n)
                if k:
                    dve.wait_ge(V.sem, at[k - 1])
                    for cc, jc in segs(l):
                        ins = dve.scalar_tensor_tensor(out=xT[:, k - 1, cc], in0=y[:, k - 1, cc], scalar=gmods[:, l, 2 * which + 1, k - 1, jc:jc + 1],
                                                       in1=xT[:, k - 1, cc], op0=ALU.mult, op1=ALU.add)
                    ins.then_inc(S("res"), 1)
            dve.wait_ge(S("res"), KD * (pc + 1))

        RQ = 2 * 2
        ROUNDS = TILES
        LAYER_VEC_LOADS = 4
        block = ctx.enter_context(nc.Block())

        @block.sync
        def _(sp):
            sp.dma_start(scT, t["c2"]).then_inc(S("c_in"), 16)
            for n in range(SLABS):
                if n >= RING:
                    sp.wait_ge(S("split_lo"), n - RING + 1)
                sp.dma_start(ring[:, n % RING], t["w"][n]).then_inc(S(f"slab_in{n % RING}"), 16)
                if n == RING - 1:
                    sp.dma_start(cst, t["cst"]).then_inc(S("cst_in"), 16)
                    sp.dma_start(xT, t["x"]).then_inc(S("x_in"), 16)
            sp.wait_ge(S("res"), KD * 2 * DEPTH)
            sp.dma_start(t["out"], xT[:, :, CTX:TOK]).then_inc(S("out_done"), 16)
            sp.wait_ge(S("out_done"), 16)

        @block.gpsimd
        def _(pool):
            def low_parts(l, n, cols):
                for k in range(KD):
                    i = KD * (2 * l + n) + k + 1
                    pool.wait_ge(S("h_f32"), i)
                    pool.wait_ge(S("h_hi"), i)
                    ins = pool.tensor_tensor(h16[:, 1, k, cols], wider[:, k, cols], h16[:, 0, k, cols], ALU.subtract)
                ins.then_inc(S(("ha", "hb")[n]), 1)

            pool.dma_start(arena[0:32, 0:4096], t["sel"]).then_inc(S("rel_in"), 16)
            pool.dma_start(arena[0:32, 4096:4096 + 56], t["rpb"]).then_inc(S("rel_in"), 16)
            pool.dma_start(wrt, t["wr"]).then_inc(S("wr_in"), 16)
            pool.dma_start(vecs.rearrange("p l c -> p (l c)"), t["vec"]).then_inc(S("vecs_in"), 16)
            pool.wait_ge(S("rel_ev"), 8)
            pool.dma_start(t["scratch"], relrow[0:56, :]).then_inc(S("rel_out"), 16)
            for l in range(DEPTH):
                if l:
                    pool.wait_ge(S("res"), KD * 2 * l)
                pool.dma_start(mux, t["mux"][l]).then_inc(S("vec_in"), 16)
                pool.dma_start(rows, t["rows"][l:l + 1, :].broadcast_to([P, B_COLS])).then_inc(S("vec_in"), 16)
                pool.dma_start(lora2, t["lora2"][l]).then_inc(S("vec_in"), 16)
                pool.dma_start(lw, t["lw"][l]).then_inc(S("vec_in"), 16)
                low_parts(l, 0, slice(0, TOK))
                pool.wait_ge(S("rel_out"), 16)
                pool.wait_ge(S("rkv_a"), TILES * (l + 1))
                pool.wait_ge(S("rkv_d"), TILES * (l + 1))
                for r in range(GRID_H):
                    for h in range(4):
                        first = (l * 4 + h) * 7 + GRID_H - 1 - r
                        pool.dma_start(bias[64 * (r % 2):64 * (r % 2) + 64, r // 2, h, :].rearrange("p (r c) -> p r c", r=GRID_H),
                                       t["scratch"][first:first + GRID_H, :].rearrange("r (q c) -> q r c", q=GRID_W)
                                       ).then_inc(S("bias_in"), 16)
                for j in range(ROUNDS):
                    rr = l * ROUNDS + j
                    for lev in range(1, LEVELS):
                        for d in range(2):
                            n = (lev - 1) % 2
                            if lev == 1:
                                pool.wait_ge(S("am_done"), 8 * rr + 4 * (d + 1))
                            if lev > 2:
                                pool.wait_ge(S("x_mm"), 10 * rr + 2 * (lev - 3) + d + 1)
                            pool.tensor_tensor(ct[:, n, 4 * d:4 * d + 4, :], am[:, 4 * d:4 * d + 4, 0, :],
                                               level(lev).unsqueeze(1).broadcast_to([P, 4, P]), ALU.mult
                                               ).then_inc(S("ct_done"), 1)
                    pool.wait_ge(S("x_mm"), 10 * rr + 8)
                    for d in range(2):
                        pool.tensor_copy(rhs2[:, 4 * d:4 * d + 4, 0:64],
                                         eX[:, d, :].rearrange("p (h c) -> p h c", h=4)).then_inc(S("rhs_left"), 1)
                low_parts(l, 1, qs(l))

        @block.scalar
        def _(act):
            A = Steps(act, S("act_steps"))

            def rsqrt(out, src, scale, eps, sem):
                A.did(act.activation(out, src, ACT.Ln, bias=eps, scale=scale))
                A.settle()
                act.activation(out, out, ACT.Exp, scale=-0.5).then_inc(sem, 1)

            def rates(rr):
                for n, x in enumerate((sw, aa)):
                    act.wait_ge(S("w_pre"), 2 * rr + n + 1)
                    act.activation(x, x, ACT.Sigmoid).then_inc(S("w_sig"), 1)

            def deviation(no):
                act.wait_ge(S("o_var"), no + 1)
                A.did(act.activation(rt[:, 16:24], rt[:, 16:24], ACT.Ln, scale=1.0 / HEAD, bias=gn_eps_col))
                A.settle()
                act.activation(rt[:, 16:24], rt[:, 16:24], ACT.Exp, scale=-0.5).then_inc(S("o_rs"), 1)

            def modulated(l, n, cols_segs):
                for k in range(KD):
                    act.wait_ge(S("unit"), KD * (2 * l + n) + k + 1)
                    for cc, jc in cols_segs:
                        ins = act.activation(h16[:, 0, k, cc], wide[:, k, cc], ACT.Identity, scale=gmods[:, l, 2 * n, k, jc:jc + 1],
                                             bias=mods[:, l, 24 * n + k, jc:jc + 1])
                    ins.then_inc(S("h_hi"), 1)

            seen, high = [0], [0]

            def highs(blocks):
                for c in fresh_slab(seen, high, blocks):
                    act.wait_ge(S(f"slab_in{c % RING}"), 16 * (c // RING + 1))
                    if c >= PARTS:
                        act.wait_ge(S("slab_used"), c - PARTS + 1)
                    act.activation(parts[:, c % PARTS, 0], ring[:, c % RING], ACT.Copy, scale=WSCALE).then_inc(S("split_hi"), 1)

            act.wait_ge(S("c_in"), 16)
            A.did(act.activation(scT, scT, ACT.Silu))
            A.settle()
            act.activation(sc16[:, :, 0], scT, ACT.Copy).then_inc(S("silu_c"), 1)
            act.activation(sc16[:, :, 2], scT, ACT.Copy).then_inc(S("silu_c"), 1)
            highs(0)
            for l in range(DEPTH):
                q, n0 = qs(l), qs(l).start
                if l == 0:
                    highs(SLAB)
                    act.wait_ge(S("wr_in"), 16)
                    act.activation(wr16[:, 0], wrt[:, 0:KD * EXPERTS], ACT.Copy, scale=WSCALE).then_inc(S("wr_hi"), 1)
                    act.wait_ge(S("cst_in"), 16)
                    act.wait_ge(S("x_in"), 16)
                    act.wait_ge(S("rel_mm"), 8)
                for k in range(KD):
                    if l:
                        act.wait_ge(S("res"), KD * (2 * l - 1) + k + 1)
                    act.activation(wide[:, k, :], xT[:, k, :], ACT.Square).then_inc(S("na_sq"), 1)
                def mod_rows(s, b):
                    i = 6 * l + s
                    act.wait_ge(S("mod_mm"), i + 1)
                    if i >= 2:
                        act.wait_ge(S("mod_tr"), i - 1)
                    for x in range(2):
                        act.activation(modrow[0:4, s % 2, 512 * x:512 * x + 512], bank[b + x][0:4, :], ACT.Copy,
                                       scale=UNSCALE).then_inc(S("mod_ev"), 1)

                for s in range(MOD_FIRST):
                    highs(KD * SLAB - (SLAB if l == 0 and s == 0 else 0))
                    mod_rows(s, 2 * s)
                act.wait_ge(S("na_ss"), l + 1)
                rsqrt(rstd, bank[4], 1.0 / D, eps_col, S("na_rstd"))
                modulated(l, 0, [(slice(CTX, TOK), 0), (slice(0, CTX), 1)])
                act.wait_ge(S("vec_in"), 16 * LAYER_VEC_LOADS * (l + 1))
                act.activation(l16[:, 0, 0], lw, ACT.Copy, scale=WSCALE).then_inc(S("l_hi"), 1)
                act.wait_ge(S("lwm"), l + 1)
                act.activation(l16[:, 0, 1], lwm, ACT.Copy, scale=WSCALE).then_inc(S("l_hi"), 1)
                if l == 0:
                    act.wait_ge(S("rel_out"), 16)
                for i in range(Z_SLABS + 4):
                    for sec in section_at(i, 1):
                        mod_rows(sec, 6)
                    if i < Z_SLABS:
                        highs(SLAB * (1 + MOD_BESIDE * (i < MOD_STEPS)))
                    if i % 2 == 0:
                        act.wait_ge(S("z_mm"), (Z_SLABS + 4) * l + i + 1)
                        if i < Z_SLABS:
                            c, qonly = Z_STREAM[i]
                            dst, cc = zT[:, c, :], (q if qonly else slice(0, TOK))
                        else:
                            g = i - Z_SLABS
                            dst, cc = (lor[:, g, :] if g < 2 else zT[:, Z_LMU + g - 2, :]), slice(0, TOK)
                        act.activation(dst[:, cc], bank[i % 3][:, 0:cc.stop - cc.start], ACT.Copy, scale=UNSCALE).then_inc(S("z_ev_a"), 1)
                    for g in norms_at(i, 0):
                        gi, cc = len(NORMS) * l + g, norm_cols(l, g)
                        act.wait_ge(S("z_ev_a"), Z_EVEN * l + i // 2 + 1)
                        act.wait_ge(S("z_ev_d"), Z_ODD * l + (i + 1) // 2)
                        if g == 0:
                            act.wait_ge(S("l_lo"), 2 * (l + 1))
                        if g >= 2:
                            act.wait_ge(S("qk_ss"), gi - 1)
                        for n, c in enumerate(NORMS[g][0]):
                            last = act.activation(sq[:, g % 2, n, cc], zT[:, c, cc], ACT.Square)
                        last.then_inc(S("qk_sq"), 1)
                    for g in norms_at(i, 2):
                        gi, cc = len(NORMS) * l + g, norm_cols(l, g)
                        act.wait_ge(S("qk_ss"), gi + 1)
                        if g >= 2:
                            act.wait_ge(S("qk_norm"), gi - 1)
                        rsqrt(rsb[:, g % 2, cc], bank[4][:, 0:cc.stop - cc.start], 1.0 / NORMS[g][2], eps_col, S("qk_rs"))
                highs(V_SLABS * SLAB)
                for tt in range(TILES):
                    act.wait_ge(S("v_mm"), TILES * l + tt + 1)
                    act.activation(vT[:, tt, 0:384], bank[4 + tt][:, 0:384], ACT.Copy, scale=UNSCALE).then_inc(S("v_ev"), 1)
                for h in range(4):
                    highs(3)
                    act.wait_ge(S("uq_mm"), 4 * l + h + 1)
                    act.activation(mid[:, h, q], bank[4 + h % 2][:, 0:q.stop - n0], ACT.Copy, scale=UNSCALE).then_inc(S("uq_ev"), 1)
                highs(4 * 2 + 4)
                for tt in range(TILES):
                    act.wait_ge(S("uv_mm"), TILES * l + tt + 1)
                    act.activation(vT[:, tt, 384:640], bank[6 + tt % 2][:, 0:256], ACT.Copy, scale=UNSCALE).then_inc(S("uv_ev"), 1)
                act.wait_ge(S("shifted"), l + 1)
                act.activation(lor[0:64, 0, :], lor[0:64, 0, :], ACT.Tanh).then_inc(S("lor_ready"), 1)
                act.activation(lor[:, 1, :], lor[:, 1, :], ACT.Sigmoid).then_inc(S("lor_ready"), 1)
                for tt in range(TILES):
                    act.wait_ge(S("rkv_tr"), 2 * TILES * l + 2 * tt + 1)
                    act.activation(rkv[:, tt, 0:512], bank[2 * (tt % 2)], ACT.Copy).then_inc(S("rkv_a"), 1)
                base = sum(len(units(i)) for i in range(l))
                U = units(l)
                for step in range(len(U) + 4):
                    u = step
                    if u < len(U):
                        tt, h = U[u]
                        n, s3 = unit_keys(tt), u % 3
                        act.wait_ge(S("smax"), base + u + 1)
                        src, sc = scores(u)[:, 0:n], unit_scale(h)
                        if 8 <= h < 12 and n == TOK:
                            src, sc = prob[:, s3, 0:n], 1.0
                        if u >= 3:
                            act.wait_ge(S("pt_mm"), base + u - 2)
                            act.wait_ge(S("diag"), base + u - 2)
                        act.activation(prob[:, s3, 0:n], src, ACT.Exp, bias=nmax[:, s3:s3 + 1], scale=sc,
                                       accum_out=rsum[:, s3:s3 + 1]).then_inc(S("exp"), 1)
                    u = step - 4
                    if u >= 0:
                        rows_, chunk, cols = unit_out(*U[u])
                        act.wait_ge(S("pv_mm"), base + u + 1)
                        act.activation(y16[rows_, 0, chunk, cols], attended(u)[rows_, 0:P], ACT.Copy).then_inc(S("o_hi"), 1)
                    u = step - 2
                    if 0 <= u < len(U):
                        n = unit_keys(U[u][0])
                        act.wait_ge(S("pt_mm"), base + u + 1)
                        if u >= 2:
                            act.wait_ge(S("pv_mm"), base + u - 1)
                        act.activation(probT[:, u % 2, 0:n], bank[2 + u % 2][:, 0:n], ACT.Copy).then_inc(S("pt_ev"), 1)
                def outputs(j):
                    no = out_rounds_before(l, j)
                    act.wait_ge(S("o_mm"), no + 1)
                    if no:
                        act.wait_ge(S("yr"), no)
                    o4 = oo.rearrange("p (q x c) -> p q x c", q=4, x=2)
                    for x, b in enumerate((7, 3)):
                        act.activation(o4[:, :, x, :], bank[b][:, 0:256].rearrange("p (q c) -> p q c", q=4), ACT.Copy).then_inc(S("o_read"), 1)

                for j in range(ROUNDS):
                    rr = l * ROUNDS + j
                    if j == 0:
                        rates(rr)
                        act.wait_ge(S("kk_ss"), l + 1)
                        A.did(act.activation(rt[:, 0:16], rt[:, 0:16], ACT.Ln))
                        A.settle()
                        act.activation(rt[:, 0:16], rt[:, 0:16], ACT.Exp, scale=-0.5).then_inc(S("kk_rs"), 1)
                    act.wait_ge(S("cum"), 2 * rr + 1)
                    for dst, b, s in ((eX, 0, -DECAY), (eL, 2, -DECAY), (eN, 2, DECAY), (eA, 4, -DECAY)):
                        act.activation(dst, bank[b].rearrange("p (d c) -> p d c", d=2), ACT.Exp, scale=s
                                       ).then_inc(S("decays"), 1)
                    act.wait_ge(S("st"), 2 * rr + l + 1)
                    act.wait_ge(S("cum"), 2 * rr + 2)
                    act.activation(ecol, bank[1][:, 0:8], ACT.Exp, scale=-DECAY).then_inc(S("decays"), 1)
                    if j and has_out(l, j - 1):
                        outputs(j - 1)
                    for i in range(0, RQ, 2):
                        act.wait_ge(S("fm_tr"), RQ * rr + i + 1)
                        act.activation(fmt[:, i], bank[i].rearrange("p (a t) -> p a t", a=4), ACT.Copy
                                       ).then_inc(S("fm_a"), 1)
                    for d in range(2):
                        act.wait_ge(S("t_tr"), 2 * rr + d + 1)
                        act.activation(Tm[:, 4 * d:4 * d + 4], bank[d].rearrange("p (u t) -> p u t", u=4), ACT.Copy
                                       ).then_inc(S("t_ev"), 1)
                    for lev in range(1, LEVELS):
                        for d in range(2):
                            act.wait_ge(S("x_mm"), 10 * rr + 2 * (lev - 1) + d + 1)
                            if lev > 1:
                                act.wait_ge(S("yt_mm"), 10 * rr + 2 * (lev - 2) + d + 1)
                            act.activation(Xs[:, 4 * d:4 * d + 4], bank[2 + d].rearrange("p (u t) -> p u t", u=4),
                                           ACT.Copy).then_inc(S("x_ev"), 1)
                        if lev == 3 and j and has_out(l, j - 1):
                            deviation(out_rounds_before(l, j - 1))
                    act.wait_ge(S("av_mm"), rr + 1)
                    act.activation(rhs2[:, :, 64:128], bank[0].rearrange("p (u c) -> p u c", u=8), ACT.Copy
                                   ).then_inc(S("av_ev"), 1)
                    for d in range(2):
                        act.wait_ge(S("wu_mm"), 2 * rr + d + 1)
                        act.activation(nwu[:, 4 * d:4 * d + 4], bank[2 + d].rearrange("p (u c) -> p u c", u=4),
                                       ACT.Copy, scale=-1.0).then_inc(S("nwu"), 1)
                    if j < ROUNDS - 1:
                        rates(rr + 1)
                    act.wait_ge(S("g0_mm"), rr + 1)
                    for c in range(2):
                        act.activation(gh[:, c], bank[(5, 1)[c]].rearrange("p (x q v) -> p x q v", x=2, q=4), ACT.Copy
                                       ).then_inc(S("g0_ev"), 1)
                outputs(ROUNDS - 1)
                deviation(out_rounds_before(l, ROUNDS - 1))
                for i, tt in enumerate(qtiles(l)):
                    act.wait_ge(S("yr_tr"), TILES * l + len(qtiles(l)))
                    act.activation(y16[:, 0, 6:8, tt * P:(tt + 1) * P], bank[i][:, 0:256].rearrange("p (k t) -> p k t", k=2),
                                   ACT.Copy).then_inc(S("yr_hi"), 1)
                w = q.stop - n0
                for i in range(4 * KD):
                    gi = 4 * KD * l + i
                    highs(KD)
                    act.wait_ge(S("gate_mm"), gi + 1)
                    if i >= 2:
                        act.wait_ge(S("gated"), gi - 1)
                    act.activation(gate_sb[:, i % 2, 0:w], bank[i % 2][:, 0:w], ACT.Sigmoid, scale=UNSCALE).then_inc(S("gate"), 1)
                    highs(BRANCH_CHUNKS[i % 4])
                post_norm(act, highs, l, 0)
                for k in range(KD):
                    act.wait_ge(S("res"), KD * 2 * l + k + 1)
                    act.activation(wide[:, k, q], xT[:, k, q], ACT.Square).then_inc(S("nb_sq"), 1)
                act.wait_ge(S("nb_ss"), l + 1)
                rsqrt(rstd[:, q], bank[0][:, 0:w], 1.0 / D, eps_col, S("nb_rstd"))
                modulated(l, 1, segs(l))
                if l % 2 == 0:
                    for j in range(FFC):
                        highs(KD)
                        act.wait_ge(S("fg_mm"), j + 1)
                        if j >= 2:
                            act.wait_ge(S("hid"), j - 1)
                        act.activation(gate_sb[:, j % 2, 0:w], bank[j % 2][:, 0:w], ACT.Silu, scale=UNSCALE).then_inc(S("silu"), 1)
                        highs(KD)
                else:
                    act.wait_ge(S("r_max"), 1)
                    for i in range(2):
                        act.activation(rt[:, 32 + 8 * i:40 + 8 * i], rt[:, 32 + 8 * i:40 + 8 * i], ACT.Exp,
                                       bias=rt[:, 48 + i:49 + i]).then_inc(S("r_exp"), 1)
                    for i in range(4):
                        act.wait_ge(S("cw_mm"), i + 1)
                        act.activation(cw[:, 2 * i:2 * i + 2], bank[i].rearrange("p (e t) -> p e t", e=2), ACT.Copy
                                       ).then_inc(S("cw_ev"), 1)
                    for e in range(EXPERTS):
                        for j in range(EFC):
                            i = e * EFC + j
                            highs(KD)
                            act.wait_ge(S("eg_mm"), i + 1)
                            if i >= 2:
                                act.wait_ge(S("ehid"), i - 1)
                            act.activation(gate_sb[:, i % 2, 0:w], bank[i % 2][:, 0:w], ACT.Silu, scale=UNSCALE).then_inc(S("esilu"), 1)
                            highs(KD)
                        highs(EFC * KD)
                post_norm(act, highs, l, 1)

        @block.tensor
        def _(pe):
            slabs = [0]

            def mm(out, lhsT, rhs, start=True, stop=True, skip=False):
                return pe.matmul(out, lhsT, rhs, start=start, stop=stop, skip_group_check=skip)

            def slab():
                n = slabs[0]
                slabs[0] += 1
                pe.wait_ge(S("split_lo"), n + 1)
                return parts[:, n % PARTS]

            def frees_last(ins):
                if slabs[0] > 1:
                    ins.then_inc(S("slab_used"), 1)

            blocks = [None, SLAB]

            def product(out, rhs_of, n, start=True, stop=True, done=None, skip=False):
                for k in range(n):
                    fresh = blocks[1] == SLAB
                    if fresh:
                        blocks[0], blocks[1] = slab(), 0
                    wh, wl = (blocks[0][:, x, blocks[1], :] for x in range(2))
                    blocks[1] += 1
                    ins = mm(out, wh, rhs_of(0, k), k == 0 and start, False, skip)
                    if fresh:
                        frees_last(ins)
                    mm(out, wh, rhs_of(1, k), False, False, skip)
                    ins = mm(out, wl, rhs_of(0, k), False, k == n - 1 and stop, skip)
                if done:
                    ins.then_inc(S(done), 1)

            def by_token(out, x_of, w_of, n):
                for k in range(n):
                    mm(out, x_of(0, k), w_of(0, k), k == 0, False)
                    mm(out, x_of(1, k), w_of(0, k), False, False)
                    ins = mm(out, x_of(0, k), w_of(1, k), False, k == n - 1)
                return ins

            pe.wait_ge(S("rel_in"), 32)
            for i in range(8):
                mm(bank[i][0:56, :], arena[0:32, 4096:4152], arena[0:32, 512 * i:512 * i + 512]).then_inc(S("rel_mm"), 1)
            pe.wait_ge(S("rel_ev"), 8)
            pe.wait_ge(S("c_low"), 2)
            for l in range(DEPTH):
                q, n0 = qs(l), qs(l).start
                w = q.stop - n0
                if l:
                    pe.wait_ge(S("res"), KD * 2 * l)
                def mod_slab(s, k, b):
                    sl = slab()
                    for x in range(2):
                        for part in range(2):
                            ins = mm(bank[b + x][0:4, :], sc16[:, k, 2 * part:2 * part + 2].rearrange("p x j -> p (x j)"),
                                     sl[:, part, 4 * x:4 * x + 4].rearrange("p b c -> p (b c)"), k == 0 and part == 0, k == KD - 1 and part == 1)
                            if x == 0 and part == 0:
                                frees_last(ins)
                    if k == KD - 1:
                        ins.then_inc(S("mod_mm"), 1)

                def mod_turn(s, out):
                    pe.wait_ge(S("mod_ev"), 2 * (6 * l + s + 1))
                    pe.wait_ge(S("cst_in"), 16)
                    for c in range(KD):
                        ins = mm(out[:, 2 * c:2 * c + 2], modrow[0:4, s % 2, P * c:P * c + P], cst[0:4, C_FOLD:C_FOLD + 2])
                    ins.then_inc(S("mod_tr"), 1)

                for s in range(MOD_FIRST):
                    for k in range(KD):
                        mod_slab(s, k, 2 * s)
                    if s:
                        mod_turn(s - 1, bank[7])
                for k in range(KD):
                    pe.wait_ge(S("na_sq"), KD * l + k + 1)
                    last = mm(bank[4], ones, wide[:, k, :], k == 0, k == KD - 1)
                last.then_inc(S("na_ss"), 1)
                mod_turn(MOD_FIRST - 1, bank[5])

                def rotate(i, b):
                    if i < 5:
                        pe.wait_ge(S("qk_norm"), len(NORMS) * l + i + 1)
                    elif i == 5:
                        pe.wait_ge(S("z_ev_a"), Z_EVEN * l + Z_STREAM.index((Z_KR, False)) // 2 + 1)
                    if i:
                        pe.wait_ge(S("rot"), 10 * l + (i if i < 6 else i - 1))
                    x, kind = rotations(l)[i]
                    mm(bank[b][:, 0:SEQ], cst[:, C_ROT + kind * P:C_ROT + (kind + 1) * P], x).then_inc(S("rot_mm"), 1)

                for i in range(Z_SLABS + 4):
                    if i >= 3:
                        pe.wait_ge(S(("z_ev_d", "z_ev_a")[i % 2]), (Z_ODD, Z_EVEN)[i % 2] * l + (i - 3) // 2 + 1)
                    elif i == 0:
                        pe.wait_ge(S("ha"), l + 1)
                    if i < Z_SLABS:
                        cc = q if Z_STREAM[i][1] else slice(0, TOK)
                        product(bank[i % 3][:, 0:cc.stop - cc.start], lambda x, k: h16[:, x, k, cc], KD, done="z_mm")
                    else:
                        g = i - Z_SLABS
                        pe.wait_ge(S("l_lo"), 2 * l + g // 2 + 1)
                        by_token(bank[i % 3], lambda x, k: l16[:, x, g // 2, g % 2, k, :], lambda x, k: h16[:, x, k, :], KD).then_inc(S("z_mm"), 1)
                    if i < MOD_STEPS:
                        if i % MOD_PERIOD == 0 and i:
                            pe.wait_ge(S("mod_ev"), 2 * (6 * l + MOD_FIRST + i // MOD_PERIOD))
                        for n in range(MOD_BESIDE):
                            mod_slab(MOD_FIRST + i // MOD_PERIOD, MOD_BESIDE * (i % MOD_PERIOD) + n, 6)
                    for sec in section_at(i, 2):
                        if sec > MOD_FIRST:
                            pe.wait_ge(S("mod_in"), (6 - MOD_FIRST) * l + sec - MOD_FIRST)
                        mod_turn(sec, bank[3])
                    for g in norms_at(i, 1):
                        gi, cc = len(NORMS) * l + g, norm_cols(l, g)
                        pe.wait_ge(S("qk_sq"), gi + 1)
                        if g:
                            pe.wait_ge(S("qk_rs"), gi)
                        n = len(NORMS[g][0])
                        for k in range(n):
                            ins = mm(bank[4][:, 0:cc.stop - cc.start], NORMS[g][1], sq[:, g % 2, k, cc], k == 0, k == n - 1)
                        ins.then_inc(S("qk_ss"), 1)
                    if i in ROT_STEP:
                        rotate(ROT_STEP.index(i), 5)
                pe.wait_ge(S("qk_norm"), len(NORMS) * (l + 1))
                pe.wait_ge(S("rot"), 10 * l + 6)
                pe.wait_ge(S("mod_in"), (6 - MOD_FIRST) * (l + 1))
                for s in range(V_SLABS):
                    wv = slab()
                    for tt in range(TILES):
                        for k in range(KD):
                            o, c = bank[4 + tt][:, s * P:(s + 1) * P], slice(tt * P, (tt + 1) * P)
                            ins = mm(o, h16[:, 0, k, c], wv[:, 0, k, :], k == 0, False)
                            if tt == 0 and k == 0:
                                frees_last(ins)
                            mm(o, h16[:, 1, k, c], wv[:, 0, k, :], False, False)
                            ins = mm(o, h16[:, 0, k, c], wv[:, 1, k, :], False, k == KD - 1)
                        if s == V_SLABS - 1:
                            ins.then_inc(S("v_mm"), 1)
                pe.wait_ge(S("v_ev"), TILES * (l + 1))
                for h in range(4):
                    if h >= 2:
                        pe.wait_ge(S("uq_ev"), 4 * l + h - 1)
                    product(bank[4 + h % 2][:, 0:w], lambda x, k: z16[Z_CQ + k][:, x, q], 3, done="uq_mm")
                for h in range(4):
                    if h == 0:
                        pe.wait_ge(S("uq_ev"), 4 * l + 4)
                    if h >= 2:
                        pe.wait_ge(S("uk_ev"), 4 * l + h - 1)
                    product(bank[4 + h % 2], lambda x, k: z16[Z_CKV + k][:, x, :], 2, done="uk_mm")
                wuv = blocks[0][:, :, blocks[1]:SLAB, :]
                blocks[1] = SLAB
                for tt in range(TILES):
                    if tt >= 2:
                        pe.wait_ge(S("uv_ev"), TILES * l + tt - 1)
                    for s in range(2):
                        ins = by_token(bank[6 + tt % 2][:, s * P:(s + 1) * P], lambda x, k: z16[Z_CKV + k][:, x, tt * P:(tt + 1) * P],
                                       lambda x, k: wuv[:, x, 2 * s + k, :], 2)
                    ins.then_inc(S("uv_mm"), 1)
                pe.wait_ge(S("z_ev_a"), Z_EVEN * (l + 1))
                pe.wait_ge(S("z_ev_d"), Z_ODD * (l + 1))
                for i in range(6, 10):
                    rotate(i, 2 + i % 2)
                pe.wait_ge(S("shifted"), l + 1)
                pe.wait_ge(S("rot"), 10 * (l + 1))
                for tt in range(TILES):
                    b = 2 * (tt % 2)
                    if tt >= 2:
                        pe.wait_ge(S("rkv_a"), TILES * l + tt - 1)
                        pe.wait_ge(S("rkv_d"), TILES * l + tt - 1)
                    for i in range(6):
                        ins = pe.transpose(bank[b + i // 4][:, (i % 4) * P:(i % 4 + 1) * P], zT[:, Z_R + i, tt * P:(tt + 1) * P], ident)
                        if i in (3, 5):
                            ins.then_inc(S("rkv_tr"), 1)
                pe.wait_ge(S("rkv_a"), TILES * (l + 1))
                pe.wait_ge(S("rkv_d"), TILES * (l + 1))
                pe.wait_ge(S("rot"), 10 * (l + 1))
                pe.wait_ge(S("uk_ev"), 4 * (l + 1))
                pe.wait_ge(S("uv_ev"), TILES * (l + 1))
                base, U = sum(len(units(i)) for i in range(l)), units(l)
                for step in range(len(U) + 3):
                    u = step
                    if u < len(U):
                        tt, h = U[u]
                        if u >= 3:
                            pe.wait_ge(S("exp"), base + u - 2)
                        mm(scores(u)[:, 0:unit_keys(tt)], unit_q(tt, h), unit_k(tt, h)).then_inc(S("s_mm"), 1)
                    u = step - 2
                    if 0 <= u < len(U):
                        pe.wait_ge(S("exp"), base + u + 1)
                        if u >= 2:
                            pe.wait_ge(S("pt_ev"), base + u - 1)
                        pe.wait_ge(S("diag"), base + u + 1)
                        for j in range(unit_keys(U[u][0]) // P):
                            ins = mm(bank[2 + u % 2][:, j * P:(j + 1) * P], prob[:, u % 3, j * P:(j + 1) * P], diag[:, u % 3])
                        ins.then_inc(S("pt_mm"), 1)
                    u = step - 3
                    if u >= 0:
                        pe.wait_ge(S("pt_ev"), base + u + 1)
                        if u >= 3:
                            pe.wait_ge(S("o_ev"), base + u - 2)
                        nk = unit_keys(U[u][0]) // P
                        for j in range(nk):
                            ins = mm(attended(u)[unit_out(*U[u])[0], 0:P], unit_v(U[u][1], j), probT[:, u % 2, j * P:(j + 1) * P],
                                     j == 0, j == nk - 1)
                        ins.then_inc(S("pv_mm"), 1)
                pe.wait_ge(S("o_ev"), base + len(U))
                pe.wait_ge(S("lor_ready"), 2 * (l + 1))

                def rates(j):
                    for n in range(2):
                        for d in range(2):
                            r0 = 64 * n + 32 * d
                            tile = RW_ORDER[d][j]
                            ins = mm(bank[RATE_BANKS[2 * n + d]][:, 0:256], lor[r0:r0 + 32, 0, tile * P:(tile + 1) * P], lora2[r0:r0 + 32, 0:256])
                        ins.then_inc(S("w_mm"), 1)

                U8 = [(d, h, 4 * d + h, 2 * d + h // 2, slice(64 * (h % 2), 64 * (h % 2) + 64)) for d in range(2) for h in range(4)]

                def sums(j):
                    rr = l * ROUNDS + j
                    pe.wait_ge(S("w_pre"), 2 * rr + 2)
                    pe.wait_ge(S("w_sig"), 2 * rr + 1)
                    for b, of in ((0, (0, 2)), (2, (1, 3)), (4, (2, 0))):
                        for d in range(2):
                            ins = mm(bank[b][:, 256 * d:256 * d + 256], tri(of[d]), sw[:, d, :])
                    ins.then_inc(S("cum"), 1)
                    if j:
                        pe.wait_ge(S("g0_ev"), 2 * rr)
                    for qq in range(RQ):
                        ins = mm(bank[1][:, 2 * qq:2 * qq + 2], sw[:, qq // 2, P * (qq % 2):P * (qq % 2) + P],
                                 blk.rearrange("p (c x) -> p c x", c=2)[:, :, 0])
                    ins.then_inc(S("cum"), 1)

                def outputs(j):
                    for d, h, u, qq, hh in U8:
                        o = bank[(7, 3)[h % 2]][:, 64 * qq:64 * qq + 64]
                        mm(o, am[:, u, 3], rkv[:, RW_ORDER[d][j], 512 + 64 * h:576 + 64 * h], True, False, True)
                        mm(o, am[:, u, 1], nwu[:, u, 64:128], False, False, True)
                        for s in range(2):
                            c = CHUNK_ORDER[d][s]
                            cs = slice(64 * c, 64 * c + 64)
                            ins = mm(o[cs, :], m1[hh, qq, cs], state[hh, (2 * j + s) % 3, qq], False, s == 1, True)
                    ins.then_inc(S("o_mm"), 1)

                def gates(j):
                    for d in range(2):
                        tile = RW_ORDER[d][j]
                        ins = mm(bank[d][:, 0:256], lor[64 * d:64 * d + 64, 1, tile * P:(tile + 1) * P], lora2[64 * d:64 * d + 64, 256:512])
                    ins.then_inc(S("g_mm"), 1)

                for j in range(ROUNDS):
                    rr = l * ROUNDS + j
                    tau = [RW_ORDER[d][j] for d in range(2)]
                    out = RW_ORDER[0][j] in qtiles(l)

                    def v_of(d, h, rows_=slice(0, P)):
                        return rkv[rows_, tau[d], 512 + 64 * h:576 + 64 * h]

                    if j == 0:
                        rates(j)
                        sums(j)
                    if j and has_out(l, j - 1):
                        pe.wait_ge(S("m1"), rr)
                        outputs(j - 1)
                    for d in range(2):
                        pe.wait_ge(S("prod"), 2 * rr + d + 1)
                        for hp in range(2):
                            if d and hp and out_rounds_before(l, j):
                                pe.wait_ge(S("o_read"), 2 * out_rounds_before(l, j))
                            for a, x in enumerate((eX, eL, Bd, eN)):
                                ins = pe.transpose(bank[2 * d + hp][:, a * P:(a + 1) * P], x[:, d, P * hp:P * hp + P], ident)
                            ins.then_inc(S("fm_tr"), 1)
                    for d, h, u, qq, hh in U8:
                        if h % 2 == 0:
                            pe.wait_ge(S(("fm_a", "fm_d")[qq % 2]), 2 * rr + qq // 2 + 1)
                        if u >= 4:
                            pe.wait_ge(S("am_done"), 8 * rr + u - 3)
                        elif u == 0:
                            pe.wait_ge(S("decays"), 5 * (rr + 1))
                        b = bank[4 + u % 4]
                        mm(b[:, 0:256], fmt[hh, qq, 2], fmt[hh, qq, 0:2])
                        mm(b[:, 256:512], fmt[hh, qq, 3], fmt[hh, qq, 0:2]).then_inc(S("a_mm"), 1)
                    for lev in range(1, LEVELS):
                        for d in range(2):
                            if lev == 1:
                                pe.wait_ge(S("tt0"), 2 * rr + d + 1)
                                for h in range(4):
                                    ins = pe.transpose(bank[d][:, h * P:(h + 1) * P], TT[:, 4 * d + h], ident)
                                ins.then_inc(S("t_tr"), 1)
                            pe.wait_ge(S("ct_done"), 10 * rr + 2 * (lev - 1) + d + 1)
                            if lev == 1:
                                pe.wait_ge(S("t_ev"), 2 * rr + d + 1)
                            else:
                                pe.wait_ge(S("inv"), 10 * rr + 2 * (lev - 2) + d + 1)
                            for h in range(4):
                                ins = mm(bank[2 + d][:, h * P:(h + 1) * P], ct[:, (lev - 1) % 2, 4 * d + h], Tm[:, 4 * d + h])
                            ins.then_inc(S("x_mm"), 1)
                        if lev == LEVELS - 1:
                            if j and has_out(l, j - 1):
                                pe.wait_ge(S("g_read"), out_rounds_before(l, j - 1) + 1)
                            for d, h, u, qq, hh in U8:
                                ins = mm(bank[0][:, 64 * u:64 * u + 64], am[:, u, 2], v_of(d, h))
                            ins.then_inc(S("av_mm"), 1)
                        for d in range(2):
                            pe.wait_ge(S("x_ev"), 10 * rr + 2 * (lev - 1) + d + 1)
                            for h in range(4):
                                u = 4 * d + h
                                if lev < LEVELS - 1:
                                    mm(bank[4 + d][:, h * P:(h + 1) * P], TT[:, u], Xs[:, u])
                                ins = mm(bank[6 + d][:, h * P:(h + 1) * P], Xs[:, u], TT[:, u])
                            ins.then_inc(S("yt_mm"), 1)
                        if lev == 2 and j and has_out(l, j - 1):
                            gates(j - 1)
                    pe.wait_ge(S("inv"), 10 * (rr + 1))
                    pe.wait_ge(S("av_ev"), rr + 1)
                    pe.wait_ge(S("rhs_left"), 2 * (rr + 1))
                    for d, h, u, qq, hh in U8:
                        ins = mm(bank[2 + d][:, h * P:(h + 1) * P], TT[:, u], rhs2[:, u])
                        if h == 3:
                            ins.then_inc(S("wu_mm"), 1)
                    if j < ROUNDS - 1:
                        rates(j + 1)
                    for d, h, u, qq, hh in U8:
                        if h == 0:
                            pe.wait_ge(S("nwu"), 2 * rr + d + 1)
                        ins = mm(bank[4][hh, qq * P:(qq + 1) * P], nwu[:, u, 0:64], am[:, u, 1])
                    ins.then_inc(S("m1_mm"), 1)
                    pe.wait_ge(S("prod_end"), rr + 1)
                    if j < ROUNDS - 1:
                        pe.wait_ge(S("w_pre"), 2 * rr + 3)
                    for d, h, u, qq, hh in U8:
                        for c in range(2):
                            cs, b = slice(64 * c, 64 * c + 64), bank[(5, 1)[c]]
                            mm(b[hh, 64 * qq:64 * qq + 64], nwu[cs, u, 0:64], Be[cs, d, 64 * h:64 * h + 64])
                            o = b[hh, 256 + 64 * qq:320 + 64 * qq]
                            mm(o, Be[cs, d, 64 * h:64 * h + 64], nwu[cs, u, 64:128], True, False)
                            ins = mm(o, eA[cs, d, 64 * h:64 * h + 64], v_of(d, h, cs), False, True)
                    ins.then_inc(S("g0_mm"), 1)
                    if j < ROUNDS - 1:
                        pe.wait_ge(S("m1"), rr + 1)
                        sums(j + 1)
                    pe.wait_ge(S("g0_ev"), 2 * (rr + 1))
                    for s in range(2):
                        pe.wait_ge(S("st"), 2 * rr + s + l + 1)
                        for d, h, u, qq, hh in U8:
                            ins = mm(bank[6][hh, 256 * s + 64 * qq:256 * s + 64 * qq + 64], g0[hh, CHUNK_ORDER[d][s], qq],
                                     state[hh, (2 * j + s) % 3, qq])
                        ins.then_inc(S("st_mm"), 1)
                pe.wait_ge(S("m1"), ROUNDS * (l + 1))
                outputs(ROUNDS - 1)
                gates(ROUNDS - 1)
                yb = TILES * l
                for i, tt in enumerate(qtiles(l)):
                    if i == 0:
                        pe.wait_ge(S("yr"), 4 if l == 0 else 6)
                    for k in range(2):
                        ins = pe.transpose(bank[i][:, k * P:(k + 1) * P], yr[tt][:, k * P:(k + 1) * P], ident)
                    ins.then_inc(S("yr_tr"), 1)
                pe.wait_ge(S("yr_ev"), yb + len(qtiles(l)))
                pe.wait_ge(S("st"), (2 * ROUNDS) * (l + 1) + l + 1)
                for i in range(4 * KD):
                    m, br = divmod(i, 4)
                    gi = 4 * KD * l + i
                    if i >= 2:
                        pe.wait_ge(S("gate"), gi - 1)
                    product(bank[i % 2][:, 0:w], lambda x, k: h16[:, x, k, q], KD, done="gate_mm")
                    if i >= 2:
                        pe.wait_ge(S("gated"), gi - 1)
                    product(bank[2 + i % 2][:, 0:w], lambda x, k: y16[:, x, BRANCH_FIRST[br] + k, q], BRANCH_CHUNKS[br], done="br_mm")
                pe.wait_ge(S("merged"), KD * (l + 1))
                for m in range(KD):
                    post_bank_free(pe, l, 0, m)
                    product(bank[4 + m % 4][:, 0:w], lambda x, k: m16[:, x, k, q], KD, done="po_mm")
                    if m:
                        post_sum(pe, l, 0, m - 1)
                post_sum(pe, l, 0, KD - 1)
                for k in range(KD):
                    pe.wait_ge(S("nb_sq"), KD * l + k + 1)
                    ins = mm(bank[0][:, 0:w], ones, wide[:, k, q], k == 0, k == KD - 1)
                ins.then_inc(S("nb_ss"), 1)
                pe.wait_ge(S("hb"), l + 1)
                if l % 2 == 0:
                    for j in range(FFC):
                        if j >= 2:
                            pe.wait_ge(S("silu"), j - 1)
                        product(bank[j % 2][:, 0:w], lambda x, k: h16[:, x, k, q], KD, done="fg_mm")
                        if j >= 2:
                            pe.wait_ge(S("hid"), j - 1)
                        product(bank[2 + j % 2][:, 0:w], lambda x, k: h16[:, x, k, q], KD, done="fu_mm")
                    pe.wait_ge(S("hid"), FFC)
                    for m in range(KD):
                        post_bank_free(pe, l, 1, m)
                        product(bank[4 + m % 4][:, 0:w], lambda x, k: hid[:, x, k, q], FFC, done="po_mm")
                        if m:
                            post_sum(pe, l, 1, m - 1)
                    post_sum(pe, l, 1, KD - 1)
                else:
                    pe.wait_ge(S("wr_lo"), 1)
                    for i in range(2):
                        ins = by_token(bank[0][:, 8 * i:8 * i + 8], lambda x, k: h16[:, x, k, CTX + P * i:CTX + P * (i + 1)],
                                       lambda x, k: wr16[:, x, 8 * k:8 * k + 8], KD)
                    ins.then_inc(S("r_mm"), 1)
                    pe.wait_ge(S("comb"), 1)
                    for e in range(EXPERTS):
                        for i in range(2):
                            ins = mm(bank[e // 2][:, 256 * (e % 2) + P * i:256 * (e % 2) + P * (i + 1)],
                                     rt[:, 64 + 8 * i + e:65 + 8 * i + e].broadcast_to([P, P]), ident)
                        if e % 2:
                            ins.then_inc(S("cw_mm"), 1)
                    pe.wait_ge(S("cw_ev"), 4)
                    for e in range(EXPERTS):
                        for j in range(EFC):
                            i = e * EFC + j
                            if i >= 2:
                                pe.wait_ge(S("esilu"), i - 1)
                            product(bank[i % 2][:, 0:w], lambda x, k: h16[:, x, k, q], KD, done="eg_mm")
                            if i >= 2:
                                pe.wait_ge(S("ehid"), i - 1)
                            product(bank[2 + i % 2][:, 0:w], lambda x, k: h16[:, x, k, q], KD, done="eu_mm")
                        pe.wait_ge(S("ehid"), EFC * (e + 1))
                        for m in range(KD):
                            product(bank[4 + m // 2][:, 256 * (m % 2):256 * (m % 2) + 256], lambda x, k: ehid[:, e % 2, x, k, :], EFC,
                                    start=e == 0 and m % 2 == 0, stop=e == EXPERTS - 1, skip=True,
                                    done="po_mm" if e == EXPERTS - 1 else "edown" if m == KD - 1 else None)
                    for k in range(KD):
                        post_sum(pe, l, 1, k)

        @block.vector
        def _(dve):
            V = Steps(dve, S("vec_steps"))
            vs = S("vec_steps")

            def bc(x, *shape):
                return x.broadcast_to(list(shape))

            seen, low = [0], [0]

            def lows(blocks):
                for c in fresh_slab(seen, low, blocks):
                    dve.wait_ge(S("split_hi"), c + 1)
                    dve.scalar_tensor_tensor(out=parts[:, c % PARTS, 1], in0=ring[:, c % RING], scalar=WSCALE, in1=parts[:, c % PARTS, 0],
                                             op0=ALU.mult, op1=ALU.subtract).then_inc(S("split_lo"), 1)

            dve.wait_ge(S("silu_c"), 2)
            dve.memset(sc16[:, :, 3], 0.0).then_inc(S("c_low"), 1)
            dve.tensor_tensor(sc16[:, :, 1], scT, sc16[:, :, 0], ALU.subtract).then_inc(S("c_low"), 1)
            lows(0)
            for i in range(8):
                dve.wait_ge(S("rel_mm"), i + 1)
                dve.tensor_copy(relrow[0:56, 512 * i:512 * i + 512], bank[i][0:56, :]).then_inc(S("rel_ev"), 1)
            for l in range(DEPTH):
                q, n0 = qs(l), qs(l).start
                w = q.stop - n0
                vec, mod, gmod = vecs[:, l], mods[:, l], gmods[:, l]
                lows((MOD_FIRST * KD - 4) * SLAB)
                dve.wait_ge(S("vec_in"), 16 * LAYER_VEC_LOADS * (l + 1))
                for i, (g, c0, c1) in enumerate(((0, 0, 64), (0, 64, 128), (1, 0, 128))):
                    ins = dve.tensor_tensor(lwm[:, g, :, c0:c1], lw[:, g, :, c0:c1],
                                            bc(mux[:, 8 * i:8 * i + 8].unsqueeze(2), P, KD, c1 - c0), ALU.mult)
                ins.then_inc(S("lwm"), 1)
                lows(4 * SLAB)
                if l == 0:
                    dve.wait_ge(S("wr_hi"), 1)
                    dve.scalar_tensor_tensor(out=wr16[:, 1], in0=wrt[:, 0:KD * EXPERTS], scalar=WSCALE, in1=wr16[:, 0],
                                             op0=ALU.mult, op1=ALU.subtract).then_inc(S("wr_lo"), 1)
                    dve.wait_ge(S("cst_in"), 16)
                    dve.wait_ge(S("vecs_in"), 16)
                def mod_section(sec, src):
                    dve.wait_ge(S("mod_tr"), 6 * l + sec + 1)
                    m = mod[:, 8 * sec:8 * sec + 8, :]
                    ins = dve.tensor_tensor(m, src.rearrange("p (n j) -> p n j", j=2), bc(vec[:, V_BMOD + 8 * sec:V_BMOD + 8 * sec + 8].unsqueeze(2), P, 8, 2), ALU.add)
                    if sec < MOD_FIRST:
                        V.did(ins)
                        V.settle()
                    else:
                        ins.then_inc(S("mod_in"), 1)
                        dve.wait_ge(S("mod_in"), (6 - MOD_FIRST) * l + sec - MOD_FIRST + 1)
                    for i, (of, col) in enumerate(((1, V_NMPRE), (2, V_NMPOST), (4, V_NFPRE), (5, V_NFPOST))):
                        gain = bc(vec[:, col:col + KD].unsqueeze(2), P, KD, 2)
                        if of == sec and sec in (1, 4):
                            V.did(dve.scalar_tensor_tensor(out=gmod[:, i], in0=m, scalar=1.0, in1=gain, op0=ALU.add, op1=ALU.mult))
                        elif of == sec:
                            V.did(dve.tensor_tensor(gmod[:, i], m, gain, ALU.mult))
                    V.settle()

                for sec in range(MOD_FIRST):
                    mod_section(sec, bank[(7, 5)[sec]][:, 0:16])

                def modulated(which, cols_segs):
                    n = 2 * l + which
                    cc = slice(min(c.start for c, _j in cols_segs), TOK)
                    for k in range(KD + 1):
                        if k < KD:
                            dve.tensor_tensor(wide[:, k, cc], xT[:, k, cc], rstd[:, cc], ALU.mult).then_inc(S("unit"), 1)
                        if k:
                            dve.wait_ge(S("unit"), KD * n + k)
                            for c2, jc in cols_segs:
                                ins = dve.tensor_scalar(wider[:, k - 1, c2], wide[:, k - 1, c2], gmod[:, 2 * which, k - 1, jc:jc + 1],
                                                        mod[:, 24 * which + k - 1, jc:jc + 1], ALU.mult, ALU.add)
                            ins.then_inc(S("h_f32"), 1)

                dve.wait_ge(S("na_rstd"), l + 1)
                if l == 0:
                    dve.wait_ge(S("rel_out"), 16)
                modulated(0, [(slice(CTX, TOK), 0), (slice(0, CTX), 1)])
                for n, of in enumerate((lw, lwm)):
                    dve.wait_ge(S("l_hi"), 2 * l + n + 1)
                    dve.scalar_tensor_tensor(out=l16[:, 1, n], in0=of, scalar=WSCALE, in1=l16[:, 0, n],
                                             op0=ALU.mult, op1=ALU.subtract).then_inc(S("l_lo"), 1)
                def rotate(i, b):
                    x, kind = rotations(l)[i]
                    dve.wait_ge(S("rot_mm"), 10 * l + i + 1)
                    r = rtmp[:, i % 2, 0:SEQ]
                    if i >= 2:
                        dve.wait_ge(S("rot"), 10 * l + i - 1)
                    V.did(dve.tensor_tensor(r, bank[b][:, 0:SEQ], rope(2 * kind + 1), ALU.mult))
                    V.did(dve.tensor_tensor(x, x, rope(2 * kind), ALU.mult))
                    V.settle()
                    dve.tensor_tensor(x, x, r, ALU.add).then_inc(S("rot"), 1)

                if l == 0:
                    dve.wait_ge(S("rel_out"), 16)
                for i in range(Z_SLABS + 4):
                    if i < Z_SLABS:
                        lows(SLAB * (1 + MOD_BESIDE * (i < MOD_STEPS)))
                    if i % 2:
                        dve.wait_ge(S("z_mm"), (Z_SLABS + 4) * l + i + 1)
                        if i < Z_SLABS:
                            c, qonly = Z_STREAM[i]
                            dst, cc = zT[:, c, :], (q if qonly else slice(0, TOK))
                        else:
                            g = i - Z_SLABS
                            dst, cc = (lor[:, g, :] if g < 2 else zT[:, Z_LMU + g - 2, :]), slice(0, TOK)
                        dve.tensor_scalar(dst[:, cc], bank[i % 3][:, 0:cc.stop - cc.start], UNSCALE, None, ALU.mult).then_inc(S("z_ev_d"), 1)
                    for g in norms_at(i, 2):
                        chunks, _m, width, gains = NORMS[g]
                        cc = norm_cols(l, g)
                        dve.wait_ge(S("qk_rs"), len(NORMS) * l + g + 1)
                        if g == 6:
                            dve.wait_ge(S("qk_norm"), len(NORMS) * l + g)
                        if g == 5:
                            dve.wait_ge(S("rot"), 10 * l + 5)
                        for n, (c, gcol) in enumerate(zip(chunks, gains)):
                            to = zT[:, c, cc] if g < 5 else rtmp[:, n % 2, cc]
                            ins = dve.scalar_tensor_tensor(out=to, in0=zT[:, c, cc], scalar=vec[:, gcol:gcol + 1],
                                                           in1=rsb[:, g % 2, cc], op0=ALU.mult, op1=ALU.mult)
                            if g >= 5:
                                V.did(ins)
                                V.settle()
                                V.did(dve.tensor_copy(z16[c][:, 0, cc], to))
                                V.settle()
                                ins = dve.tensor_tensor(z16[c][:, 1, cc], to, z16[c][:, 0, cc], ALU.subtract)
                                if n < len(chunks) - 1:
                                    V.did(ins)
                                    V.settle()
                        ins.then_inc(S("qk_norm"), 1)
                    for sec in section_at(i, 2):
                        mod_section(sec, bank[3][:, 0:16])
                    if i in ROT_STEP:
                        if i == ROT_STEP[5]:
                            dve.wait_ge(S("qk_norm"), len(NORMS) * (l + 1))
                        rotate(ROT_STEP.index(i), 5)
                lows(SLAB)
                dve.wait_ge(S("z_ev_a"), Z_EVEN * (l + 1))
                dve.wait_ge(S("z_ev_d"), Z_ODD * (l + 1))
                dve.wait_ge(S("qk_norm"), len(NORMS) * (l + 1))
                src = arena[:, Z_R * TOK:(Z_R + 8) * TOK].rearrange("p (s t) -> p s t", t=CTX)
                nb = yflat[:, 0:8 * TOK].rearrange("p (s t) -> p s t", t=CTX)
                shift = yflat[:, 0:8 * TOK].rearrange("p (k t) -> p k t", k=8)
                V.did(dve.tensor_tensor(nb[:, :, 1:CTX - 1], src[:, :, 0:CTX - 2], src[:, :, 2:CTX], ALU.add))
                V.did(dve.tensor_copy(nb[:, :, 0:1], src[:, :, 1:2]))
                V.did(dve.tensor_copy(nb[:, :, CTX - 1:CTX], src[:, :, CTX - 2:CTX - 1]))
                V.settle()
                lows(SLAB)
                V.did(dve.scalar_tensor_tensor(out=nb, in0=nb, scalar=0.5, in1=src, op0=ALU.mult, op1=ALU.subtract))
                V.settle()
                lows(SLAB)
                for i in range(6):
                    z = zT[:, Z_R + i, :]
                    dve.scalar_tensor_tensor(out=z, in0=shift[:, i, :], scalar=vec[:, V_MUP + i:V_MUP + i + 1], in1=z,
                                             op0=ALU.mult, op1=ALU.add)
                dve.tensor_tensor(lor, lor, shift[:, 6:8, :], ALU.add).then_inc(S("shifted"), 1)
                lows(4 * 3)
                dve.wait_ge(S("rot"), 10 * l + 6)
                for h in range(4):
                    lows(2)
                    dve.wait_ge(S("uk_mm"), 4 * l + h + 1)
                    dve.scalar_tensor_tensor(out=mid[:, 4 + h, :], in0=bank[4 + h % 2], scalar=UNSCALE, in1=zT[:, Z_KR, :],
                                             op0=ALU.mult, op1=ALU.add).then_inc(S("uk_ev"), 1)
                lows(4)
                for i in range(6, 10):
                    rotate(i, 2 + i % 2)
                dve.wait_ge(S("rot"), 10 * (l + 1))
                for tt in range(TILES):
                    dve.wait_ge(S("rkv_tr"), 2 * TILES * l + 2 * tt + 2)
                    dve.tensor_copy(rkv[:, tt, 512:768], bank[2 * (tt % 2) + 1][:, 0:256]).then_inc(S("rkv_d"), 1)
                base, U = sum(len(units(i)) for i in range(l)), units(l)
                for step in range(len(U) + 4):
                    u = step
                    if u < len(U):
                        tt, h = U[u]
                        s3, n = u % 3, unit_keys(tt)
                        src = scores(u)
                        dve.wait_ge(S("s_mm"), base + u + 1)
                        if u >= 3:
                            dve.wait_ge(S("exp"), base + u - 2)
                        nm = nmax[:, s3:s3 + 1]
                        if 8 <= h < 12 and n == TOK:
                            if u >= 3:
                                dve.wait_ge(S("pt_mm"), base + u - 2)
                            dve.wait_ge(S("bias_in"), 16 * 16 * (l + 1))
                            V.did(dve.scalar_tensor_tensor(out=prob[:, s3, CTX:TOK], in0=src[:, CTX:TOK], scalar=unit_scale(h),
                                                           in1=bias[:, tt - T_LAT, h - 8, :], op0=ALU.mult, op1=ALU.add))
                            V.did(dve.tensor_scalar(prob[:, s3, 0:CTX], src[:, 0:CTX], unit_scale(h), None, ALU.mult))
                            V.settle()
                            dve.tensor_reduce(nm, prob[:, s3, 0:n], AX.X, ALU.max, negate=True).then_inc(S("smax"), 1)
                        else:
                            V.did(dve.tensor_reduce(bmax[:, s3:s3 + 1], src[:, 0:n], AX.X, ALU.max))
                            V.settle()
                            dve.tensor_scalar(nm, bmax[:, s3:s3 + 1], -unit_scale(h), None, ALU.mult).then_inc(S("smax"), 1)
                    u = step - 1
                    if 0 <= u < len(U):
                        s3 = u % 3
                        dve.wait_ge(S("exp"), base + u + 1)
                        V.did(dve.reciprocal(rinv[:, s3:s3 + 1], rsum[:, s3:s3 + 1]))
                        V.settle()
                        if u >= 3:
                            dve.wait_ge(S("pt_mm"), base + u - 2)
                        dve.tensor_scalar(diag[:, s3], ident, rinv[:, s3:s3 + 1], None, ALU.mult).then_inc(S("diag"), 1)
                    u = step - 4
                    if u >= 0:
                        rows_, chunk, cols = unit_out(*U[u])
                        dve.wait_ge(S("o_hi"), base + u + 1)
                        dve.tensor_tensor(y16[rows_, 1, chunk, cols], attended(u)[rows_, 0:P], y16[rows_, 0, chunk, cols],
                                          ALU.subtract).then_inc(S("o_ev"), 1)
                for tile in range(TILES):
                    V.did(dve.memset(yr[tile], 0.0))
                dve.memset(state[:, 0], 0.0).then_inc(S("st"), 1)
                o3 = oo.rearrange("p (u c) -> p u c", u=8)
                o2 = oo.rearrange("p (d c) -> p d c", d=2)
                t13 = t1.rearrange("p d (h c) -> p (d h) c", h=4)

                def rates(j):
                    rr = l * ROUNDS + j
                    for n, (dst, row) in enumerate(((sw, B_W0), (aa, B_A0))):
                        dve.wait_ge(S("w_mm"), 2 * rr + n + 1)
                        for d in range(2):
                            ins = dve.tensor_tensor(dst[:, d], bank[RATE_BANKS[2 * n + d]][:, 0:256], rows[:, row + 256 * d:row + 256 * d + 256], ALU.add)
                        ins.then_inc(S("w_pre"), 1)

                def keys(j):
                    rr = l * ROUNDS + j
                    dve.wait_ge(S("w_sig"), 2 * rr + 2)
                    if rr:
                        dve.wait_ge(S("prod_end"), rr)
                    V.did(dve.scalar_tensor_tensor(out=kd, in0=aa, scalar=-1.0, in1=bc(rows[:, B_KA:B_KA + 256].unsqueeze(1), P, 2, 256),
                                                   op0=ALU.add, op1=ALU.mult))
                    for d in range(2):
                        V.did(dve.tensor_tensor(bb[:, d], kk[:, RW_ORDER[d][j]], aa[:, d], ALU.mult))
                    V.settle()
                    for d in range(2):
                        V.did(dve.scalar_tensor_tensor(out=kd[:, d], in0=kd[:, d], scalar=1.0, in1=rkv[:, RW_ORDER[d][j], 256:512],
                                                       op0=ALU.add, op1=ALU.mult))
                    V.settle()

                def bonus_of(j):
                    for d in range(2):
                        V.did(dve.tensor_tensor(t2[:, d], rkv[:, RW_ORDER[d][j], 0:256], kd[:, d], ALU.mult))
                    V.settle()
                    V.did(dve.tensor_tensor(t2, t2, bc(rows[:, B_RK:B_RK + 256].unsqueeze(1), P, 2, 256), ALU.mult))
                    V.settle()
                    V.did(dve.tensor_reduce(bonus, t2.rearrange("p d (h c) -> p (d h) c", h=4), AX.X, ALU.add))
                    V.settle()

                def readout(j, part):
                    no = out_rounds_before(l, j)
                    if part == 0:
                        dve.wait_ge(S("o_read"), 2 * (no + 1))
                        V.did(dve.tensor_reduce(rt[:, 24:32], o3, AX.X, ALU.add))
                        V.settle()
                        V.did(dve.scalar_tensor_tensor(out=o3, in0=bc(rt[:, 24:32].unsqueeze(2), P, 8, 64), scalar=-1.0 / HEAD, in1=o3,
                                                       op0=ALU.mult, op1=ALU.add))
                        V.settle()
                    elif part == 1:
                        V.did(dve.tensor_tensor(t13, o3, o3, ALU.mult))
                        V.settle()
                        dve.tensor_reduce(rt[:, 16:24], t13, AX.X, ALU.add).then_inc(S("o_var"), 1)
                    elif part == 2:
                        dve.wait_ge(S("o_rs"), no + 1)
                        V.did(dve.tensor_tensor(o3, o3, bc(rt[:, 16:24].unsqueeze(2), P, 8, 64), ALU.mult))
                        V.settle()
                        V.did(dve.tensor_tensor(o2, o2, bc(rows[:, B_LNW:B_LNW + 256].unsqueeze(1), P, 2, 256), ALU.mult))
                        for d in range(2):
                            V.did(dve.tensor_tensor(t2[:, d].rearrange("p (h c) -> p h c", h=4),
                                                    rkv[:, RW_ORDER[d][j], 512:768].rearrange("p (h c) -> p h c", h=4),
                                                    bc(bonus[:, 4 * d:4 * d + 4].unsqueeze(2), P, 4, 64), ALU.mult))
                        V.settle()
                    elif part == 3:
                        V.did(dve.tensor_tensor(o2, o2, bc(rows[:, B_LNB:B_LNB + 256].unsqueeze(1), P, 2, 256), ALU.add))
                        V.settle()
                        V.did(dve.tensor_tensor(o2, o2, t2, ALU.add))
                        V.settle()
                        dve.wait_ge(S("g_mm"), no + 1)
                        for d in range(2):
                            ins = dve.tensor_tensor(o2[:, d], o2[:, d], bank[d][:, 0:256], ALU.mult)
                        ins.then_inc(S("g_read"), 1)
                    else:
                        dve.wait_ge(S("g_read"), no + 1)
                        for d in range(2):
                            tile = RW_ORDER[d][j]
                            ins = dve.tensor_tensor(yr[tile], yr[tile], o2[:, d], ALU.add)
                        ins.then_inc(S("yr"), 1)
                        dve.wait_ge(S("yr"), no + 1)

                for j in range(ROUNDS):
                    rr = l * ROUNDS + j
                    tau = [RW_ORDER[d][j] for d in range(2)]
                    out = RW_ORDER[0][j] in qtiles(l)
                    if j == 0:
                        rates(j)
                        dve.wait_ge(S("rkv_a"), TILES * (l + 1))
                        hs = kk.rearrange("p t (h c) -> p (t h) c", h=4)
                        V.did(dve.tensor_tensor(kk, rkv[:, :, 256:512], bc(rows[:, B_KK:B_KK + 256].unsqueeze(1), P, TILES, 256), ALU.mult))
                        V.settle()
                        scr = TT.rearrange("p u t -> p (u t)").rearrange("p (t c) -> p t c", t=TILES)
                        V.did(dve.tensor_tensor(scr, kk, kk, ALU.mult))
                        V.settle()
                        V.did(dve.tensor_reduce(rt[:, 0:16], scr.rearrange("p t (h c) -> p (t h) c", h=4), AX.X, ALU.add))
                        V.settle()
                        dve.tensor_scalar(rt[:, 0:16], rt[:, 0:16], 1e-12, None, ALU.max).then_inc(S("kk_ss"), 1)
                        dve.wait_ge(S("kk_rs"), l + 1)
                        dve.tensor_tensor(hs, hs, bc(rt[:, 0:16].unsqueeze(2), P, 16, 64), ALU.mult).then_inc(S("kk_ready"), 1)
                        dve.wait_ge(S("kk_ready"), l + 1)
                        keys(j)
                    dve.wait_ge(S("decays"), 5 * (rr + 1))
                    for d in range(2):
                        dve.tensor_tensor(eX[:, d], eX[:, d], kk[:, tau[d]], ALU.mult)
                        dve.tensor_tensor(eL[:, d], eL[:, d], rkv[:, tau[d], 0:256], ALU.mult)
                        dve.tensor_tensor(Bd[:, d], bb[:, d], eN[:, d], ALU.mult)
                        dve.tensor_tensor(eN[:, d], eN[:, d], kd[:, d], ALU.mult).then_inc(S("prod"), 1)
                    dve.tensor_tensor(Be, bb, eA, ALU.mult)
                    dve.tensor_tensor(eA, eA, kd, ALU.mult).then_inc(S("prod_end"), 1)
                    for i in range(1, RQ, 2):
                        dve.wait_ge(S("fm_tr"), RQ * rr + i + 1)
                        dve.tensor_copy(fmt[:, i], bank[i].rearrange("p (a t) -> p a t", a=4)).then_inc(S("fm_d"), 1)
                    for u in range(8):
                        d = u // 4
                        dve.wait_ge(S("a_mm"), 8 * rr + u + 1)
                        m2 = cst[:, C_TRI + 256 * d:C_TRI + 256 * d + 256]
                        dve.tensor_tensor(am[:, u].rearrange("p (x a) t -> p x (a t)", x=2), bank[4 + u % 4].rearrange("p (x t) -> p x t", x=2),
                                          bc(m2.unsqueeze(1), P, 2, 256), ALU.mult).then_inc(S("am_done"), 1)
                        if u % 4 == 3:
                            dve.wait_ge(S("am_done"), 8 * rr + u + 1)
                            half = slice(4 * d, 4 * d + 4)
                            V.did(dve.scalar_tensor_tensor(out=TT[:, half], in0=am[:, half, 0, :], scalar=-1.0,
                                                           in1=bc(level(0).unsqueeze(1), P, 4, P), op0=ALU.mult, op1=ALU.mult))
                            V.settle()
                            dve.tensor_tensor(TT[:, half], TT[:, half], bc(ident.unsqueeze(1), P, 4, P), ALU.add).then_inc(S("tt0"), 1)
                    dve.wait_ge(S("t_ev"), 2 * (rr + 1))
                    for lev in range(1, LEVELS):
                        for d in range(2):
                            half = slice(4 * d, 4 * d + 4)
                            dve.wait_ge(S("yt_mm"), 10 * rr + 2 * (lev - 1) + d + 1)
                            if lev > 1:
                                dve.wait_ge(S("inv"), 10 * rr + 2 * (lev - 2) + d + 1)
                            else:
                                dve.wait_ge(S("tt0"), 2 * rr + d + 1)
                            if lev < LEVELS - 1:
                                dve.tensor_tensor(Tm[:, half], Tm[:, half], bank[4 + d].rearrange("p (u t) -> p u t", u=4), ALU.subtract)
                            dve.tensor_tensor(TT[:, half], TT[:, half], bank[6 + d].rearrange("p (u t) -> p u t", u=4),
                                              ALU.subtract).then_inc(S("inv"), 1)
                        if j and has_out(l, j - 1) and lev < LEVELS - 1:
                            readout(j - 1, lev - 1)
                    if j < ROUNDS - 1:
                        rates(j + 1)
                    dve.wait_ge(S("m1_mm"), rr + 1)
                    dve.tensor_tensor(m1, bank[4].rearrange("p (q t) -> p q t", q=4), fmt[:, :, 1, :], ALU.add).then_inc(S("m1"), 1)
                    if j and has_out(l, j - 1):
                        readout(j - 1, LEVELS - 2)
                    if out:
                        bonus_of(j)
                    if j < ROUNDS - 1:
                        keys(j + 1)
                    dve.wait_ge(S("g0_ev"), 2 * (rr + 1))
                    for s in range(2):
                        dve.wait_ge(S("st"), 2 * rr + s + l + 1)
                        new = state[:, (2 * j + s + 1) % 3]
                        for qq in range(RQ):
                            c = CHUNK_ORDER[qq // 2][s]
                            V.did(dve.scalar_tensor_tensor(out=new[:, qq], in0=state[:, (2 * j + s) % 3, qq],
                                                           scalar=ecol[:, 2 * qq + c:2 * qq + c + 1],
                                                           in1=h0[:, c, qq], op0=ALU.mult, op1=ALU.add))
                        V.settle()
                        dve.wait_ge(S("st_mm"), 2 * rr + s + 1)
                        dve.tensor_tensor(new, new, bank[6][:, 256 * s:256 * s + 256].rearrange("p (q v) -> p q v", q=4),
                                          ALU.add).then_inc(S("st"), 1)
                for part in range(5):
                    readout(ROUNDS - 1, part)
                for i, tt in enumerate(qtiles(l)):
                    dve.wait_ge(S("yr_hi"), TILES * l + i + 1)
                    c = slice(tt * P, (tt + 1) * P)
                    dve.tensor_tensor(y16[:, 1, 6:8, c], bank[i][:, 0:256].rearrange("p (k t) -> p k t", k=2), y16[:, 0, 6:8, c],
                                      ALU.subtract).then_inc(S("yr_ev"), 1)
                for i in range(4 * KD):
                    m, br = divmod(i, 4)
                    gi = 4 * KD * l + i
                    lows(KD)
                    lows(BRANCH_CHUNKS[br])
                    dve.wait_ge(S("gate"), gi + 1)
                    dve.wait_ge(S("br_mm"), gi + 1)
                    dst = merged[:, m, q] if br == 0 else prod[:, i % 2, 0:w]
                    if br == 1 and KD * l + m:
                        dve.wait_ge(S("merged"), KD * l + m)
                    dve.scalar_tensor_tensor(out=dst, in0=bank[2 + i % 2][:, 0:w], scalar=UNSCALE, in1=gate_sb[:, i % 2, 0:w],
                                             op0=ALU.mult, op1=ALU.mult).then_inc(S("gated"), 1)
                    if br:
                        dve.wait_ge(S("gated"), gi + 1)
                        ins = dve.tensor_tensor(merged[:, m, q], merged[:, m, q], dst, ALU.add)
                        V.did(ins)
                        V.settle()
                        if br == 3:
                            V.did(dve.tensor_copy(m16[:, 0, m, q], merged[:, m, q]))
                            V.settle()
                            dve.tensor_tensor(m16[:, 1, m, q], merged[:, m, q], m16[:, 0, m, q], ALU.subtract).then_inc(S("merged"), 1)
                residual(dve, V, lows, l, 0)
                dve.wait_ge(S("nb_rstd"), l + 1)
                modulated(1, segs(l))
                if l % 2 == 0:
                    for j in range(FFC):
                        lows(2 * KD)
                        dve.wait_ge(S("silu"), j + 1)
                        dve.wait_ge(S("fu_mm"), j + 1)
                        if j >= 2:
                            dve.wait_ge(S("hid"), j - 1)
                        V.did(dve.scalar_tensor_tensor(out=prod[:, j % 2, 0:w], in0=bank[2 + j % 2][:, 0:w], scalar=UNSCALE,
                                                       in1=gate_sb[:, j % 2, 0:w], op0=ALU.mult, op1=ALU.mult))
                        V.settle()
                        V.did(dve.tensor_copy(hid[:, 0, j, q], prod[:, j % 2, 0:w]))
                        V.settle()
                        dve.tensor_tensor(hid[:, 1, j, q], prod[:, j % 2, 0:w], hid[:, 0, j, q], ALU.subtract).then_inc(S("hid"), 1)
                else:
                    dve.wait_ge(S("r_mm"), 1)
                    dve.wait_ge(S("wr_in"), 16)
                    lg = rt[:, 32:48].rearrange("p (i e) -> p i e", i=2)
                    V.did(dve.scalar_tensor_tensor(out=lg, in0=bank[0][:, 0:16].rearrange("p (i e) -> p i e", i=2), scalar=UNSCALE,
                                                   in1=bc(wrt[:, 64:72].unsqueeze(1), P, 2, EXPERTS), op0=ALU.mult, op1=ALU.add))
                    V.settle()
                    dve.tensor_reduce(rt[:, 48:50], lg, AX.X, ALU.max, negate=True).then_inc(S("r_max"), 1)
                    dve.wait_ge(S("r_exp"), 2)
                    V.did(dve.tensor_reduce(rt[:, 50:52], lg, AX.X, ALU.add))
                    V.settle()
                    V.did(dve.reciprocal(rt[:, 50:52], rt[:, 50:52]))
                    V.settle()
                    V.did(dve.tensor_tensor(lg, lg, bc(rt[:, 50:52].unsqueeze(2), P, 2, EXPERTS), ALU.mult))
                    V.settle()
                    for i in range(2):
                        pi = lg[:, i, :].unsqueeze(2).broadcast_to([P, 8, 8])
                        pj = lg[:, i, :].unsqueeze(1).broadcast_to([P, 8, 8])
                        gt = prod[:, 0, 64 * i:64 * i + 64].rearrange("p (i j) -> p i j", i=8)
                        eq = prod[:, 1, 64 * i:64 * i + 64].rearrange("p (i j) -> p i j", i=8)
                        V.did(dve.tensor_tensor(gt, pj, pi, ALU.is_gt))
                        V.did(dve.tensor_tensor(eq, pj, pi, ALU.is_equal))
                        V.settle()
                        V.did(dve.tensor_tensor(eq, eq, cst[:, C_LOW:C_LOW + 64].rearrange("p (i j) -> p i j", i=8), ALU.mult))
                        V.settle()
                        V.did(dve.tensor_tensor(gt, gt, eq, ALU.add))
                        V.settle()
                        V.did(dve.tensor_reduce(rt[:, 64 + 8 * i:72 + 8 * i], gt, AX.X, ALU.add))
                    V.settle()
                    cm = rt[:, 64:80]
                    V.did(dve.tensor_scalar(cm, cm, 1.5, None, ALU.is_lt))
                    V.settle()
                    V.did(dve.tensor_tensor(cm, cm, rt[:, 32:48], ALU.mult))
                    V.settle()
                    V.did(dve.tensor_reduce(rt[:, 50:52], cm.rearrange("p (i e) -> p i e", i=2), AX.X, ALU.add))
                    V.settle()
                    V.did(dve.reciprocal(rt[:, 50:52], rt[:, 50:52]))
                    V.settle()
                    dve.tensor_tensor(cm.rearrange("p (i e) -> p i e", i=2), cm.rearrange("p (i e) -> p i e", i=2),
                                      bc(rt[:, 50:52].unsqueeze(2), P, 2, EXPERTS), ALU.mult).then_inc(S("comb"), 1)
                    dve.wait_ge(S("cw_ev"), 4)
                    dve.wait_ge(S("comb"), 1)
                    for e in range(EXPERTS):
                        for j in range(EFC):
                            i = e * EFC + j
                            lows(2 * KD)
                            dve.wait_ge(S("esilu"), i + 1)
                            dve.wait_ge(S("eu_mm"), i + 1)
                            if j == 0 and e >= 2:
                                dve.wait_ge(S("edown"), e - 1)
                            if i >= 2:
                                dve.wait_ge(S("ehid"), i - 1)
                            p = prod[:, i % 2, 0:w]
                            V.did(dve.scalar_tensor_tensor(out=p, in0=bank[2 + i % 2][:, 0:w], scalar=UNSCALE, in1=gate_sb[:, i % 2, 0:w],
                                                           op0=ALU.mult, op1=ALU.mult))
                            V.settle()
                            V.did(dve.tensor_tensor(p, p, cw[:, e, :], ALU.mult))
                            V.settle()
                            V.did(dve.tensor_copy(ehid[:, e % 2, 0, j, :], p))
                            V.settle()
                            dve.tensor_tensor(ehid[:, e % 2, 1, j, :], p, ehid[:, e % 2, 0, j, :], ALU.subtract).then_inc(S("ehid"), 1)
                        if e < EXPERTS - 1:
                            lows(EFC * KD)
                residual(dve, V, lows, l, 1)


def constants():
    c = np.zeros((P, C_COLS), np.float32)
    i = np.arange(P)
    c[:, C_ID:C_ID + P] = np.eye(P)
    c[:, C_ONES:C_ONES + P] = 1
    c[:, C_BLK:C_BLK + P] = i[:, None] // HEAD == i[None, :] // HEAD
    for first, half in ((0, 32), (HEAD, 32)):
        for m in range(half):
            c[first + m + half, C_ROT + first + m] = -1
            c[first + m, C_ROT + first + m + half] = 1
    for m in range(16):
        c[HEAD + m + 16, C_ROTM + HEAD + m] = -1
        c[HEAD + m, C_ROTM + HEAD + m + 16] = 1
    same = i[:, None] // CHUNK == i[None, :] // CHUNK
    s, t = i[:, None], i[None, :]
    for n, m in enumerate((s < t, s <= t, s > t, s >= t)):
        c[:, C_TRI + n * P:C_TRI + (n + 1) * P] = m & same
    for lev in range(LEVELS):
        b = 1 << lev
        c[:, C_LEV + lev * P:C_LEV + (lev + 1) * P] = (s // (2 * b) == t // (2 * b)) & (s // b != t // b)
    pos = np.arange(SEQ)
    for kind, rot in enumerate((HEAD, 32)):
        pairs = rot // 4
        inv = (np.float32(10000.0) ** (-np.arange(pairs, dtype=np.float32) / np.float32(pairs))).astype(np.float32)
        ang = np.concatenate([(pos // GRID_W).astype(np.float32)[:, None] * inv, (pos % GRID_W).astype(np.float32)[:, None] * inv], 1)
        cos, sin = np.ones((P, SEQ), np.float32), np.zeros((P, SEQ), np.float32)
        for first in ((0, HEAD) if kind == 0 else (HEAD,)):
            for r in range(rot):
                cos[first + r] = np.cos(ang[:, r % (rot // 2)])
                sin[first + r] = np.sin(ang[:, r % (rot // 2)])
        c[:, C_ROPE + 2 * kind * SEQ:C_ROPE + (2 * kind + 1) * SEQ] = cos
        c[:, C_ROPE + (2 * kind + 1) * SEQ:C_ROPE + (2 * kind + 2) * SEQ] = sin
    c[:, C_EPS] = NORM_EPS
    c[:, C_EPS + 1] = GN_EPS
    for r in range(4):
        c[r, C_FOLD + r % 2] = 1
    e = np.arange(EXPERTS)
    c[:, C_LOW:C_LOW + 64] = (e[None, :] < e[:, None]).astype(np.float32).reshape(1, 64)
    sel = np.zeros((32, GRID_W * GRID_W), np.float32)
    for qc in range(GRID_W):
        start = min(max(qc - 8, 0), GRID_W - 16)
        for kc in range(GRID_W):
            if start <= kc < start + 16:
                sel[kc - qc + 15, qc * GRID_W + kc] = 1
            else:
                sel[31, qc * GRID_W + kc] = NEG
    return c, sel


def cut_blocks(w):
    r, c = w.shape
    return w.reshape(r // P, P, c // P, P).transpose(0, 2, 1, 3)


def by_output(w):
    b = cut_blocks(w)
    return b.transpose(1, 0, 2, 3).reshape(-1, P, P)


def columns(v):
    return np.ascontiguousarray(np.asarray(v).reshape(-1, P).T)


def padded(w, c):
    out = np.zeros((w.shape[0], c), w.dtype)
    out[:, :w.shape[1]] = w
    return out


def lay_out(i):
    i = {k: np.asarray(v) for k, v in i.items()}
    blocks, vecs, muxs, rows, lora2s, lws, rpbs = [], [], [], [], [], [], []
    for l in range(DEPTH):
        mod = cut_blocks(i["w_mod"][l]).reshape(KD, 6, KD, P, P).transpose(1, 0, 2, 3, 4).reshape(MOD_SLABS, SLAB, P, P)
        blocks.append(mod[:MOD_FIRST * KD].reshape(-1, P, P))
        w = i["w_in"][l]
        o = np.cumsum([0, 512, 128, 128, 256, 256, 256, 256, 256, 256, 384, 256, 32, 4096])
        part = [w[:, o[n]:o[n + 1]] for n in range(13)]
        heads = part[0].reshape(D, 8, HEAD)[:, [0, 4, 1, 5, 2, 6, 3, 7]].reshape(D, 512)
        kr = np.zeros((D, P), np.float32)
        kr[:, HEAD:HEAD + 32] = part[11]
        z = by_output(np.concatenate([heads, part[1], part[3], part[4], part[9], part[10], kr, part[6], part[7], part[8]], 1)).reshape(Z_SLABS, SLAB, P, P)
        for n in range(Z_SLABS):
            blocks.append(z[n])
            if n < MOD_STEPS:
                first = MOD_FIRST * KD + MOD_BESIDE * n
                blocks.append(mod[first:first + MOD_BESIDE].reshape(-1, P, P))
        blocks.append(by_output(np.concatenate([part[2], part[5]], 1)))
        uq = i["mla_w_uq"][l].reshape(384, 4, 96)
        blocks.append(by_output(np.concatenate([padded(uq[:, h], P) for h in range(4)], 1)))
        ukv = i["mla_w_ukv"][l].reshape(256, 4, 128)
        blocks.append(by_output(np.concatenate([padded(ukv[:, h, :64], P) for h in range(4)], 1)))
        blocks.append(by_output(np.ascontiguousarray(ukv[:, :, 64:]).reshape(256, 256)))
        gates, br = cut_blocks(part[12]), cut_blocks(i["w_branch"][l])
        for m in range(KD):
            for b in range(4):
                blocks.append(gates[:, b * KD + m])
                blocks.append(br[BRANCH_FIRST[b]:BRANCH_FIRST[b] + BRANCH_CHUNKS[b], m])
        blocks.append(by_output(i["w_out"][l]))
        if l % 2 == 0:
            g, u, d = (i[n][l // 2] for n in ("ffn_w_gate", "ffn_w_up", "ffn_w_down"))
            g, u = cut_blocks(g), cut_blocks(u)
            for j in range(FFC):
                blocks += [g[:, j], u[:, j]]
            blocks.append(by_output(d))
        else:
            for e in range(EXPERTS):
                g, u, d = (i[n][l // 2][e] for n in ("moe_w_gate", "moe_w_up", "moe_w_down"))
                g, u = cut_blocks(g), cut_blocks(u)
                for j in range(EFC):
                    blocks += [g[:, j], u[:, j]]
                blocks.append(by_output(d))
        two = lambda v: np.concatenate([v, v])
        vecs.append(np.concatenate([columns(i[n][l]) for n in ("b_mod", "norm_mix_pre", "norm_mix_post", "norm_ffn_pre", "norm_ffn_post")]
                                   + [columns(i["rwkv_mu_p"][l].reshape(-1)), columns(two(i["gqa_q_norm"][l])), columns(two(i["gqa_k_norm"][l])),
                                      columns(i["mla_q_norm"][l]), columns(i["mla_kv_norm"][l])], 1))
        muxs.append(columns(i["rwkv_mu_x"][l].reshape(-1)))
        rows.append(np.concatenate([i[n][l].reshape(-1) for n in ("rwkv_w0", "rwkv_a0", "rwkv_k_k", "rwkv_k_a", "rwkv_r_k", "rwkv_ln_w", "rwkv_ln_b")]))
        lora2s.append(np.concatenate([np.concatenate([i["rwkv_w2"][l].reshape(64, 256), i["rwkv_a2"][l].reshape(64, 256)]),
                                      i["rwkv_g2"][l].reshape(128, 256)], 1))
        one = np.concatenate([i["rwkv_w1"][l][0], i["rwkv_w1"][l][1], i["rwkv_a1"][l][0], i["rwkv_a1"][l][1]], 1)
        two_ = np.concatenate([i["rwkv_g1"][l][0], i["rwkv_g1"][l][1]], 1)
        lws.append(np.stack([x.reshape(KD, P, P).transpose(1, 0, 2) for x in (one, two_)], 1))
        r = i["na_rpb"][l][:, 8 - GRID_H:7 + GRID_H]
        rpbs.append(r.reshape(-1, NA_COLS).T)
    blocks = np.concatenate(blocks)
    slabs = np.ascontiguousarray(blocks.reshape(-1, SLAB, P, P).transpose(0, 2, 1, 3))
    rpb = np.concatenate([np.concatenate(rpbs, 1), np.ones((1, 56), np.float32)])
    cst, sel = constants()
    fm = np.concatenate([i["ctx"][0], i["x"][0]]).T.reshape(KD, P, TOK).transpose(1, 0, 2)
    c2 = np.stack([columns(i["c"][0]), columns(i["c_ctx"])], 2)
    wr = np.concatenate([i["moe_w_router"][0].reshape(KD, P, EXPERTS).transpose(1, 0, 2).reshape(P, KD * EXPERTS),
                         np.tile(i["moe_b_router"][0][None, :], (P, 1))], 1)
    return {"w": slabs, "vec": np.concatenate(vecs, 1), "mux": np.stack(muxs), "rows": np.stack(rows), "lora2": np.stack(lora2s), "lw": np.stack(lws),
            "rpb": rpb, "sel": sel, "cst": cst, "x": fm, "c2": c2, "wr": wr}


def program(nc, arrays):
    t = {name: nc.dram_tensor(f"in_{name}", a.shape, mybir.dt.from_np(a.dtype), kind="ExternalInput").ap() for name, a in arrays.items()}
    t["scratch"] = nc.dram_tensor("rel_bias", [DEPTH * 4 * 7, GRID_W * GRID_W], F32, kind="Internal").ap()
    t["out"] = nc.dram_tensor("out_0", [P, KD, SEQ], F32, kind="ExternalOutput").ap()
    build(nc, t)


def kernel(**inputs):
    import concourse.bacc as bacc
    from concourse.bass_utils import run_bass_kernel_spmd as run

    nc = bacc.Bacc("TRN2", target_bir_lowering=False, num_devices=1)
    arrays = {name: np.ascontiguousarray(a) for name, a in lay_out(inputs).items()}
    program(nc, arrays)
    r = run(nc, [{f"in_{name}": a for name, a in arrays.items()}], core_ids=[0])
    got = r.results[0]["out_0"]
    return np.ascontiguousarray(got.transpose(2, 1, 0).reshape(1, SEQ, D))
```
